# Optimizing a Trainium2 kernel written in Bass

```python
import math
import jax, jax.numpy as jnp
from jax import lax
import numpy as np

D_MODEL = 1024
BATCH = 1
SEQ = 256
DEPTH = 2

N_A_LAYERS = DEPTH // 2
N_B_LAYERS = DEPTH - N_A_LAYERS
ALPHA = (2.0 * DEPTH) ** 0.25
BETA = (8.0 * DEPTH) ** -0.25
LN_EPS = 1e-5
ROPE_THETA = 10000.0
NEG = -1e30

RET_HEADS = 4
RET_DK = D_MODEL // RET_HEADS
RET_DV = 2 * RET_DK
RET_CHUNK = 128

NSA_HEADS = 16
NSA_GROUPS = 4
NSA_REP = NSA_HEADS // NSA_GROUPS
NSA_DH = D_MODEL // NSA_HEADS
KV_W = NSA_GROUPS * NSA_DH
CMP_LEN = 32
CMP_STRIDE = 16
CMP_HIDDEN = 256
SLC_BLOCK = 64
SLC_TOPK = 16
WINDOW = 512
Q_BLOCK = 128
FORCE_BONUS = 1e3

N_EXPERTS = 16
N_EXPERT_GROUPS = 4
EXPERTS_PER_GROUP = N_EXPERTS // N_EXPERT_GROUPS
TOP_K = 2
D_EXPERT = 512


def layer_norm(x, g, b):
    xf = x.astype(jnp.float32)
    mu = xf.mean(-1, keepdims=True)
    var = jnp.square(xf - mu).mean(-1, keepdims=True)
    y = (xf - mu) * lax.rsqrt(var + LN_EPS) * g.astype(jnp.float32) + b.astype(jnp.float32)
    return y.astype(x.dtype)

def rope(x, pos):
    d = x.shape[-1]
    inv = ROPE_THETA ** (-jnp.arange(0, d, 2, dtype=jnp.float32) / d)
    ang = pos.astype(jnp.float32)[:, None] * inv[None, :]
    cos = jnp.cos(ang)[None, :, None, :]
    sin = jnp.sin(ang)[None, :, None, :]
    xf = x.astype(jnp.float32)
    x1, x2 = xf[..., : d // 2], xf[..., d // 2:]
    return jnp.concatenate([x1 * cos - x2 * sin, x2 * cos + x1 * sin], -1).astype(x.dtype)

def masked_softmax(s, mask):
    p = jax.nn.softmax(jnp.where(mask, s, NEG), axis=-1)
    return jnp.where(mask, p, 0.0)

def retention(h, w_in, w_out):
    B, S, _ = h.shape
    dt = h.dtype
    H, dk, dv, C = RET_HEADS, RET_DK, RET_DV, RET_CHUNK
    proj = h @ w_in
    q, k, v, g = jnp.split(proj, [H * dk, 2 * H * dk, 2 * H * dk + H * dv], axis=-1)
    pos = jnp.arange(S)
    q = rope(q.reshape(B, S, H, dk), pos)
    k = rope(k.reshape(B, S, H, dk), pos) * (dk ** -0.5)
    v = v.reshape(B, S, H, dv)
    nC = S // C

    def chunks(t):
        return t.reshape(B, nC, C, H, -1).transpose(0, 3, 1, 2, 4)

    qc, kc, vc = chunks(q), chunks(k), chunks(v)
    log_gamma = jnp.log1p(-(2.0 ** (-5.0 - jnp.arange(H, dtype=jnp.float32))))
    idx = jnp.arange(C, dtype=jnp.float32)
    diff = idx[:, None] - idx[None, :]
    decay_mask = jnp.where(diff >= 0, jnp.exp(log_gamma[:, None, None] * jnp.maximum(diff, 0.0)), 0.0).astype(dt)
    inner = jnp.einsum('bhncd,bhnmd->bhncm', qc, kc) * decay_mask[None, :, None]
    o_inner = jnp.einsum('bhncm,bhnme->bhnce', inner, vc)
    q_decay = jnp.exp(log_gamma[:, None] * (idx[None, :] + 1.0)).astype(dt)
    k_decay = jnp.exp(log_gamma[:, None] * (C - 1.0 - idx[None, :])).astype(dt)
    chunk_decay = jnp.exp(log_gamma * C).astype(dt)

    def step(state, xs):
        q_i, k_i, v_i = xs
        o = jnp.einsum('bhcd,bhde->bhce', q_i * q_decay[None, :, :, None], state)
        state = state * chunk_decay[None, :, None, None] + jnp.einsum(
            'bhcd,bhce->bhde', k_i * k_decay[None, :, :, None], v_i)
        return state, o

    state0 = jnp.zeros((B, H, dk, dv), dt)
    _, o_cross = lax.scan(step, state0, (qc.transpose(2, 0, 1, 3, 4),
                                         kc.transpose(2, 0, 1, 3, 4),
                                         vc.transpose(2, 0, 1, 3, 4)))
    o = o_inner + o_cross.transpose(1, 2, 0, 3, 4)
    o = o.transpose(0, 2, 3, 1, 4).reshape(B, S, H, dv)
    of = o.astype(jnp.float32)
    mu = of.mean(-1, keepdims=True)
    var = jnp.square(of - mu).mean(-1, keepdims=True)
    o = ((of - mu) * lax.rsqrt(var + LN_EPS)).reshape(B, S, H * dv).astype(dt)
    return (jax.nn.silu(g) * o) @ w_out

def nsa_shared_kv(h, w_kv, cmp_pe_k, cmp_pe_v, cmp_k_w1, cmp_k_w2, cmp_v_w1, cmp_v_w2):
    B, S, _ = h.shape
    G, dh = NSA_GROUPS, NSA_DH
    pos = jnp.arange(S)
    parts = jnp.split(h @ w_kv, 6, axis=-1)
    kc, vc, ks, vs, kw, vw = [p.reshape(B, S, G, dh) for p in parts]
    kc, ks, kw = rope(kc, pos), rope(ks, pos), rope(kw, pos)
    n_cmp = (S - CMP_LEN) // CMP_STRIDE + 1
    cidx = jnp.arange(n_cmp)[:, None] * CMP_STRIDE + jnp.arange(CMP_LEN)[None, :]

    def compress(t, pe, w1, w2):
        blk = t[:, cidx] + pe[None, None, :, None, :]
        blk = blk.transpose(0, 3, 1, 2, 4).reshape(B, G, n_cmp, CMP_LEN * dh)
        return jax.nn.gelu(blk @ w1) @ w2

    k_cmp = compress(kc, cmp_pe_k, cmp_k_w1, cmp_k_w2)
    v_cmp = compress(vc, cmp_pe_v, cmp_v_w1, cmp_v_w2)
    nS = S // SLC_BLOCK

    def to_blocks(t):
        return t.transpose(0, 2, 1, 3).reshape(B, G, nS, SLC_BLOCK, dh)

    def pad_win(t):
        return jnp.pad(t.transpose(0, 2, 1, 3), ((0, 0), (0, 0), (WINDOW, 0), (0, 0)))

    return (k_cmp, v_cmp, to_blocks(ks), to_blocks(vs), pad_win(kw), pad_win(vw))

def nsa_attention(h, w_in, w_out, shared):
    k_cmp, v_cmp, k_slc, v_slc, k_win, v_win = shared
    B, S, _ = h.shape
    dt = h.dtype
    H, G, R, dh = NSA_HEADS, NSA_GROUPS, NSA_REP, NSA_DH
    proj = h @ w_in
    q = rope(proj[..., : H * dh].reshape(B, S, H, dh), jnp.arange(S)) * (dh ** -0.5)
    gates = jax.nn.sigmoid(proj[..., H * dh:].astype(jnp.float32)).reshape(B, S, H, 3)
    nQ = S // Q_BLOCK
    q_blocks = q.reshape(B, nQ, Q_BLOCK, G, R, dh).transpose(1, 0, 3, 4, 2, 5)
    g_blocks = gates.reshape(B, nQ, Q_BLOCK, G, R, 3).transpose(1, 0, 3, 4, 2, 5)
    n_cmp = k_cmp.shape[2]
    nS = k_slc.shape[2]
    top_k = min(SLC_TOPK, nS)
    ci = jnp.arange(n_cmp)
    sj = jnp.arange(nS)
    cmp_end = ci * CMP_STRIDE + CMP_LEN - 1
    overlap = ((ci[:, None] * CMP_STRIDE < (sj[None, :] + 1) * SLC_BLOCK)
               & (ci[:, None] * CMP_STRIDE + CMP_LEN > sj[None, :] * SLC_BLOCK)).astype(jnp.float32)
    gather_blocks = jax.vmap(jax.vmap(lambda kb, ix: kb[ix]))

    def block(xs):
        i, qb, gb = xs
        t = i * Q_BLOCK + jnp.arange(Q_BLOCK)
        s = jnp.einsum('bgrqd,bgnd->bgrqn', qb, k_cmp).astype(jnp.float32)
        p_cmp = masked_softmax(s, cmp_end[None, :] <= t[:, None])
        o_cmp = jnp.einsum('bgrqn,bgnd->bgrqd', p_cmp.astype(dt), v_cmp)
        imp = jnp.einsum('bgrqn,ns->bgqs', p_cmp, overlap)
        valid = sj[None, :] * SLC_BLOCK <= t[:, None]
        cur = t // SLC_BLOCK
        forced = (sj[None, :] == 0) | (sj[None, :] == cur[:, None]) | (sj[None, :] == cur[:, None] - 1)
        score = jnp.where(valid, imp + jnp.where(forced, FORCE_BONUS, 0.0), NEG)
        _, sel = lax.top_k(score, top_k)
        ks = gather_blocks(k_slc, sel).reshape(B, G, Q_BLOCK, top_k * SLC_BLOCK, dh)
        vs = gather_blocks(v_slc, sel).reshape(B, G, Q_BLOCK, top_k * SLC_BLOCK, dh)
        key_pos = (sel[..., None] * SLC_BLOCK + jnp.arange(SLC_BLOCK)).reshape(B, G, Q_BLOCK, top_k * SLC_BLOCK)
        s = jnp.einsum('bgrqd,bgqkd->bgrqk', qb, ks).astype(jnp.float32)
        p = masked_softmax(s, (key_pos <= t[:, None])[:, :, None])
        o_slc = jnp.einsum('bgrqk,bgqkd->bgrqd', p.astype(dt), vs)
        kw = lax.dynamic_slice_in_dim(k_win, i * Q_BLOCK, Q_BLOCK + WINDOW, axis=2)
        vw = lax.dynamic_slice_in_dim(v_win, i * Q_BLOCK, Q_BLOCK + WINDOW, axis=2)
        wpos = i * Q_BLOCK - WINDOW + jnp.arange(Q_BLOCK + WINDOW)
        dist = t[:, None] - wpos[None, :]
        wmask = (dist >= 0) & (dist < WINDOW) & (wpos[None, :] >= 0)
        s = jnp.einsum('bgrqd,bgkd->bgrqk', qb, kw).astype(jnp.float32)
        p = masked_softmax(s, wmask)
        o_win = jnp.einsum('bgrqk,bgkd->bgrqd', p.astype(dt), vw)
        o = gb[..., 0:1] * o_cmp + gb[..., 1:2] * o_slc + gb[..., 2:3] * o_win
        return o.astype(dt)

    o = lax.map(block, (jnp.arange(nQ), q_blocks, g_blocks))
    o = o.transpose(1, 0, 4, 2, 3, 5).reshape(B, S, H * dh)
    return o @ w_out

def moe(h, router_w, router_b, w_gate, w_up, w_down):
    B, S, D = h.shape
    x = h.reshape(-1, D)
    T = x.shape[0]
    aff = jax.nn.sigmoid((x @ router_w).astype(jnp.float32))
    sel_score = aff + router_b.astype(jnp.float32)
    grp_score = lax.top_k(sel_score.reshape(T, N_EXPERT_GROUPS, EXPERTS_PER_GROUP), TOP_K)[0].sum(-1)
    best = jnp.argmax(grp_score, axis=-1)
    in_group = (jnp.arange(N_EXPERTS) // EXPERTS_PER_GROUP)[None, :] == best[:, None]
    _, top_idx = lax.top_k(jnp.where(in_group, sel_score, NEG), TOP_K)
    chosen = jax.nn.one_hot(top_idx, N_EXPERTS, dtype=jnp.float32).sum(1)
    w = aff * chosen
    w = (w / w.sum(-1, keepdims=True)).astype(x.dtype)
    y = jnp.zeros_like(x)
    for e in range(N_EXPERTS):
        he = (jax.nn.silu(x @ w_gate[e]) * (x @ w_up[e])) @ w_down[e]
        y = y + w[:, e:e + 1] * he
    return y.reshape(B, S, D)

def first_inputs(seed: int = 0) -> dict:
    key = jax.random.key(seed)
    ks = jax.random.split(key, 32)
    f32 = jnp.float32
    D = D_MODEL

    def nrm(k, shape, scale):
        return jax.random.normal(k, shape, f32) * scale

    x = nrm(ks[0], (BATCH, SEQ, D), 1.0)
    ret_w_in = jnp.concatenate([
        nrm(ks[1], (N_A_LAYERS, D, 2 * RET_HEADS * RET_DK), D ** -0.5),
        nrm(ks[2], (N_A_LAYERS, D, RET_HEADS * RET_DV), D ** -0.5 * BETA),
        nrm(ks[3], (N_A_LAYERS, D, RET_HEADS * RET_DV), D ** -0.5)], axis=-1)
    ret_w_out = nrm(ks[4], (N_A_LAYERS, RET_HEADS * RET_DV, D), (RET_HEADS * RET_DV) ** -0.5 * BETA)
    kv_k = nrm(ks[5], (3, D, KV_W), D ** -0.5)
    kv_v = nrm(ks[6], (3, D, KV_W), D ** -0.5 * BETA)
    nsa_w_kv = jnp.stack([kv_k, kv_v], 1).transpose(2, 0, 1, 3).reshape(D, 6 * KV_W)
    cmp_pe_k = nrm(ks[7], (CMP_LEN, NSA_DH), 0.1)
    cmp_pe_v = nrm(ks[8], (CMP_LEN, NSA_DH), 0.1)
    cmp_k_w1 = nrm(ks[9], (CMP_LEN * NSA_DH, CMP_HIDDEN), (CMP_LEN * NSA_DH) ** -0.5)
    cmp_k_w2 = nrm(ks[10], (CMP_HIDDEN, NSA_DH), CMP_HIDDEN ** -0.5)
    cmp_v_w1 = nrm(ks[11], (CMP_LEN * NSA_DH, CMP_HIDDEN), (CMP_LEN * NSA_DH) ** -0.5)
    cmp_v_w2 = nrm(ks[12], (CMP_HIDDEN, NSA_DH), CMP_HIDDEN ** -0.5)
    nsa_w_in = nrm(ks[13], (N_B_LAYERS, D, NSA_HEADS * NSA_DH + 3 * NSA_HEADS), D ** -0.5)
    nsa_w_out = nrm(ks[14], (N_B_LAYERS, NSA_HEADS * NSA_DH, D), (NSA_HEADS * NSA_DH) ** -0.5 * BETA)
    router_w = nrm(ks[15], (D, N_EXPERTS), D ** -0.5)
    router_b = nrm(ks[16], (N_EXPERTS,), 0.01)
    moe_w_gate = nrm(ks[17], (DEPTH, N_EXPERTS, D, D_EXPERT), D ** -0.5)
    moe_w_up = nrm(ks[18], (DEPTH, N_EXPERTS, D, D_EXPERT), D ** -0.5 * BETA)
    moe_w_down = nrm(ks[19], (DEPTH, N_EXPERTS, D_EXPERT, D), D_EXPERT ** -0.5 * BETA)
    ln_mix_g = 1.0 + nrm(ks[20], (DEPTH, D), 0.02)
    ln_mix_b = nrm(ks[21], (DEPTH, D), 0.02)
    ln_ffn_g = 1.0 + nrm(ks[22], (DEPTH, D), 0.02)
    ln_ffn_b = nrm(ks[23], (DEPTH, D), 0.02)
    return {'x': x, 'ret_w_in': ret_w_in, 'ret_w_out': ret_w_out, 'nsa_w_kv': nsa_w_kv,
            'cmp_pe_k': cmp_pe_k, 'cmp_pe_v': cmp_pe_v, 'cmp_k_w1': cmp_k_w1, 'cmp_k_w2': cmp_k_w2,
            'cmp_v_w1': cmp_v_w1, 'cmp_v_w2': cmp_v_w2, 'nsa_w_in': nsa_w_in, 'nsa_w_out': nsa_w_out,
            'router_w': router_w, 'router_b': router_b, 'moe_w_gate': moe_w_gate, 'moe_w_up': moe_w_up,
            'moe_w_down': moe_w_down, 'ln_mix_g': ln_mix_g, 'ln_mix_b': ln_mix_b,
            'ln_ffn_g': ln_ffn_g, 'ln_ffn_b': ln_ffn_b}

def first_block(x, ret_w_in, ret_w_out, nsa_w_kv, cmp_pe_k, cmp_pe_v, cmp_k_w1, cmp_k_w2, cmp_v_w1, cmp_v_w2,
              nsa_w_in, nsa_w_out, router_w, router_b, moe_w_gate, moe_w_up, moe_w_down,
              ln_mix_g, ln_mix_b, ln_ffn_g, ln_ffn_b):
    h = x
    shared = None
    for l in range(DEPTH):
        if l < N_A_LAYERS:
            mix = retention(h, ret_w_in[l], ret_w_out[l])
        else:
            if l == N_A_LAYERS:
                shared = nsa_shared_kv(h, nsa_w_kv, cmp_pe_k, cmp_pe_v, cmp_k_w1, cmp_k_w2, cmp_v_w1, cmp_v_w2)
            j = l - N_A_LAYERS
            mix = nsa_attention(h, nsa_w_in[j], nsa_w_out[j], shared)
        h = layer_norm(ALPHA * h + mix, ln_mix_g[l], ln_mix_b[l])
        h = layer_norm(ALPHA * h + moe(h, router_w, router_b, moe_w_gate[l], moe_w_up[l], moe_w_down[l]),
                       ln_ffn_g[l], ln_ffn_b[l])
    return h


DEPTH_2 = 1

A_HEADS = 4
A_QK_DIM = 64
A_V_DIM = 2 * A_QK_DIM
A_WIDTH = A_HEADS * A_V_DIM
B_PAIRS = ((128, 1), (512, 4), (2048, 16))
B_GROUPS = len(B_PAIRS)
B_HEADS = 4
B_HEAD_DIM = 128
B_WIDTH = B_HEADS * B_HEAD_DIM
B_BLOCK = 128
A_Q_COLS = A_HEADS * 2 * A_QK_DIM
A_K_COLS = A_HEADS * 2 * A_QK_DIM
A_V_COLS = A_HEADS * A_V_DIM
B_COLS = B_GROUPS * B_WIDTH
GATE_COLS = 2 * D_MODEL
IN_COLS = A_Q_COLS + A_K_COLS + A_V_COLS + 3 * B_COLS + GATE_COLS
D_FF = 2816
CONV_WIDTH = 3
NORM_EPS = 1e-6


def rms_norm(x, g):
    xf = x.astype(jnp.float32)
    y = xf * lax.rsqrt(jnp.mean(xf * xf, axis=-1, keepdims=True) + NORM_EPS)
    return (y * g.astype(jnp.float32)).astype(x.dtype)

def rope_tables(positions, dim):
    inv = ROPE_THETA ** (-jnp.arange(0, dim, 2, dtype=jnp.float32) / dim)
    ang = positions.astype(jnp.float32)[..., None] * inv
    return jnp.cos(ang)[:, :, None, None, :], jnp.sin(ang)[:, :, None, None, :]

def apply_rope(t, cos, sin):
    tf = t.astype(jnp.float32)
    t1, t2 = jnp.split(tf, 2, axis=-1)
    return jnp.concatenate([t1 * cos - t2 * sin, t2 * cos + t1 * sin], axis=-1).astype(t.dtype)

def diff_attention(q, k, v, lam):
    b, s, h, _, dqk = q.shape
    nq = s // Q_BLOCK
    scale = dqk ** -0.5
    qb = q.reshape(b, nq, Q_BLOCK, h, 2, dqk).transpose(1, 0, 2, 3, 4, 5)
    kpos = jnp.arange(s)

    def one_block(args):
        qi, i = args
        sc = jnp.einsum('bqhcd,bkhcd->bchqk', qi, k).astype(jnp.float32) * scale
        qpos = i * Q_BLOCK + jnp.arange(Q_BLOCK)
        causal = kpos[None, :] <= qpos[:, None]
        p = jax.nn.softmax(jnp.where(causal, sc, -jnp.inf), axis=-1)
        a = p[:, 0] - lam * p[:, 1]
        return jnp.einsum('bhqk,bkhd->bqhd', a.astype(v.dtype), v)

    o = lax.map(one_block, (qb, jnp.arange(nq)))
    return o.transpose(1, 0, 2, 3, 4).reshape(b, s, h, v.shape[-1])

def dilated_group(q, k, v, window, dil):
    b, s, h, d = q.shape
    L = s // dil
    nwin = window // dil
    nb = -(-L // B_BLOCK)
    Lp = nb * B_BLOCK

    def to_blocks(t):
        t = t.reshape(b, L, dil, h, d).transpose(0, 2, 1, 3, 4)
        t = jnp.pad(t, ((0, 0), (0, 0), (0, Lp - L), (0, 0), (0, 0)))
        return t.reshape(b, dil, nb, B_BLOCK, h, d)

    def with_prev(t):
        prev = jnp.pad(t[:, :, :-1], ((0, 0), (0, 0), (1, 0), (0, 0), (0, 0), (0, 0)))
        return jnp.concatenate([prev, t], axis=3)

    qb, kb, vb = to_blocks(q), to_blocks(k), to_blocks(v)
    kk, vv = with_prev(kb), with_prev(vb)
    sc = jnp.einsum('brnqhd,brnkhd->brnhqk', qb, kk).astype(jnp.float32) * (d ** -0.5)
    qi = jnp.arange(B_BLOCK)[:, None]
    kj = jnp.arange(2 * B_BLOCK)[None, :]
    rel = qi - kj + B_BLOCK
    kabs = jnp.arange(nb)[:, None, None] * B_BLOCK + kj - B_BLOCK
    valid = (rel >= 0) & (rel <= nwin) & (kabs >= 0)
    sc = jnp.where(valid[None, None, :, None], sc, -jnp.inf)
    m = jnp.max(sc, axis=-1, keepdims=True)
    p = jnp.exp(sc - m)
    den = jnp.sum(p, axis=-1, keepdims=True)
    o = jnp.einsum('brnhqk,brnkhd->brnqhd', (p / den).astype(v.dtype), vv)
    lse = (m + jnp.log(den))[..., 0].transpose(0, 1, 2, 4, 3)

    def from_blocks(t):
        t = t.reshape((b, dil, Lp) + t.shape[4:])[:, :, :L]
        t = jnp.moveaxis(t, 1, 2)
        return t.reshape((b, s) + t.shape[3:])

    return from_blocks(o), from_blocks(lse)

def causal_depthwise_conv(u, w, bias):
    s = u.shape[1]
    up = jnp.pad(u, ((0, 0), (CONV_WIDTH - 1, 0), (0, 0)))
    out = sum(up[:, j:j + s] * w[j] for j in range(CONV_WIDTH))
    return out + bias

def second_inputs(seed: int = 0) -> dict:
    key = jax.random.key(seed)
    ks = jax.random.split(key, 20)
    f32 = jnp.float32

    def nrm(k, shape, scale):
        return jax.random.normal(k, shape, f32) * scale

    def gain(k, shape):
        return 1.0 + 0.05 * jax.random.normal(k, shape, f32)

    x = jax.random.normal(ks[0], (BATCH, SEQ, D_MODEL), f32)
    offset = jax.random.randint(ks[1], (BATCH, 1), 0, 1024, dtype=jnp.int32)
    positions = (offset + jnp.arange(SEQ, dtype=jnp.int32)[None, :]).astype(jnp.int32)
    return {
        "x": x,
        "positions": positions,
        "pre_mix_g": gain(ks[2], (DEPTH_2, D_MODEL)),
        "w_in": nrm(ks[3], (DEPTH_2, D_MODEL, IN_COLS), D_MODEL ** -0.5),
        "diff_lambda": nrm(ks[4], (DEPTH_2, 4, A_QK_DIM), 0.1),
        "diff_head_g": gain(ks[5], (DEPTH_2, A_V_DIM)),
        "w_a_out": nrm(ks[6], (DEPTH_2, A_WIDTH, D_MODEL), A_WIDTH ** -0.5),
        "w_b_out": nrm(ks[7], (DEPTH_2, B_WIDTH, D_MODEL), B_WIDTH ** -0.5),
        "w_mix_out": nrm(ks[8], (DEPTH_2, D_MODEL, D_MODEL), D_MODEL ** -0.5),
        "post_mix_g": gain(ks[9], (DEPTH_2, D_MODEL)),
        "pre_ffn_g": gain(ks[10], (DEPTH_2, D_MODEL)),
        "w_up": nrm(ks[11], (DEPTH_2, D_MODEL, 2 * D_FF), D_MODEL ** -0.5),
        "conv_w": nrm(ks[12], (DEPTH_2, CONV_WIDTH, 2 * D_FF), CONV_WIDTH ** -0.5),
        "conv_b": nrm(ks[13], (DEPTH_2, 2 * D_FF), 0.01),
        "w_down": nrm(ks[14], (DEPTH_2, D_FF, D_MODEL), D_FF ** -0.5),
        "post_ffn_g": gain(ks[15], (DEPTH_2, D_MODEL)),
    }

def second_block(x, positions, pre_mix_g, w_in, diff_lambda, diff_head_g, w_a_out, w_b_out,
              w_mix_out, post_mix_g, pre_ffn_g, w_up, conv_w, conv_b, w_down, post_ffn_g):
    b, s, _ = x.shape
    cos_a, sin_a = rope_tables(positions, A_QK_DIM)
    cos_b, sin_b = rope_tables(positions, B_HEAD_DIM)
    split_at = np.cumsum([A_Q_COLS, A_K_COLS, A_V_COLS, B_COLS, B_COLS, B_COLS]).tolist()

    for l in range(DEPTH_2):
        h = rms_norm(x, pre_mix_g[l])
        proj = h @ w_in[l]
        qa, ka, va, qb, kb, vb, gates = jnp.split(proj, split_at, axis=-1)

        qa = apply_rope(qa.reshape(b, s, A_HEADS, 2, A_QK_DIM), cos_a, sin_a)
        ka = apply_rope(ka.reshape(b, s, A_HEADS, 2, A_QK_DIM), cos_a, sin_a)
        va = va.reshape(b, s, A_HEADS, A_V_DIM)
        lam_init = 0.8 - 0.6 * math.exp(-0.3 * l)
        lv = diff_lambda[l].astype(jnp.float32)
        lam = jnp.exp(jnp.sum(lv[0] * lv[1])) - jnp.exp(jnp.sum(lv[2] * lv[3])) + lam_init
        oa = diff_attention(qa, ka, va, lam)
        oa = rms_norm(oa, diff_head_g[l]) * (1.0 - lam_init)
        ya = oa.reshape(b, s, A_WIDTH) @ w_a_out[l]

        qb = apply_rope(qb.reshape(b, s, B_GROUPS, B_HEADS, B_HEAD_DIM), cos_b, sin_b)
        kb = apply_rope(kb.reshape(b, s, B_GROUPS, B_HEADS, B_HEAD_DIM), cos_b, sin_b)
        vb = vb.reshape(b, s, B_GROUPS, B_HEADS, B_HEAD_DIM)
        outs, lses = [], []
        for g, (window, dil) in enumerate(B_PAIRS):
            o_g, lse_g = dilated_group(qb[:, :, g], kb[:, :, g], vb[:, :, g], window, dil)
            outs.append(o_g)
            lses.append(lse_g)
        wts = jax.nn.softmax(jnp.stack(lses, axis=0), axis=0)
        ob = jnp.einsum('gbsh,gbshd->bshd', wts.astype(x.dtype), jnp.stack(outs, axis=0))
        yb = ob.reshape(b, s, B_WIDTH) @ w_b_out[l]

        g_a, g_b = jnp.split(jax.nn.sigmoid(gates), 2, axis=-1)
        mix = (g_a * ya + g_b * yb) @ w_mix_out[l]
        x = x + rms_norm(mix, post_mix_g[l])

        h = rms_norm(x, pre_ffn_g[l])
        u = causal_depthwise_conv(h @ w_up[l], conv_w[l], conv_b[l])
        gate, val = jnp.split(u, 2, axis=-1)
        y = (jax.nn.gelu(gate, approximate=True) * val) @ w_down[l]
        x = x + rms_norm(y, post_ffn_g[l])
    return x


def setup_inputs(seed=0):
    out = dict(first_inputs(seed))
    for name, value in second_inputs(seed + 1).items():
        if name != "x":
            out[name + "_2"] = value
    return out


def reference(
    x, ret_w_in, ret_w_out, nsa_w_kv, cmp_pe_k, cmp_pe_v, cmp_k_w1, cmp_k_w2, cmp_v_w1,
    cmp_v_w2, nsa_w_in, nsa_w_out, router_w, router_b, moe_w_gate, moe_w_up, moe_w_down,
    ln_mix_g, ln_mix_b, ln_ffn_g, ln_ffn_b, positions_2, pre_mix_g_2, w_in_2, diff_lambda_2,
    diff_head_g_2, w_a_out_2, w_b_out_2, w_mix_out_2, post_mix_g_2, pre_ffn_g_2, w_up_2,
    conv_w_2, conv_b_2, w_down_2, post_ffn_g_2,
):
    x = first_block(
        x, ret_w_in, ret_w_out, nsa_w_kv, cmp_pe_k, cmp_pe_v, cmp_k_w1, cmp_k_w2, cmp_v_w1,
        cmp_v_w2, nsa_w_in, nsa_w_out, router_w, router_b, moe_w_gate, moe_w_up, moe_w_down,
        ln_mix_g, ln_mix_b, ln_ffn_g, ln_ffn_b,
    )
    return second_block(
        x, positions_2, pre_mix_g_2, w_in_2, diff_lambda_2, diff_head_g_2, w_a_out_2, w_b_out_2,
        w_mix_out_2, post_mix_g_2, pre_ffn_g_2, w_up_2, conv_w_2, conv_b_2, w_down_2,
        post_ffn_g_2,
    )


_drawn_inputs = setup_inputs


def setup_inputs(seed=0):
    import zlib

    import numpy as np

    out = dict(_drawn_inputs(seed))
    spreads = {}
    factors = {'cmp_pe_k': 8.0, 'cmp_k_w1': 3.35, 'cmp_k_w2': 3.041, 'conv_b_2': 7.004}
    for name, (base, spread) in spreads.items():
        noise = np.random.default_rng([zlib.crc32(name.encode()), seed]).standard_normal(out[name].shape)
        drawn = base * np.exp(spread * noise) if base else spread * noise
        out[name] = __import__('jax').numpy.asarray(drawn.astype(out[name].dtype))
    for name, factor in factors.items():
        out[name] = (out[name] * factor).astype(out[name].dtype)
    return out
```

```python
from contextlib import ExitStack

import concourse.bass as bass
from concourse import mybir

F32 = mybir.dt.float32
F32R = mybir.dt.float32r
I32 = mybir.dt.int32
ALU = mybir.AluOpType
ACT = mybir.ActivationFunctionType
AX = mybir.AxisListType

P = 128
D = 1024
SEQ = 256
TT = SEQ // P
DC = D // P
DEPTH = 2
ALPHA = (2.0 * DEPTH) ** 0.25
LN_EPS = 1e-5
RMS_EPS = 1e-6
NEG = -1e30

RET_H, RET_DK, RET_DV, RET_CHUNK = 4, 256, 512, 128
NSA_H, NSA_G, NSA_DH = 16, 4, 64
NSA_REP = NSA_H // NSA_G
CMP_LEN, CMP_STRIDE, CMP_HID = 32, 16, 256
N_CMP = (SEQ - CMP_LEN) // CMP_STRIDE + 1
E, E_GROUPS, D_EXP = 16, 4, 512
E_PER = E // E_GROUPS

A_H, A_DQK, A_DV = 4, 64, 128
B_PAIRS = ((128, 1), (512, 4), (2048, 16))
B_G, B_H, B_DH = 3, 4, 128
D_FF = 2816
FFC = D_FF // P
CONV_W = 3

KC = 4
BW = 512
RAW = 6
SPLIT = 3
ROUND = 12582912.0

C_ID, C_ROW, C_BEFORE, C_ONES, C_COL, C_I16, C_I4, C_END = 0, 128, 384, 512, 640, 642, 658, 662
R_DECAY, R_COS, R_SIN, R_END = 0, 1536, 1792, 2048
N_MASK, N_CMASK, N_VALID, N_COS, N_SIN, N_END = 0, 512, 542, 544, 608, 672
B_MASK, B_CAUSAL, B_INV, B_END = 0, 1152, 1408, 1504
LAM_INIT = 0.8 - 0.6


class Order:

    def __init__(self, eng, sem):
        self.eng, self.sem, self.n = eng, sem, 0

    def __call__(self, ins):
        self.n += 1
        ins.then_inc(self.sem, 1)

    def wait(self):
        self.eng.wait_ge(self.sem, self.n)

    def then(self, ins):
        self(ins)
        self.wait()


class Linear:

    def __init__(self, b0, n0, n, groups, sources):
        self.b0, self.n0, self.n, self.groups, self.sources = b0, n0, n, groups, sources
        self.looped = n >= 6 and len(groups) == 2 and n != 11


class State:

    def __init__(self, name, inbox):
        self.name, self.inbox = name, inbox
        self.turn = self.stage = self.hand = self.unit = self.params = 0
        self.pt_a = self.pt_v = 0


def block_program(nc, a, out, stop=None):
    with ExitStack() as ctx:
        def sem(name):
            return ctx.enter_context(nc.semaphore(name))

        cursor = [16512]

        def size_of(shape):
            size = 4
            for s in shape[1:]:
                size *= s
            return (size + 31) // 32 * 32

        def keep(name, shape, dt):
            t = nc.alloc_sbuf_tensor_at(name, shape, dt, offset=cursor[0])
            cursor[0] += size_of(shape)
            return t

        raw = keep("raw", [P, RAW, KC, BW], F32)
        whi = keep("whi", [P, SPLIT, KC, BW], F32R)
        wlo = keep("wlo", [P, SPLIT, KC, BW], F32R)
        cst = keep("cst", [P, C_END], F32)
        ident_r = keep("ident_r", [P, P], F32R)
        X = keep("X", [P, TT, D], F32)
        gb_at = cursor[0]
        gb = keep("gb", [P, 2, D], F32)
        th_at = cursor[0]
        th = keep("th", [P, DC, SEQ], F32R)
        tl = keep("tl", [P, DC, SEQ], F32R)
        small = keep("small", [P, 256], F32)
        flag_i = keep("flag_i", [P, 8], I32)
        rw = keep("rw", [P, DC, E], F32)
        rwh = keep("rwh", [P, DC, E], F32R)
        rwl = keep("rwl", [P, DC, E], F32R)
        rb = keep("rb", [P, E], F32)
        arena = cursor[0]

        class Arena:

            def __init__(self, at=arena):
                self.at = at

            def __call__(self, name, shape, dt=F32, at=None):
                if at is None:
                    at = self.at
                    self.at += size_of(shape)
                assert at + size_of(shape) <= nc.sbuf_usable_end, name
                return nc.alloc_sbuf_tensor_at(name, shape, dt, offset=at)

        PS = ctx.enter_context(nc.psum_tensor("PS", [P, 8, 512], F32))
        ident = cst[:, C_ID:C_ID + P]
        before = cst[:, C_BEFORE:C_BEFORE + P]
        ones = cst[:, C_ONES:C_ONES + P]

        A = Arena()
        K16 = 16384
        ret_proj = A("ret_proj", [P, 12, TT, BW])
        ret_qkT = A("ret_qkT", [P, 16, SEQ])
        ret_c = A("ret_c", [P, R_END])
        ret_sd = A("ret_sd", [P, 2, 3, P], at=th_at)
        ret_o = A("ret_o", [P, TT, RET_H, RET_DV], at=arena)
        ret_oTh = A("ret_oTh", [P, 16, SEQ], F32R, at=arena + K16)
        ret_oTl = A("ret_oTl", [P, 16, SEQ], F32R, at=arena + 3 * K16)
        A = Arena()
        xn_h = A("xn_h", [P, TT, D], F32R)
        xn_l = A("xn_l", [P, TT, D], F32R)
        xg_h = A("xg_h", [P, DC, P], F32R)
        xg_l = A("xg_l", [P, DC, P], F32R)
        slot_of = A("slot_of", [P, E, SEQ])
        pick = A("pick", [P, TT, P], F32R)
        pickT = A("pickT", [P, SEQ], F32R)
        silu = A("silu", [P, D_EXP])
        hbuf = A("hbuf", [P, D_EXP])
        hT_h = A("hT_h", [P, 4, P], F32R)
        hT_l = A("hT_l", [P, 4, P], F32R)
        y_h = A("y_h", [P, 2, BW], F32R)
        y_l = A("y_l", [P, 2, BW], F32R)
        route = A("route", [P, 8, TT, E])
        pairs = A("pairs", [P, 8, TT, E_GROUPS])
        tops = A("tops", [P, 4, TT])
        w_split = A("w_split", [P, TT, E, 2], F32R)
        slot_r = A("slot_r", [P, TT, E], F32R)
        zero_r = A("zero_r", [P, P], F32R)
        w_slot = A("w_slot", [P, 1])
        affinity, picked, slot_no, w_tok, score, rt1, rt2, rt3 = (route[:, i] for i in range(8))
        A = Arena()
        n_kv = A("n_kv", [P, 3, TT, BW])
        n_q = A("n_q", [P, 2, TT, BW])
        n_g48 = A("n_g48", [P, TT, 3 * NSA_H])
        n_gate = A("n_gate", [P, TT, 3, NSA_H])
        n_c = A("n_c", [P, N_END])
        nT_at = A.at
        n_T = A("n_T", [P, 24, SEQ])
        dup_at = A.at
        n_dup = A("n_dup", [P, TT, 4, NSA_G, P])
        cmp_pe = A("cmp_pe", [P, 2, P])
        cmp_peT = A("cmp_peT", [P, 2, CMP_LEN // 2])
        cmp_w2k = A("cmp_w2k", [P, 2, 2, NSA_DH])
        cmp_w2v = A("cmp_w2v", [P, 2, NSA_DH])
        cmp_kT = A("cmp_kT", [P, 64])
        cmp_v = A("cmp_v", [P, NSA_G, NSA_DH])
        cmp_h = A("cmp_h", [P, 2, 2, 60])
        cmp_w1 = [A("cmp_w1k", [P, 16, CMP_HID], at=th_at), A("cmp_w1v", [P, 16, CMP_HID], at=dup_at)]
        cmp_x = A("cmp_x", [P, 2, 16, 64], at=gb_at)
        n_o = A("n_o", [P, TT, D], at=nT_at)
        def attention_buffers(A, tag, at):
            t = A("scores_" + tag, [P, 2, 3, SEQ], at=at)
            pt = A("probsT_" + tag, [P, 6, P], at=at + 6144)
            return t, pt, A("tops_" + tag, [P, 2, 4], at=at + 9216), A("sums_" + tag, [P, 2, 4], at=at + 9248), \
                A("coef_" + tag, [P, 2, 4], at=at + 9280), A("rec_" + tag, [P, 2, 4], at=at + 9312)
        n_att = attention_buffers(A, "n", dup_at)
        A = Arena()
        oaT_h = A("oaT_h", [P, 4, SEQ], F32R, at=gb_at + 4096)
        oaT_l = A("oaT_l", [P, 4, SEQ], F32R)
        b_c = A("b_c", [P, B_END])
        trig = A("trig", [P, 2, TT, 96])
        part_at = A.at
        a_proj = A("a_proj", [P, 3, TT, BW])
        a_qkT = A("a_qkT", [P, 8, SEQ])
        a_o = A("a_o", [P, TT, 4, P])
        a_sq = A("a_sq", [P, TT, 4, P])
        head_g = A("head_g", [P, P])
        lam_in = A("lam_in", [P, 4, A_DQK])
        ang = A("ang", [P, 4, TT, 96])
        pos_i = A("pos_i", [P, TT], I32)
        pos_f = A("pos_f", [P, TT])
        at_a = A.at
        a_att = attention_buffers(A, "a", at_a)
        A = Arena(part_at)
        b_qkT = A("b_qkT", [P, 24, SEQ])
        bproj_at = A.at
        b_proj = A("b_proj", [P, 9, TT, BW])
        b_att = attention_buffers(A, "b", bproj_at)
        b_o = A("b_o", [P, TT, 4, P], at=bproj_at + 10240)
        gates = A("gates", [P, 4, TT, BW], at=part_at)
        obT_h = A("obT_h", [P, 4, SEQ], F32R, at=part_at + 16384)
        obT_l = A("obT_l", [P, 4, SEQ], F32R, at=part_at + 20480)
        mix = A("mix", [P, TT, D], at=part_at + 38912)
        mix_t = A("mix_t", [P, TT, D], at=part_at + 47104)
        hn = A("hn", [P, TT, D], at=part_at + 53248)
        A = Arena()
        ffT_h = A("ffT_h", [P, FFC, SEQ], F32R)
        ffT_l = A("ffT_l", [P, FFC, SEQ], F32R)
        ff_u = A("ff_u", [P, 2, 4, SEQ])
        ff_a = A("ff_a", [P, 4, SEQ])
        conv_in = A("conv_in", [P, 4, P])
        conv_c = A("conv_c", [P, 4, 2 * FFC])
        ff_y = A("ff_y", [P, TT, D], at=A.at - size_of([P, 4, 2 * FFC]) - 2048 - 4096 - 8192)
        ff_sq = A("ff_sq", [P, TT, D], at=arena)

        rope_t = nc.alloc_sbuf_tensor_at("rope_t", [P, 4, 256], F32, offset=gb_at)

        stage_done = sem("stage_done")
        raw_ready = [sem(f"raw_ready{i}") for i in range(RAW)]
        hi_done, lo_done, block_used, acc_free = (sem(n) for n in ("hi_done", "lo_done", "block_used", "acc_free"))
        x_in, consts_in, params_in = sem("x_in"), sem("consts_in"), sem("params_in")
        turned, turned_hi, turned_lo = sem("turned"), sem("turned_hi"), sem("turned_lo")
        vector_order, scalar_order = sem("vector_order"), sem("scalar_order")
        to_scalar, to_vector, to_tensor = sem("to_scalar"), sem("to_vector"), sem("to_tensor")
        flag_ready, out_ready, out_done = sem("flag_ready"), sem("out_ready"), sem("out_done")
        att_scores, att_max, att_probs, att_turned, att_pt_a, att_pt_v, att_pv, att_out = (
            sem("att_" + n) for n in ("scores", "max", "probs", "turned", "pt_a", "pt_v", "pv", "out"))
        ret_scores, ret_decayed, ret_pv, ret_out = (sem("ret_" + n) for n in ("scores", "decayed", "pv", "out"))
        conv_first, ff_product, ff_gelu, ff_hi = (sem(n) for n in ("conv_first", "ff_product", "ff_gelu", "ff_hi"))
        conv_done = sem("conv_done")
        moe_names = ("silu_done", "h_done", "gathered", "xg_hi", "xg_lo", "h_turned", "h_hi", "h_lo", "y_hi", "y_lo",
                     "wg_done", "wg_out", "pick_ready", "pickT_ready", "scattered")

        class Sweep:

            def __init__(self, tag, ring):
                (self.silu_done, self.h_done, self.gathered, self.xg_hi, self.xg_lo, self.h_turned, self.h_hi,
                 self.h_lo, self.y_hi, self.y_lo, self.wg_done, self.wg_out, self.pick_ready, self.pickT_ready,
                 self.scattered) = (sem(f"{n}_{tag}") for n in moe_names)
                self.raw_ready, self.hi_done, self.lo_done, self.block_used = ring

        ring = (raw_ready, hi_done, lo_done, block_used)
        sweep_first = Sweep("first", ring)
        sweep_second = [Sweep(f"second{i}", ([sem(f"raw_ready{k}_second{i}") for k in range(RAW)],
                                             sem(f"hi_done_second{i}"), sem(f"lo_done_second{i}"),
                                             sem(f"block_used_second{i}"))) for i in range(DEPTH)]

        blocks, columns = [0], [0]

        def linear(n, groups, sources):
            l = Linear(blocks[0], columns[0], n, groups, sources)
            blocks[0] += n * len(groups)
            columns[0] += n
            return l

        def plain(W, first=0):
            def sources(j, turn):
                at = first + BW * j + BW * 3 * turn
                wide = min(BW, W.shape[1] - first - BW * j) if isinstance(turn, int) else BW
                return [(W[:, bass.ds(at, wide)], 0, wide)]
            return sources

        def up_sources(j, turn):
            W = a["w_up_2"][0]
            if j < 10:
                at = (j // 2) * BW + D_FF * (j % 2)
                return [(W[:, at:at + BW], 0, BW)]
            return [(W[:, 5 * BW:D_FF], 0, BW // 2), (W[:, D_FF + 5 * BW:2 * D_FF], BW // 2, BW // 2)]

        l_ret_in = linear(12, [4, 4], plain(a["ret_w_in"][0]))
        l_ret_out = linear(2, [4, 4, 4, 4], plain(a["ret_w_out"][0]))
        moe_b0 = [blocks[0]]
        blocks[0] += 6 * E
        l_nsa_kv = linear(3, [4, 4], plain(a["nsa_w_kv"]))
        l_nsa_in = linear(3, [4, 4], plain(a["nsa_w_in"][0]))
        l_nsa_out = linear(2, [4, 4], plain(a["nsa_w_out"][0]))
        moe_b0.append(blocks[0])
        blocks[0] += 6 * E
        l_a_in = linear(3, [4, 4], plain(a["w_in_2"][0]))
        l_b_in = linear(9, [4, 4], plain(a["w_in_2"][0], 3 * BW))
        l_gates = linear(4, [4, 4], plain(a["w_in_2"][0], 12 * BW))
        l_a_out = linear(2, [4], plain(a["w_a_out_2"][0]))
        l_b_out = linear(2, [4], plain(a["w_b_out_2"][0]))
        l_mix = linear(2, [4, 4], plain(a["w_mix_out_2"][0]))
        l_up = linear(11, [4, 4], up_sources)
        l_down = linear(2, [4, 4, 4, 4, 4, 2], plain(a["w_down_2"][0]))
        two_piece = [l_up.b0 + 20, l_up.b0 + 21]

        def stage_end(eng, st, stages=None):
            st.stage += 1
            eng.drain().then_inc(stage_done, 1)
            eng.wait_ge(stage_done, 3 * st.stage)

        def inbox(eng, st):
            st.hand += 1
            eng.wait_ge(st.inbox, st.hand)

        def hand(eng, s):
            eng.drain().then_inc(s, 1)

        def cols_loop(eng, l, body):
            if not l.looped:
                for j in range(l.n):
                    body(j, 0)
                return
            for j in range(3):
                body(j, 0)
            with eng.Fori(1, l.n // 3) as turn:
                for j in range(3):
                    body(j, turn)

        def is_first(turn):
            return isinstance(turn, int) and turn == 0

        def raw_value(b, turn):
            extra = sum(1 for t in two_piece if t % RAW == b % RAW and t <= b)
            return 16 * (b // RAW + 1 + extra) + 16 * turn

        def load_block(sp, s, b, turn, pieces):
            slot = b % RAW
            if not is_first(turn) or b >= RAW:
                sp.wait_ge(s.lo_done, b - RAW + 1 + RAW * turn)
            for src, kc, at, wide in pieces:
                sp.dma_start(raw[:, slot, 0:kc, at:at + wide],
                             src.rearrange("(c p) n -> p c n", p=P)).then_inc(s.raw_ready[slot], 16)

        def split_hi(act, s, b, turn, kc=KC, wide=BW):
            slot, q = b % RAW, b % SPLIT
            act.wait_ge(s.raw_ready[slot], raw_value(b, turn))
            if not is_first(turn) or b >= SPLIT:
                act.wait_ge(s.block_used, b - SPLIT + 1 + RAW * turn)
            nc.scalar.activation(whi[:, q, 0:kc, 0:wide], raw[:, slot, 0:kc, 0:wide], ACT.Copy).then_inc(s.hi_done, 1)

        def split_lo(dve, s, b, turn, kc=KC, wide=BW):
            slot, q = b % RAW, b % SPLIT
            dve.wait_ge(s.hi_done, b + 1 + RAW * turn)
            nc.vector.tensor_tensor(wlo[:, q, 0:kc, 0:wide], raw[:, slot, 0:kc, 0:wide], whi[:, q, 0:kc, 0:wide],
                                    ALU.subtract).then_inc(s.lo_done, 1)

        def width_of(l, j, turn):
            return max(at + wide for _, at, wide in l.sources(j, turn))

        def linear_sync(sp, l):
            def body(j, turn):
                for kb, kc in enumerate(l.groups):
                    row = sum(l.groups[:kb]) * P
                    load_block(sp, sweep_first, l.b0 + len(l.groups) * j + kb, turn,
                               [(src[row:row + kc * P, :], kc, at, wide) for src, at, wide in l.sources(j, turn)])
            cols_loop(sp, l, body)

        def linear_tensor(pe, l, xh, xl, channels=False):
            nk = len(l.groups)

            def body(j, turn):
                p = j % 3
                if not is_first(turn) or j >= 3:
                    pe.wait_ge(acc_free, 2 * (l.n0 + j - 2) + 6 * turn)
                wide = width_of(l, j, turn)
                for kb, kc in enumerate(l.groups):
                    b = l.b0 + nk * j + kb
                    pe.wait_ge(lo_done, b + 1 + RAW * turn)
                    c0, q = sum(l.groups[:kb]), b % SPLIT
                    if channels:
                        for m in range(4):
                            for c in range(kc):
                                for i, (w, x) in enumerate(((whi, xh), (wlo, xh), (whi, xl))):
                                    last = nc.tensor.matmul(
                                        PS[:, 2 * p + m // 2, (m % 2) * SEQ:(m % 2 + 1) * SEQ],
                                        w[:, q, c, m * P:(m + 1) * P], x[:, c0 + c, :],
                                        start=(kb == 0 and c == 0 and i == 0 and m % 2 == 0),
                                        stop=(kb == nk - 1 and c == kc - 1 and i == 2), skip_group_check=True)
                    else:
                        for tt in range(TT):
                            for c in range(kc):
                                for i, (x, w) in enumerate(((xh, whi), (xh, wlo), (xl, whi))):
                                    last = nc.tensor.matmul(
                                        PS[:, 2 * p + tt, 0:wide], x[:, c0 + c, tt * P:(tt + 1) * P],
                                        w[:, q, c, 0:wide], start=(kb == 0 and c == 0 and i == 0),
                                        stop=(kb == nk - 1 and c == kc - 1 and i == 2))
                    last.then_inc(block_used, 1)
            cols_loop(pe, l, body)

        def linear_side(eng, l, split, evacuate=None):
            nk = len(l.groups)

            def take(j, turn):
                if evacuate is not None:
                    eng.wait_ge(block_used, l.b0 + nk * (j + 1) + RAW * turn)
                    evacuate(j, turn)

            def body(j, turn):
                for kb, kc in enumerate(l.groups):
                    split(eng, sweep_first, l.b0 + nk * j + kb, turn, kc, width_of(l, j, turn))
                if j > 0 or not is_first(turn):
                    take(j - 1, turn)
            cols_loop(eng, l, body)
            take(l.n - 1, 0)

        def scalar_evacuate(dst, func=ACT.Copy, scale=1.0):
            def evacuate(j, turn):
                for tt in range(TT):
                    o = dst[:, j + 3 * turn, tt, :] if is_first(turn) else dst[:, bass.ds(3 * turn + j, 1), tt, :]
                    src = PS[:, 2 * (j % 3) + tt, :]
                    if not is_first(turn):
                        src = src.unsqueeze(1)
                    nc.scalar.activation(o, src, func, scale=scale).then_inc(acc_free, 1)
            return evacuate

        def turn_tensor(pe, st, source, chunks):
            for c in range(0, chunks, 2):
                if c >= 16:
                    pe.wait_ge(turned_lo, st.turn - 7)
                st.turn += 1
                for i in range(2):
                    for tt in range(TT):
                        last = nc.tensor.transpose(
                            PS[:, (c // 2) % 8, i * SEQ + tt * P:i * SEQ + (tt + 1) * P], source(tt, c + i), ident)
                last.then_inc(turned, 1)

        def turn_scalar(act, st, hi, chunks):
            for c in range(0, chunks, 2):
                st.turn += 1
                act.wait_ge(turned, st.turn)
                nc.scalar.activation(hi[:, c:c + 2, :].rearrange("p c t -> p (c t)"), PS[:, (c // 2) % 8, :],
                                     ACT.Copy).then_inc(turned_hi, 1)

        def turn_vector(dve, st, hi, lo, chunks):
            for c in range(0, chunks, 2):
                st.turn += 1
                dve.wait_ge(turned_hi, st.turn)
                if lo is None:
                    nc.vector.drain().then_inc(turned_lo, 1)
                else:
                    nc.vector.tensor_tensor(lo[:, c:c + 2, :].rearrange("p c t -> p (c t)"), PS[:, (c // 2) % 8, :],
                                            hi[:, c:c + 2, :].rearrange("p c t -> p (c t)"),
                                            ALU.subtract).then_inc(turned_lo, 1)

        def root_scalar(act, st, cols):
            inbox(act, st)
            nc.scalar.activation(small[:, cols], small[:, cols], ACT.Sqrt).then_inc(to_vector, 1)

        def root_vector(dve, st, o, cols):
            hand(dve, to_scalar)
            inbox(dve, st)
            o.then(nc.vector.reciprocal(small[:, cols], small[:, cols]))

        def layer_norm_vector(dve, st, o):
            o.wait()
            for tt in range(TT):
                for h in range(2):
                    o(nc.vector.bn_stats(small[:, 16 + 12 * tt + 6 * h:22 + 12 * tt + 6 * h],
                                         X[:, tt, 512 * h:512 * h + 512]))
            o.wait()
            for tt in range(TT):
                o(nc.vector.bn_aggr(small[:, 2 * tt:2 * tt + 2], small[:, 16 + 12 * tt:28 + 12 * tt]))
            o.wait()
            for tt in range(TT):
                o(nc.vector.tensor_scalar(small[:, 8 + tt:9 + tt], small[:, 2 * tt + 1:2 * tt + 2], LN_EPS, None,
                                          ALU.add))
            root_vector(dve, st, o, slice(8, 8 + TT))
            dve.wait_ge(params_in, 16 * st.params)
            for tt in range(TT):
                o(nc.vector.tensor_scalar(X[:, tt, :], X[:, tt, :], small[:, 2 * tt:2 * tt + 1],
                                          small[:, 8 + tt:9 + tt], ALU.subtract, ALU.mult))
            o.wait()
            for tt in range(TT):
                o(nc.vector.tensor_tensor(X[:, tt, :], X[:, tt, :], gb[:, 0, :], ALU.mult))
            o.wait()
            for tt in range(TT):
                o(nc.vector.tensor_tensor(X[:, tt, :], X[:, tt, :], gb[:, 1, :], ALU.add))
            o.wait()

        def rope_vector(dve, o, x, cos, sin, heads, half):
            c = cos.unsqueeze(1).broadcast_to([P, heads, half])
            s = sin.unsqueeze(1).broadcast_to([P, heads, half])
            t = [rope_t[:, i, 0:heads * half].rearrange("p (h d) -> p h d", h=heads) for i in range(4)]
            x1, x2 = x[:, :, 0, :], x[:, :, 1, :]
            o.wait()
            for i, (u, v) in enumerate(((x1, c), (x2, s), (x2, c), (x1, s))):
                o(nc.vector.tensor_tensor(t[i], u, v, ALU.mult))
            o.wait()
            o(nc.vector.tensor_tensor(x1, t[0], t[1], ALU.subtract))
            o(nc.vector.tensor_tensor(x2, t[2], t[3], ALU.add))

        def ret_pairs():
            return [(0, 0), (0, 1), (1, 1)]

        def retention_tensor(pe, st):
            def products(h):
                if h >= 2:
                    pe.wait_ge(ret_decayed, h - 1)
                for i, (kt, qt) in enumerate(ret_pairs()):
                    for c in range(2):
                        last = nc.tensor.matmul(PS[:, h % 2, i * P:(i + 1) * P],
                                                ret_qkT[:, 8 + 2 * h + c, kt * P:(kt + 1) * P],
                                                ret_qkT[:, 2 * h + c, qt * P:(qt + 1) * P],
                                                start=(c == 0), stop=(c == 1))
                last.then_inc(ret_scores, 1)

            products(0)
            for h in range(RET_H):
                if h + 1 < RET_H:
                    products(h + 1)
                pe.wait_ge(ret_decayed, h + 1)
                if h >= 2:
                    pe.wait_ge(ret_out, 2 * (h - 1))
                sd = ret_sd[:, h % 2]
                v = [ret_proj[:, 4 + h, kt, :] for kt in range(2)]
                nc.tensor.matmul(PS[:, 2 + 2 * (h % 2), :], sd[:, 0, :], v[0], start=True, stop=True)
                nc.tensor.matmul(PS[:, 3 + 2 * (h % 2), :], sd[:, 1, :], v[0], start=True, stop=False)
                nc.tensor.matmul(PS[:, 3 + 2 * (h % 2), :], sd[:, 2, :], v[1], start=False,
                                 stop=True).then_inc(ret_pv, 1)

        def retention_scalar(act, st):
            for h in range(RET_H):
                root_scalar(act, st, slice(8, 10))

        def retention_vector(dve, st, o):
            def decay(h):
                dve.wait_ge(ret_scores, h + 1)
                if h >= 2:
                    dve.wait_ge(ret_pv, h - 1)
                nc.vector.tensor_tensor(ret_sd[:, h % 2].rearrange("p a b -> p (a b)"), PS[:, h % 2, 0:3 * P],
                                        ret_c[:, R_DECAY + 3 * P * h:R_DECAY + 3 * P * (h + 1)],
                                        ALU.mult).then_inc(ret_decayed, 1)

            decay(0)
            for h in range(RET_H):
                if h + 1 < RET_H:
                    decay(h + 1)
                dve.wait_ge(ret_pv, h + 1)
                for qt in range(TT):
                    o(nc.vector.bn_stats(small[:, 16 + 6 * qt:22 + 6 * qt], PS[:, 2 + 2 * (h % 2) + qt, :]))
                o.wait()
                for qt in range(TT):
                    o(nc.vector.bn_aggr(small[:, 2 * qt:2 * qt + 2], small[:, 16 + 6 * qt:22 + 6 * qt]))
                o.wait()
                for qt in range(TT):
                    o(nc.vector.tensor_scalar(small[:, 8 + qt:9 + qt], small[:, 2 * qt + 1:2 * qt + 2], LN_EPS, None,
                                              ALU.add))
                root_vector(dve, st, o, slice(8, 10))
                for qt in range(TT):
                    nc.vector.tensor_scalar(ret_o[:, qt, h, :], PS[:, 2 + 2 * (h % 2) + qt, :],
                                            small[:, 2 * qt:2 * qt + 1], small[:, 8 + qt:9 + qt],
                                            ALU.subtract, ALU.mult).then_inc(ret_out, 1)
                dve.wait_ge(ret_out, 2 * (h + 1))
                for qt in range(TT):
                    o(nc.vector.tensor_tensor(ret_o[:, qt, h, :], ret_o[:, qt, h, :], ret_proj[:, 8 + h, qt, :],
                                              ALU.mult))
            o.wait()

        def residual_evacuate(o, factor):
            def evacuate(j, turn):
                for tt in range(TT):
                    x = X[:, tt, j * BW:(j + 1) * BW]
                    nc.vector.scalar_tensor_tensor(x, x, factor, PS[:, 2 * (j % 3) + tt, :], ALU.mult,
                                                   ALU.add).then_inc(acc_free, 1)
            return evacuate

        def router_tensor_logits(pe):
            for tt in range(TT):
                for c in range(DC):
                    for i, (x, w) in enumerate(((th, rwh), (th, rwl), (tl, rwh))):
                        last = nc.tensor.matmul(PS[:, 0, tt * E:(tt + 1) * E], x[:, c, tt * P:(tt + 1) * P],
                                                w[:, c, :], start=(c == 0 and i == 0), stop=(c == DC - 1 and i == 2))
            hand(pe, to_scalar)

        def router_tensor(pe, st):
            router_tensor_logits(pe)
            inbox(pe, st)
            nc.tensor.matmul(PS[:, 1, 0:E], before, picked[:, 0, :], start=True, stop=True)
            nc.tensor.matmul(PS[:, 1, E:2 * E], ones, picked[:, 0, :], start=True, stop=False)
            nc.tensor.matmul(PS[:, 1, E:2 * E], before, picked[:, 1, :], start=False, stop=True)
            nc.tensor.matmul(PS[:, 2, 0:E], ones, picked[:, 0, :], start=True, stop=False)
            nc.tensor.matmul(PS[:, 2, 0:E], ones, picked[:, 1, :], start=False, stop=True)
            hand(pe, to_vector)
            inbox(pe, st)
            for e in range(E):
                for tt in range(TT):
                    at = (e % 2) * SEQ + tt * P
                    nc.tensor.matmul(PS[:, e // 2, at:at + P], slot_r[:, tt, e:e + 1].broadcast_to([P, P]),
                                     ident_r[:, :], start=True, stop=True)

        def router_scalar(act, st):
            inbox(act, st)
            nc.scalar.activation(affinity.rearrange("p t e -> p (t e)"), PS[:, 0, 0:TT * E],
                                 ACT.Sigmoid).then_inc(to_vector, 1)

        def router_vector(dve, st, o):
            def wide(v, *shape):
                for _ in range(len(shape) - len(v.shape)):
                    v = v.unsqueeze(len(v.shape))
                return v.broadcast_to(list(shape))

            inbox(dve, st)
            o.then(nc.vector.tensor_tensor(score, affinity, rb[:, :].unsqueeze(1).broadcast_to([P, TT, E]), ALU.add))
            s4 = score.rearrange("p t (g e) -> p t g e", e=E_PER)
            pr = [pairs[:, i] for i in range(8)]
            o(nc.vector.tensor_tensor(pr[0], s4[:, :, :, 0], s4[:, :, :, 1], ALU.max))
            o(nc.vector.tensor_tensor(pr[1], s4[:, :, :, 0], s4[:, :, :, 1], ALU.min))
            o(nc.vector.tensor_tensor(pr[2], s4[:, :, :, 2], s4[:, :, :, 3], ALU.max))
            o(nc.vector.tensor_tensor(pr[3], s4[:, :, :, 2], s4[:, :, :, 3], ALU.min))
            o.wait()
            o(nc.vector.tensor_tensor(pr[4], pr[0], pr[2], ALU.max))
            o(nc.vector.tensor_tensor(pr[5], pr[0], pr[2], ALU.min))
            o(nc.vector.tensor_tensor(pr[6], pr[1], pr[3], ALU.max))
            o.wait()
            o.then(nc.vector.tensor_tensor(pr[7], pr[5], pr[6], ALU.max))
            o.then(nc.vector.tensor_tensor(pr[0], pr[4], pr[7], ALU.add))
            top = [tops[:, i] for i in range(4)]
            i4 = cst[:, C_I4:C_I4 + 4].unsqueeze(1).broadcast_to([P, TT, E_GROUPS])
            i16 = cst[:, C_I16:C_I16 + E].unsqueeze(1).broadcast_to([P, TT, E])
            o.then(nc.vector.tensor_reduce(top[0], pr[0], AX.X, ALU.max))
            o.then(nc.vector.tensor_tensor(pr[1], pr[0], wide(top[0], P, TT, E_GROUPS), ALU.is_ge))
            o.then(nc.vector.tensor_scalar(pr[2], pr[1], -99.0, 99.0, ALU.mult, ALU.add))
            o.then(nc.vector.tensor_tensor(pr[3], pr[2], i4, ALU.add))
            o.then(nc.vector.tensor_reduce(top[1], pr[3], AX.X, ALU.min))
            o.then(nc.vector.tensor_tensor(pr[4], i4, wide(top[1], P, TT, E_GROUPS), ALU.is_equal))
            o.then(nc.vector.tensor_scalar(pr[5], pr[4], -NEG, NEG, ALU.mult, ALU.add))
            m4 = rt1.rearrange("p t (g e) -> p t g e", e=E_PER)
            for tt in range(TT):
                o(nc.vector.tensor_tensor(m4[:, tt], s4[:, tt], wide(pr[4][:, tt], P, E_GROUPS, E_PER), ALU.mult))
            o.wait()
            for tt in range(TT):
                o(nc.vector.tensor_tensor(m4[:, tt], m4[:, tt], wide(pr[5][:, tt], P, E_GROUPS, E_PER), ALU.add))
            o.wait()
            for k in range(2):
                o.then(nc.vector.tensor_reduce(top[0], rt1, AX.X, ALU.max))
                o.then(nc.vector.tensor_tensor(rt2, rt1, wide(top[0], P, TT, E), ALU.is_ge))
                o.then(nc.vector.tensor_scalar(rt3, rt2, -99.0, 99.0, ALU.mult, ALU.add))
                o.then(nc.vector.tensor_tensor(rt2, rt3, i16, ALU.add))
                o.then(nc.vector.tensor_reduce(top[1], rt2, AX.X, ALU.min))
                if k == 0:
                    o.then(nc.vector.tensor_tensor(picked, i16, wide(top[1], P, TT, E), ALU.is_equal))
                    o.then(nc.vector.scalar_tensor_tensor(rt1, picked, 3.0 * NEG, rt1, ALU.mult, ALU.add))
                else:
                    o.then(nc.vector.tensor_tensor(rt3, i16, wide(top[1], P, TT, E), ALU.is_equal))
                    o.then(nc.vector.tensor_tensor(picked, picked, rt3, ALU.add))
            hand(dve, to_tensor)
            o.then(nc.vector.tensor_tensor(w_tok, affinity, picked, ALU.mult))
            o.then(nc.vector.tensor_reduce(top[2], w_tok, AX.X, ALU.add))
            o.then(nc.vector.reciprocal(top[3], top[2]))
            o.then(nc.vector.tensor_tensor(w_tok, w_tok, wide(top[3], P, TT, E), ALU.mult))
            o.then(nc.vector.tensor_copy(w_split[:, :, :, 0], w_tok))
            o(nc.vector.tensor_tensor(w_split[:, :, :, 1], w_tok, w_split[:, :, :, 0], ALU.subtract))
            inbox(dve, st)
            o.then(nc.vector.scalar_tensor_tensor(rt2.rearrange("p t e -> p (t e)"), PS[:, 1, 0:TT * E], 1.0,
                                                  picked.rearrange("p t e -> p (t e)"), ALU.add, ALU.mult))
            o.then(nc.vector.tensor_scalar(slot_no, rt2, -1.0, None, ALU.add))
            o.then(nc.vector.tensor_copy(slot_r[:, :, :], slot_no))
            o.then(nc.vector.tensor_reduce(top[0][:, 0:1], PS[:, 2, 0:E], AX.X, ALU.max))
            hand(dve, to_tensor)
            o.then(nc.vector.tensor_scalar(top[1][:, 0:1], top[0][:, 0:1], float(P) + 0.5, None, ALU.is_gt))
            o.then(nc.vector.tensor_copy(flag_i[:, 0:1], top[1][:, 0:1]))
            hand(dve, flag_ready)

        def expert_blocks(layer, e):
            gate, up, down = (a[n][layer] for n in ("moe_w_gate", "moe_w_up", "moe_w_down"))

            def of(W):
                return W[e] if isinstance(e, int) else W[bass.ds(e, 1)].rearrange("a k n -> (a k) n")
            g, u, d = of(gate), of(up), of(down)
            half = KC * P
            return [g[0:half], g[half:], u[0:half], u[half:], d[:, BW:], d[:, 0:BW]]

        def experts_loop(eng, body):
            body(0, True, False)
            with eng.Fori(1, E - 1) as e:
                body(e, False, False)
            body(E - 1, False, True)

        def sweep_sync(sp, s, layer, b0):
            def body(e, first, last):
                for i, src in enumerate(expert_blocks(layer, e)):
                    if isinstance(e, int):
                        load_block(sp, s, b0 + RAW * e + i, 0, [(src, KC, 0, BW)])
                    else:
                        load_block(sp, s, b0 + i, e, [(src, KC, 0, BW)])
            experts_loop(sp, body)

        def at_block(b0, i, e):
            return (b0 + i + RAW * e, 0) if isinstance(e, int) else (b0 + i, e)

        def sweep_tensor(pe, s, b0, v0, second):
            def gather(v, half):
                for c in range(4 * half, 4 * half + 4):
                    for i, (x, tt) in enumerate(((xn_h, 0), (xn_l, 0), (xn_h, 1), (xn_l, 1))):
                        last = nc.tensor.matmul(PS[:, 6 + half, (c % 4) * P:(c % 4 + 1) * P],
                                                x[:, tt, c * P:(c + 1) * P], pick[:, tt, :],
                                                start=(i == 0), stop=(i == 3))
                last.then_inc(s.gathered, 1)

            def product(bank, b, turn, x0, xh, xl, start, stop):
                pe.wait_ge(s.lo_done, b + 1 + RAW * turn)
                q = b % SPLIT
                for c in range(KC):
                    for i, (x, w) in enumerate(((xh, whi), (xh, wlo), (xl, whi))):
                        last = nc.tensor.matmul(PS[:, bank, :], x[:, x0 + c, :], w[:, q, c, :],
                                                start=(start and c == 0 and i == 0),
                                                stop=(stop and c == KC - 1 and i == 2))
                last.then_inc(s.block_used, 1)

            def scatter(v):
                pe.wait_ge(s.pickT_ready, v)
                pe.wait_ge(s.y_lo, 2 * v)
                for tt in range(TT):
                    for half in range(2):
                        for y in (y_h, y_l):
                            last = nc.tensor.matmul(PS[:, 2 * tt + half, :], pickT[:, tt * P:(tt + 1) * P],
                                                    y[:, half, :], start=False, stop=False, skip_group_check=True)
                last.then_inc(s.scattered, 1)

            def body(e, first, last_one):
                v = v0 + e
                blk = [at_block(b0, i, e) for i in range(6)]
                pe.wait_ge(s.xg_lo, 2 * v + 2)
                if not first:
                    pe.wait_ge(s.y_lo, 2 * v - 1)
                product(4, *blk[0], 0, xg_h, xg_l, True, False)
                product(4, *blk[1], 4, xg_h, xg_l, False, True)
                if not first:
                    pe.wait_ge(s.y_lo, 2 * v)
                for tt in range(TT):
                    w = w_split[:, tt, e, :] if isinstance(e, int) else \
                        w_split[:, tt, bass.ds(e, 1), :].rearrange("p a b -> p (a b)")
                    m = nc.tensor.matmul(PS[:, 5, 0:2], pick[:, tt, :], w, start=(tt == 0), stop=(tt == 1))
                m.then_inc(s.wg_done, 1)
                if not first:
                    scatter(v)
                pe.wait_ge(s.wg_out, v + 1)
                product(5, *blk[2], 0, xg_h, xg_l, True, False)
                product(5, *blk[3], 4, xg_h, xg_l, False, True)
                if not last_one:
                    pe.wait_ge(s.pick_ready, v + 2)
                    gather(v + 1, 0)
                pe.wait_ge(s.h_done, v + 1)
                for f in range(4):
                    m = nc.tensor.transpose(PS[:, 4, f * P:(f + 1) * P], hbuf[:, f * P:(f + 1) * P], ident)
                m.then_inc(s.h_turned, 1)
                if not last_one:
                    gather(v + 1, 1)
                pe.wait_ge(s.h_lo, v + 1)
                product(4, *blk[4], 0, hT_h, hT_l, True, True)
                product(5, *blk[5], 0, hT_h, hT_l, True, True)

            if not second:
                for bank in range(4):
                    nc.tensor.matmul(PS[:, bank, :], zero_r[:, :], xn_h[:, 0, 0:512], start=True, stop=False,
                                     skip_group_check=True)
            pe.wait_ge(s.pick_ready, v0 + 1)
            gather(v0, 0)
            gather(v0, 1)
            experts_loop(pe, body)
            scatter(v0 + E)

        def sweep_scalar(act, s, b0, v0):
            def xg(n, half):
                act.wait_ge(s.gathered, n)
                nc.scalar.activation(xg_h[:, 4 * half:4 * half + 4, :].rearrange("p c j -> p (c j)"),
                                     PS[:, 6 + half, :], ACT.Copy).then_inc(s.xg_hi, 1)

            def y(v, half, b, turn):
                act.wait_ge(s.block_used, b + 1 + RAW * turn)
                nc.scalar.activation(y_h[:, half, :], PS[:, 5 - half, :], ACT.Identity,
                                     scale=w_slot[:, 0:1]).then_inc(s.y_hi, 1)

            def body(e, first, last_one):
                v = v0 + e
                blk = [at_block(b0, i, e) for i in range(9)]
                split_hi(act, s, *blk[3])
                act.wait_ge(s.block_used, blk[1][0] + 1 + RAW * blk[1][1])
                if not first:
                    act.wait_ge(s.h_done, v)
                nc.scalar.activation(silu[:, :], PS[:, 4, :], ACT.Silu).then_inc(s.silu_done, 1)
                split_hi(act, s, *blk[4])
                split_hi(act, s, *blk[5])
                if not last_one:
                    xg(2 * v + 3, 0)
                    split_hi(act, s, *blk[6])
                act.wait_ge(s.h_turned, v + 1)
                nc.scalar.activation(hT_h[:, :, :].rearrange("p f j -> p (f j)"), PS[:, 4, :],
                                     ACT.Copy).then_inc(s.h_hi, 1)
                if not last_one:
                    xg(2 * v + 4, 1)
                act.wait_ge(s.wg_out, v + 1)
                y(v, 1, *blk[4])
                if not last_one:
                    split_hi(act, s, *blk[7])
                y(v, 0, *blk[5])
                if not last_one:
                    split_hi(act, s, *blk[8])

            for i in range(3):
                split_hi(act, s, b0 + i, 0)
            xg(2 * v0 + 1, 0)
            xg(2 * v0 + 2, 1)
            experts_loop(act, body)

        def sweep_vector(dve, s, b0, v0, second):
            slots = cst[:, C_ROW + P * second:C_ROW + P * second + P]

            def xg(n, half):
                dve.wait_ge(s.xg_hi, n)
                nc.vector.tensor_tensor(xg_l[:, 4 * half:4 * half + 4, :].rearrange("p c j -> p (c j)"),
                                        PS[:, 6 + half, :],
                                        xg_h[:, 4 * half:4 * half + 4, :].rearrange("p c j -> p (c j)"),
                                        ALU.subtract).then_inc(s.xg_lo, 1)

            def y(n, half):
                dve.wait_ge(s.y_hi, n)
                nc.vector.scalar_tensor_tensor(y_l[:, half, :], PS[:, 5 - half, :], w_slot[:, 0:1], y_h[:, half, :],
                                               ALU.mult, ALU.subtract).then_inc(s.y_lo, 1)

            def selection(e):
                for tt in range(TT):
                    mine = slot_no[:, tt, e:e + 1] if isinstance(e, int) else slot_no[:, tt, bass.ds(e, 1)]
                    last = nc.vector.tensor_scalar(pick[:, tt, :], slots, mine, None, ALU.is_equal)
                last.then_inc(s.pick_ready, 1)

            def body(e, first, last_one):
                v = v0 + e
                blk = [at_block(b0, i, e) for i in range(9)]
                split_lo(dve, s, *blk[3])
                dve.wait_ge(s.wg_done, v + 1)
                nc.vector.tensor_reduce(w_slot[:, 0:1], PS[:, 5, 0:2], AX.X, ALU.add).then_inc(s.wg_out, 1)
                if not last_one:
                    selection(e + 1)
                if not first:
                    dve.wait_ge(s.scattered, v)
                rows = slot_of[:, e, :] if isinstance(e, int) else \
                    slot_of[:, bass.ds(e, 1), :].rearrange("p a b -> p (a b)")
                nc.vector.tensor_scalar(pickT[:, :], rows, cst[:, C_COL + second:C_COL + second + 1], None,
                                        ALU.is_equal).then_inc(s.pickT_ready, 1)
                split_lo(dve, s, *blk[4])
                split_lo(dve, s, *blk[5])
                dve.wait_ge(s.silu_done, v + 1)
                dve.wait_ge(s.block_used, blk[3][0] + 1 + RAW * blk[3][1])
                nc.vector.tensor_tensor(hbuf[:, :], silu[:, :], PS[:, 5, :], ALU.mult).then_inc(s.h_done, 1)
                if not last_one:
                    xg(2 * v + 3, 0)
                    split_lo(dve, s, *blk[6])
                dve.wait_ge(s.h_hi, v + 1)
                nc.vector.tensor_tensor(hT_l[:, :, :].rearrange("p f j -> p (f j)"), PS[:, 4, :],
                                        hT_h[:, :, :].rearrange("p f j -> p (f j)"), ALU.subtract).then_inc(s.h_lo, 1)
                if not last_one:
                    xg(2 * v + 4, 1)
                y(2 * v + 1, 1)
                if not last_one:
                    split_lo(dve, s, *blk[7])
                y(2 * v + 2, 0)
                if not last_one:
                    split_lo(dve, s, *blk[8])

            selection(0)
            for i in range(3):
                split_lo(dve, s, b0 + i, 0)
            xg(2 * v0 + 1, 0)
            xg(2 * v0 + 2, 1)
            experts_loop(dve, body)

        class Unit:

            def __init__(self, tt, segs, masks, joint, scale, values, extra=None, finish=None):
                self.tt, self.segs, self.masks, self.joint, self.scale = tt, segs, masks, joint, scale
                self.values, self.extra, self.finish = values, extra, finish
                self.w = P * (tt + 1)
                self.blocks = len(segs) * (tt + 1)
                self.apart = len({q.start_partition() if callable(q.start_partition) else q.start_partition
                                  for q, _ in segs}) > 1

            def scores_at(self, i, k):
                bank, at = (k, 0) if self.apart else (k // 2, (k % 2) * SEQ)
                return PS[:, 2 * (i % 2) + bank, at:at + self.w]

        def attention_tensor(pe, st, units, buf):
            t, pt = buf[0], buf[1]
            u0 = st.unit

            def scores(i):
                u, n = units[i], u0 + i
                if i >= 2:
                    pe.wait_ge(att_max, n - 1)
                for k, (q, key) in enumerate(u.segs):
                    last = nc.tensor.matmul(u.scores_at(i, k), q, key[:, 0:u.w], start=True, stop=True)
                if u.extra:
                    q, key, _, _ = u.extra
                    last = nc.tensor.matmul(PS[:, 2 * (i % 2) + 1, 0:N_CMP], q, key, start=True, stop=True)
                last.then_inc(att_scores, 1)

            scores(0)
            for i, u in enumerate(units):
                n = u0 + i
                if i + 1 < len(units):
                    scores(i + 1)
                pe.wait_ge(att_probs, n + 1)
                if i >= 1:
                    pe.wait_ge(att_pt_a, st.pt_a)
                    pe.wait_ge(att_pt_v, st.pt_v)
                for b in range(u.blocks):
                    k, kt = b // (u.tt + 1), b % (u.tt + 1)
                    last = nc.tensor.transpose(PS[:, 4 + b // 4, (b % 4) * P:(b % 4 + 1) * P],
                                               t[:, i % 2, k, kt * P:(kt + 1) * P], ident)
                if u.extra:
                    last = nc.tensor.transpose(PS[0:N_CMP, 5, 0:P], t[:, i % 2, 2, 0:N_CMP], ident)
                last.then_inc(att_turned, 1)
                st.pt_a += 1
                st.pt_v += 1 if (u.blocks > 4 or u.extra) else 0
                pe.wait_ge(att_pt_a, st.pt_a)
                pe.wait_ge(att_pt_v, st.pt_v)
                if i >= 2:
                    pe.wait_ge(att_out, n - 1)
                o_bank = PS[:, 6 + i % 2, :]
                for k, (at, vals) in enumerate(u.values):
                    for kt in range(u.tt + 1):
                        b = k * (u.tt + 1) + kt
                        width = vals[kt].shape[-1]
                        first = kt == 0 and (k == 0 or not u.joint)
                        final = kt == u.tt and (k == len(u.values) - 1 or not u.joint)
                        last = nc.tensor.matmul(o_bank[:, at:at + width], pt[:, b, :], vals[kt], start=first,
                                                stop=final)
                if u.extra:
                    _, _, at, v = u.extra
                    last = nc.tensor.matmul(o_bank[:, at:at + NSA_DH], pt[0:N_CMP, 5, :], v, start=True, stop=True)
                last.then_inc(att_pv, 1)
            st.unit += len(units)

        def attention_scalar(act, st, units, buf):
            t, pt, top, sums = buf[0:4]
            u0 = st.unit

            def probs(i):
                u = units[i]
                act.wait_ge(att_max, u0 + i + 1)
                if i >= 2:
                    act.wait_ge(att_out, u0 + i - 1)
                s, m, n = t[:, i % 2], top[:, i % 2], sums[:, i % 2]
                if u.joint:
                    x = s[:, 0:len(u.segs), 0:u.w]
                    last = nc.scalar.activation(x, x, ACT.Exp, bias=m[:, 0:1], accum_out=n[:, 0:1])
                else:
                    for k in range(len(u.segs)):
                        x = s[:, k, 0:u.w]
                        last = nc.scalar.activation(x, x, ACT.Exp, bias=m[:, k:k + 1], accum_out=n[:, k:k + 1])
                if u.extra:
                    x = s[:, 2, 0:N_CMP]
                    last = nc.scalar.activation(x, x, ACT.Exp, bias=m[:, 2:3], accum_out=n[:, 2:3])
                last.then_inc(att_probs, 1)

            probs(0)
            for i, u in enumerate(units):
                if i + 1 < len(units):
                    probs(i + 1)
                act.wait_ge(att_turned, u0 + i + 1)
                if i >= 1:
                    act.wait_ge(att_pv, u0 + i)
                w = min(u.blocks, 4)
                nc.scalar.activation(pt[:, 0:w, :].rearrange("p b q -> p (b q)"), PS[:, 4, 0:w * P],
                                     ACT.Copy).then_inc(att_pt_a, 1)
            st.unit += len(units)

        def attention_vector(dve, st, o, units, buf):
            t, pt, top, sums, coef, rec = buf
            u0 = st.unit

            def masked(i):
                u = units[i]
                dve.wait_ge(att_scores, u0 + i + 1)
                if i >= 2:
                    dve.wait_ge(att_turned, u0 + i - 1)
                s, m = t[:, i % 2], top[:, i % 2]
                for k in range(len(u.segs)):
                    o(nc.vector.scalar_tensor_tensor(s[:, k, 0:u.w], u.scores_at(i, k), u.scale, u.masks[k], ALU.mult, ALU.add))
                if u.extra:
                    o(nc.vector.tensor_tensor(s[:, 2, 0:N_CMP], PS[:, 2 * (i % 2) + 1, 0:N_CMP],
                                              n_c[:, N_CMASK + 15 * u.tt:N_CMASK + 15 * u.tt + 15], ALU.add))
                o.wait()
                n = len(u.segs)
                if u.extra:
                    o(nc.vector.tensor_reduce(m[:, 2:3], s[:, 2, 0:N_CMP], AX.X, ALU.max, negate=True))
                if u.joint:
                    last = nc.vector.tensor_reduce(m[:, 0:1], s[:, 0:n, 0:u.w], AX.XY, ALU.max, negate=True)
                else:
                    last = nc.vector.tensor_reduce(m[:, 0:n], s[:, 0:n, 0:u.w], AX.X, ALU.max, negate=True)
                last.then_inc(att_max, 1)

            masked(0)
            for i, u in enumerate(units):
                if i + 1 < len(units):
                    masked(i + 1)
                if u.blocks > 4 or u.extra:
                    dve.wait_ge(att_turned, u0 + i + 1)
                    if i >= 1:
                        dve.wait_ge(att_pv, u0 + i)
                    if u.extra:
                        nc.vector.tensor_copy(pt[0:N_CMP, 5, :], PS[0:N_CMP, 5, 0:P]).then_inc(att_pt_v, 1)
                    else:
                        w = u.blocks - 4
                        nc.vector.tensor_copy(pt[:, 4:4 + w, :].rearrange("p b q -> p (b q)"),
                                              PS[:, 5, 0:w * P]).then_inc(att_pt_v, 1)
                dve.wait_ge(att_pv, u0 + i + 1)
                u.finish(o, u, PS[:, 6 + i % 2, :], sums[:, i % 2], rec[:, i % 2], coef[:, i % 2]).then_inc(att_out, 1)
            dve.wait_ge(att_out, u0 + len(units))
            st.unit += len(units)

        def nsa_rope_vector(dve, st, o):
            dve.wait_ge(params_in, 16 * st.params)
            for tt in range(TT):
                cos, sin = (n_c[:, at + 32 * tt:at + 32 * tt + 32] for at in (N_COS, N_SIN))
                for k in range(3):
                    rope_vector(dve, o, n_kv[:, k, tt, 0:256].rearrange("p (h b d) -> p h b d", h=4, b=2), cos, sin, 4, 32)
                for k in range(2):
                    rope_vector(dve, o, n_q[:, k, tt, :].rearrange("p (h b d) -> p h b d", h=8, b=2), cos, sin, 8, 32)
                g = n_g48[:, tt, :].rearrange("p (h k) -> p k h", k=3)
                o(nc.vector.tensor_copy(n_gate[:, tt, 0, :], g[:, 1, :]))
                o(nc.vector.tensor_copy(n_gate[:, tt, 1, :], g[:, 2, :]))
                o(nc.vector.tensor_scalar(n_gate[:, tt, 2, :], g[:, 0, :], n_c[:, N_VALID + tt:N_VALID + tt + 1], None,
                                          ALU.mult))

        def nsa_double_scalar(act):
            for tt in range(TT):
                for i, (k, at) in enumerate(((0, 0), (0, 256), (1, 0), (2, 0))):
                    src = n_kv[:, k, tt, at:at + 256].rearrange("p (g d) -> p g d", g=NSA_G)
                    for b in range(2):
                        nc.scalar.activation(n_dup[:, tt, i, :, b * NSA_DH:(b + 1) * NSA_DH], src, ACT.Copy)

        def compress_tensor(pe, st):
            inbox(pe, st)
            half = CMP_LEN // 2
            for k in range(2):
                nc.tensor.transpose(PS[:, 0, k * half:(k + 1) * half], cmp_pe[0:half, k, :], cst[0:half, C_ID:C_ID + half])
            hand(pe, to_vector)
            inbox(pe, st)
            for k in range(2):
                for c in range(2):
                    for i in range(half):
                        nc.tensor.matmul(PS[:, 1, (2 * k + c) * 64:(2 * k + c) * 64 + 60],
                                         cmp_w1[k][:, i, c * P:(c + 1) * P], cmp_x[:, k, i, 0:60],
                                         start=(i == 0), stop=(i == half - 1))
            hand(pe, to_scalar)
            inbox(pe, st)
            for c in range(2):
                nc.tensor.matmul(PS[:, 2, 0:60], cmp_w2k[:, c, :, :].rearrange("p b d -> p (b d)"), cmp_h[:, 0, c, :],
                                 start=(c == 0), stop=(c == 1))
            for g in range(NSA_G):
                for c in range(2):
                    nc.tensor.matmul(PS[0:N_CMP, 3, g * NSA_DH:(g + 1) * NSA_DH], cmp_h[:, 1, c, 15 * g:15 * g + 15],
                                     cmp_w2v[:, c, :], start=(c == 0), stop=(c == 1))
            hand(pe, to_vector)

        def compress_scalar(act, st):
            inbox(act, st)
            for k in range(2):
                last = nc.scalar.activation(cmp_h[:, k, :, :], PS[:, 1, k * P:(k + 1) * P].rearrange(
                    "p (c n) -> p c n", c=2)[:, :, 0:60], ACT.Gelu_apprx_tanh)
            last.then_inc(to_tensor, 1)

        def compress_vector(dve, st, o):
            dve.wait_ge(params_in, 16 * st.params)
            hand(dve, to_tensor)
            inbox(dve, st)
            o.then(nc.vector.tensor_copy(cmp_peT[:, :, :].rearrange("p a b -> p (a b)"), PS[:, 0, 0:CMP_LEN]))
            for k in range(2):
                for g in range(NSA_G):
                    for b in range(2):
                        rows = slice(64 * b, 64 * b + 64)
                        tokens = n_T[rows, 4 * k + g, :].rearrange("p (i s b) -> p s i b", s=8, b=2)
                        for h in range(2):
                            o(nc.vector.tensor_tensor(
                                cmp_x[rows, k, 8 * h:8 * h + 8, 15 * g:15 * g + 15], tokens[:, :, h:h + 15, b],
                                cmp_peT[rows, k, 8 * h:8 * h + 8].unsqueeze(2).broadcast_to([64, 8, 15]), ALU.add))
            hand(dve, to_tensor)
            inbox(dve, st)
            o(nc.vector.tensor_copy(cmp_kT[:, 0:60], PS[:, 2, 0:60]))
            o(nc.vector.tensor_copy(cmp_v[0:N_CMP, :, :].rearrange("p g d -> p (g d)"), PS[0:N_CMP, 3, 0:256]))

        def nsa_units():
            def finish(o, u, bank, sums, rec, coef):
                h = u.head
                o.then(nc.vector.reciprocal(rec[:, 0:3], sums[:, 0:3]))
                o.then(nc.vector.tensor_tensor(coef[:, 0:3], rec[:, 0:3], n_gate[:, u.tt, :, h], ALU.mult))
                dst = n_o[:, u.tt, h * NSA_DH:(h + 1) * NSA_DH]
                o.then(nc.vector.tensor_scalar(dst, bank[:, 0:64], coef[:, 0:1], None, ALU.mult))
                o.then(nc.vector.scalar_tensor_tensor(dst, bank[:, 64:128], coef[:, 1:2], dst, ALU.mult, ALU.add))
                return nc.vector.scalar_tensor_tensor(dst, bank[:, 128:192], coef[:, 2:3], dst, ALU.mult, ALU.add)

            units = []
            for h in range(NSA_H):
                g, rows = h // NSA_REP, slice(64 * (h % 2), 64 * (h % 2) + 64)
                for tt in range(TT):
                    q = n_T[rows, 16 + h // 2, tt * P:(tt + 1) * P]
                    mask = n_c[:, N_MASK + SEQ * tt:N_MASK + SEQ * tt + P * (tt + 1)]
                    vals = [[n_kv[:, k, kt, 256 + g * 64:320 + g * 64] for kt in range(2)] for k in (1, 2)]
                    u = Unit(tt, [(q, n_T[rows, 8 + g, :]), (q, n_T[rows, 12 + g, :])], [mask, mask], False,
                             1.0, [(0, vals[0]), (64, vals[1])],
                             (q, cmp_kT[rows, 15 * g:15 * g + 15], 128, cmp_v[0:N_CMP, g, :]), finish)
                    u.head = h
                    units.append(u)
            return units

        def square_scalar(act, st, src, scratch):
            for tt in range(TT):
                nc.scalar.activation(scratch[:, tt], src[:, tt], ACT.Square, accum_out=small[:, 8 + tt:9 + tt])
            hand(act, to_vector)
            root_scalar(act, st, slice(8, 10))

        def rms_vector(dve, st, o, n):
            inbox(dve, st)
            o(nc.vector.tensor_scalar(small[:, 8:10], small[:, 8:10], 1.0 / n, RMS_EPS, ALU.mult, ALU.add))
            root_vector(dve, st, o, slice(8, 10))

        def scaled_rows(dve, o, dst, src, gain):
            o.wait()
            for tt in range(TT):
                o(nc.vector.scalar_tensor_tensor(dst[:, tt, :], src[:, tt, :], small[:, 8 + tt:9 + tt],
                                                 gb[:, gain, :], ALU.mult, ALU.mult))
            o.wait()

        def heads_norm_vector(dve, st, o):
            heads = a_o[:, :, :, :].rearrange("p t h d -> p (t h) d")
            squares = a_sq[:, :, :, :].rearrange("p t h d -> p (t h) d")
            o.then(nc.vector.tensor_tensor(squares, heads, heads, ALU.mult))
            o.then(nc.vector.tensor_reduce(small[:, 48:56], squares, AX.X, ALU.add))
            o.then(nc.vector.tensor_scalar(small[:, 48:56], small[:, 48:56], 1.0 / A_DV, RMS_EPS, ALU.mult, ALU.add))
            root_vector(dve, st, o, slice(48, 56))
            for i in range(8):
                o(nc.vector.scalar_tensor_tensor(heads[:, i, :], heads[:, i, :], small[:, 48 + i:49 + i],
                                                 head_g[:, :], ALU.mult, ALU.mult))
            o.wait()
            o.then(nc.vector.tensor_scalar(a_o[:, :, :, :], a_o[:, :, :, :], 1.0 - LAM_INIT, None, ALU.mult))

        def angles_vector(dve, st, o):
            two_pi = 6.283185307179586
            c1 = 6.28125
            c2 = 0.0019350051879882812
            c3 = two_pi - c1 - c2
            half = 3.1415925
            dve.wait_ge(params_in, 16 * st.params)
            o.then(nc.vector.tensor_copy(pos_f[:, :], pos_i[:, :]))
            for tt in range(TT):
                o(nc.vector.tensor_scalar(ang[:, 0, tt, :], b_c[:, B_INV:B_INV + 96], pos_f[:, tt:tt + 1], None,
                                          ALU.mult))
            o.wait()
            x, k, r, m = (ang[:, i].rearrange("p t f -> p (t f)") for i in range(4))
            o.then(nc.vector.tensor_scalar(k, x, 1.0 / two_pi, ROUND, ALU.mult, ALU.add))
            o.then(nc.vector.tensor_scalar(k, k, -ROUND, None, ALU.add))
            o.then(nc.vector.scalar_tensor_tensor(r, k, -c1, x, ALU.mult, ALU.add))
            o.then(nc.vector.scalar_tensor_tensor(r, k, -c2, r, ALU.mult, ALU.add))
            o.then(nc.vector.scalar_tensor_tensor(r, k, -c3, r, ALU.mult, ALU.add))

            def wrap():
                o.then(nc.vector.tensor_scalar(m, r, two_pi / 2, None, ALU.is_gt))
                o.then(nc.vector.scalar_tensor_tensor(r, m, -two_pi, r, ALU.mult, ALU.add))
                o.then(nc.vector.tensor_scalar(m, r, -two_pi / 2, None, ALU.is_lt))
                o.then(nc.vector.scalar_tensor_tensor(r, m, two_pi, r, ALU.mult, ALU.add))
            wrap()
            o.then(nc.vector.tensor_scalar(x, r, half, -half, ALU.min, ALU.max))
            o.then(nc.vector.tensor_scalar(r, r, two_pi / 4, None, ALU.add))
            wrap()
            o.then(nc.vector.tensor_scalar(k, r, half, -half, ALU.min, ALU.max))

        def a_units():
            def finish(o, u, bank, sums, rec, coef):
                o.then(nc.vector.reciprocal(rec[:, 0:2], sums[:, 0:2]))
                o.then(nc.vector.tensor_tensor(coef[:, 1:2], rec[:, 1:2], small[:, 40:41], ALU.mult))
                dst = a_o[:, u.tt, u.head, :]
                o.then(nc.vector.tensor_scalar(dst, bank[:, 0:P], rec[:, 0:1], None, ALU.mult))
                return nc.vector.scalar_tensor_tensor(dst, bank[:, P:2 * P], coef[:, 1:2], dst, ALU.mult, ALU.add)

            units = []
            for h in range(A_H):
                for tt in range(TT):
                    mask = b_c[:, B_MASK:B_MASK + P] if tt == 0 else b_c[:, B_CAUSAL:B_CAUSAL + SEQ]
                    segs = [(a_qkT[64 * c:64 * c + 64, h, tt * P:(tt + 1) * P], a_qkT[64 * c:64 * c + 64, 4 + h, :])
                            for c in range(2)]
                    vals = [a_proj[:, 2, kt, h * P:(h + 1) * P] for kt in range(2)]
                    u = Unit(tt, segs, [mask, mask], False, A_DQK ** -0.5, [(0, vals), (P, vals)], None, finish)
                    u.head = h
                    units.append(u)
            return units

        def b_units():
            def finish(o, u, bank, sums, rec, coef):
                o.then(nc.vector.reciprocal(rec[:, 0:1], sums[:, 0:1]))
                return nc.vector.tensor_scalar(b_o[:, u.tt, u.head, :], bank[:, 0:P], rec[:, 0:1], None, ALU.mult)

            units = []
            for h in range(B_H):
                for tt in range(TT):
                    masks, segs, values = [], [], []
                    for g in range(B_G):
                        at = B_MASK + 3 * P * g + P * tt
                        masks.append(b_c[:, at:at + P * (tt + 1)])
                        segs.append((b_qkT[:, 4 * g + h, tt * P:(tt + 1) * P], b_qkT[:, 12 + 4 * g + h, :]))
                        values.append((0, [b_proj[:, 6 + g, kt, h * P:(h + 1) * P] for kt in range(2)]))
                    u = Unit(tt, segs, masks, True, B_DH ** -0.5, values, None, finish)
                    u.head = h
                    units.append(u)
            return units

        def conv_coef(j, m):
            if j < 10:
                return 4 * (j // 2) + m + FFC * (j % 2)
            return 20 + m if m < 2 else FFC + 20 + m - 2

        def ff_place(j, m):
            return (j % 2, m) if j < 10 else (m // 2, m % 2)

        def ff_scalar(act, st):
            def evacuate(j, turn):
                if j % 2 == 0 and j > 0:
                    act.wait_ge(ff_product, j // 2)
                for m in range(4):
                    k, c = ff_place(j, m)
                    n = conv_coef(j, m)
                    last = nc.scalar.activation(
                        ff_u[:, k, c, :], PS[:, 2 * (j % 3) + m // 2, (m % 2) * SEQ:(m % 2 + 1) * SEQ], ACT.Identity,
                        scale=conv_c[:, 2, n:n + 1], bias=conv_c[:, 3, n:n + 1])
                    if m % 2:
                        last.then_inc(conv_first, 1)
                if j % 2 or j == 10:
                    pair, n = j // 2, 4 if j < 10 else 2
                    act.wait_ge(conv_done, 2 * (j + 1))
                    nc.scalar.activation(ff_u[:, 0, 0:n, :], ff_u[:, 0, 0:n, :],
                                         ACT.Gelu_apprx_tanh).then_inc(ff_gelu, 1)
                    act.wait_ge(ff_product, pair + 1)
                    nc.scalar.activation(ffT_h[:, 4 * pair:4 * pair + n, :], ff_a[:, 0:n, :],
                                         ACT.Copy).then_inc(ff_hi, 1)
            return evacuate

        def ff_vector(dve, st, o):
            def evacuate(j, turn):
                for half in range(2):
                    dve.wait_ge(conv_first, 2 * j + half + 1)
                    for tap in (1, 0):
                        for m in (2 * half, 2 * half + 1):
                            k, c = ff_place(j, m)
                            n = conv_coef(j, m)
                            late = 2 - tap
                            src = PS[:, 2 * (j % 3) + half, (m % 2) * SEQ:(m % 2 + 1) * SEQ]
                            dst = ff_u[:, k, c, late:SEQ]
                            last = nc.vector.scalar_tensor_tensor(dst, src[:, 0:SEQ - late], conv_c[:, tap, n:n + 1],
                                                                  dst, ALU.mult, ALU.add)
                            o(last)
                        o.wait()
                    nc.vector.drain().then_inc(conv_done, 1)
                    nc.vector.drain().then_inc(acc_free, 1)
                if j % 2 or j == 10:
                    pair, n = j // 2, 4 if j < 10 else 2
                    dve.wait_ge(ff_gelu, pair + 1)
                    if pair:
                        dve.wait_ge(ff_hi, pair)
                        o.wait()
                    nc.vector.tensor_tensor(ff_a[:, 0:n, :], ff_u[:, 0, 0:n, :], ff_u[:, 1, 0:n, :],
                                            ALU.mult).then_inc(ff_product, 1)
                    dve.wait_ge(ff_hi, pair + 1)
                    o(nc.vector.tensor_tensor(ffT_l[:, 4 * pair:4 * pair + n, :], ff_a[:, 0:n, :],
                                              ffT_h[:, 4 * pair:4 * pair + n, :], ALU.subtract))
            return evacuate

        def params(eng, st, loads):
            for dst, src in loads:
                st.params += 1
                if st.name == "scalar":
                    eng.dma_start(dst, src, allow_slow_non_contiguous=dst.dtype == I32).then_inc(params_in, 16)

        def row(v):
            return v.unsqueeze(0).broadcast_to([P, v.shape[0]])

        def norm_params(g, b=None):
            return [(gb[:, 0, :], row(g))] + ([(gb[:, 1, :], row(b))] if b is not None else [])

        def nsa_params():
            w1 = [a["cmp_k_w1"], a["cmp_v_w1"]]
            w2k = a["cmp_k_w2"].rearrange("(c p) d -> p c d", p=P)
            return [(cmp_w1[k][:, :, :], w1[k].rearrange("(c p) n -> p c n", p=P)) for k in range(2)] + [
                (cmp_w2k[:, :, 0, :], w2k), (cmp_w2k[:, :, 1, :], w2k),
                (cmp_w2v[:, :, :], a["cmp_v_w2"].rearrange("(c p) d -> p c d", p=P))] + [
                (cmp_pe[0:CMP_LEN // 2, k, :], a[n].rearrange("(s b) d -> s (b d)", b=2))
                for k, n in enumerate(("cmp_pe_k", "cmp_pe_v"))]

        def a_params():
            return [(b_c[:, :], a["c_block"]), (pos_i[:, :], a["positions_2"].rearrange("a (t p) -> p (a t)", p=P)),
                    (lam_in[:, :, :].rearrange("p a d -> p (a d)"), row(a["diff_lambda_2"].rearrange("l a d -> (l a d)"))),
                    (head_g[:, :], row(a["diff_head_g_2"][0]))]

        def conv_params():
            return [(conv_in[0:2 * FFC, i, :], a["conv_w_2"][0, i].rearrange("(c p) -> c p", p=P))
                    for i in range(CONV_W)] + [
                (conv_in[0:2 * FFC, CONV_W, :], a["conv_b_2"][0].rearrange("(c p) -> c p", p=P))]

        def moe_layer_tensor(pe, st, layer):
            turn_tensor(pe, st, lambda tt, c: X[:, tt, c * P:(c + 1) * P], DC)
            stage_end(pe, st)
            router_tensor(pe, st)
            stage_end(pe, st)
            stage_end(pe, st)
            sweep_tensor(pe, sweep_first, moe_b0[layer], E * layer, 0)
            stage_end(pe, st)
            crowded = pe.value_load(flag_i[0:1, 0:1], min_val=0, max_val=1)
            with pe.If(crowded > 0):
                sweep_tensor(pe, sweep_second[layer], 0, 0, 1)
            stage_end(pe, st)
            stage_end(pe, st)

        def moe_layer_scalar(act, st, layer):
            params(act, st, norm_params(a["ln_ffn_g"][layer], a["ln_ffn_b"][layer]))
            turn_scalar(act, st, th, DC)
            nc.scalar.activation(xn_h[:, :, :], X[:, :, :], ACT.Copy).then_inc(to_vector, 1)
            stage_end(act, st)
            router_scalar(act, st)
            stage_end(act, st)
            for i in range(4):
                nc.scalar.activation(slot_of[:, 2 * i:2 * i + 2, :].rearrange("p e t -> p (e t)"), PS[:, i, :], ACT.Copy)
            stage_end(act, st)
            sweep_scalar(act, sweep_first, moe_b0[layer], E * layer)
            stage_end(act, st)
            crowded = act.value_load(flag_i[0:1, 0:1], min_val=0, max_val=1)
            with act.If(crowded > 0):
                sweep_scalar(act, sweep_second[layer], 0, 0)
            stage_end(act, st)
            root_scalar(act, st, slice(8, 10))
            stage_end(act, st)

        def moe_layer_vector(dve, st, o, layer):
            params(dve, st, norm_params(a["ln_ffn_g"][layer], a["ln_ffn_b"][layer]))
            turn_vector(dve, st, th, tl, DC)
            inbox(dve, st)
            o(nc.vector.tensor_tensor(xn_l[:, :, :], X[:, :, :], xn_h[:, :, :], ALU.subtract))
            o(nc.vector.memset(zero_r[:, :].bitcast(F32), 0.0))
            stage_end(dve, st)
            router_vector(dve, st, o)
            stage_end(dve, st)
            for i in range(4, 8):
                o(nc.vector.tensor_copy(slot_of[:, 2 * i:2 * i + 2, :].rearrange("p e t -> p (e t)"), PS[:, i, :]))
            stage_end(dve, st)
            sweep_vector(dve, sweep_first, moe_b0[layer], E * layer, 0)
            stage_end(dve, st)
            crowded = dve.value_load(flag_i[0:1, 0:1], min_val=0, max_val=1)
            with dve.If(crowded > 0):
                sweep_vector(dve, sweep_second[layer], 0, 0, 1)
            stage_end(dve, st)
            for tt in range(TT):
                for half in range(2):
                    x = X[:, tt, half * BW:(half + 1) * BW]
                    o(nc.vector.scalar_tensor_tensor(x, x, ALPHA, PS[:, 2 * tt + half, :], ALU.mult, ALU.add))
            layer_norm_vector(dve, st, o)
            stage_end(dve, st)

        def moe_layer_sync(sp, layer):
            sweep_sync(sp, sweep_first, layer, moe_b0[layer])
            sp.wait_ge(flag_ready, layer + 1)
            crowded = sp.value_load(flag_i[0:1, 0:1], min_val=0, max_val=1)
            with sp.If(crowded > 0):
                sp.wait_ge(lo_done, moe_b0[layer] + RAW * E)
                sweep_sync(sp, sweep_second[layer], layer, 0)
                sp.wait_ge(sweep_second[layer].lo_done, RAW * E)

        block = ctx.enter_context(nc.Block())

        def tokens(t):
            return lambda tt, c: t[:, tt, c * P:(c + 1) * P]

        def by_column(t, per=4):
            return lambda tt, c: t[:, c // per, tt, (c % per) * P:(c % per + 1) * P]

        @block.tensor
        def _(pe):
            st = State("tensor", to_tensor)

            def end():
                stage_end(pe, st)

            def turn(source, chunks):
                turn_tensor(pe, st, source, chunks)
                end()

            def product(l, xh, xl, channels=False):
                linear_tensor(pe, l, xh, xl, channels)
                end()

            end()
            turn(tokens(X), DC)
            product(l_ret_in, th, tl)
            end()
            turn(by_column(ret_proj), 16)
            retention_tensor(pe, st)
            end()
            turn(lambda tt, c: ret_o[:, tt, c // 4, (c % 4) * P:(c % 4 + 1) * P], 16)
            product(l_ret_out, ret_oTh, ret_oTl)
            end()
            moe_layer_tensor(pe, st, 0)

            turn(tokens(X), DC)
            product(l_nsa_kv, th, tl)
            product(l_nsa_in, th, tl)
            end()
            end()
            turn(lambda tt, c: n_dup[:, tt, c // 4, c % 4, :] if c < 16 else by_column(n_q)(tt, c - 16), 24)
            compress_tensor(pe, st)
            end()
            attention_tensor(pe, st, nsa_units(), n_att)
            end()
            turn(tokens(n_o), DC)
            product(l_nsa_out, th, tl)
            end()
            moe_layer_tensor(pe, st, 1)

            end()
            turn(tokens(hn), DC)
            product(l_a_in, th, tl)
            end()
            turn(by_column(a_proj), 8)
            attention_tensor(pe, st, a_units(), a_att)
            end()
            end()
            turn(lambda tt, c: a_o[:, tt, c, :], 4)
            product(l_b_in, th, tl)
            end()
            turn(by_column(b_proj), 24)
            attention_tensor(pe, st, b_units(), b_att)
            end()
            turn(lambda tt, c: b_o[:, tt, c, :], 4)
            product(l_gates, th, tl)
            product(l_a_out, oaT_h, oaT_l)
            product(l_b_out, obT_h, obT_l)
            turn(tokens(mix), DC)
            product(l_mix, th, tl)
            end()
            turn(tokens(hn), DC)
            for i in range(4):
                nc.tensor.transpose(PS[:, 0, 2 * FFC * i:2 * FFC * (i + 1)], conv_in[0:2 * FFC, i, :],
                                    cst[0:2 * FFC, C_ID:C_ID + 2 * FFC])
            end()
            end()
            product(l_up, th, tl, channels=True)
            product(l_down, ffT_h, ffT_l)

        @block.scalar
        def _(act):
            st = State("scalar", to_scalar)

            def end():
                stage_end(act, st)

            def turn(hi, chunks):
                turn_scalar(act, st, hi, chunks)
                end()

            def product(l, evacuate=None):
                linear_side(act, l, split_hi, evacuate)
                end()

            act.dma_start(cst[:, :], a["c_keep"]).then_inc(consts_in, 16)
            act.dma_start(rw[:, :, :], a["router_w"].rearrange("(c p) e -> p c e", p=P)).then_inc(consts_in, 16)
            act.dma_start(rb[:, :], row(a["router_b"])).then_inc(consts_in, 16)
            act.dma_start(X[:, :, :], a["x"].rearrange("b (t p) d -> p (b t) d", p=P)).then_inc(consts_in, 16)
            params(act, st, [(ret_c[:, :], a["c_ret"])])
            end()
            turn(th, DC)
            product(l_ret_in, scalar_evacuate(ret_proj))
            nc.scalar.activation(ret_proj[:, 8:12, :, :], ret_proj[:, 8:12, :, :], ACT.Silu)
            end()
            params(act, st, norm_params(a["ln_mix_g"][0], a["ln_mix_b"][0]))
            turn(ret_qkT, 16)
            retention_scalar(act, st)
            end()
            turn(ret_oTh, 16)
            product(l_ret_out)
            root_scalar(act, st, slice(8, 10))
            end()
            moe_layer_scalar(act, st, 0)

            params(act, st, [(n_c[:, :], a["c_nsa"])])
            turn(th, DC)
            product(l_nsa_kv, scalar_evacuate(n_kv))

            def queries_and_gates(j, turn):
                if j < 2:
                    scalar_evacuate(n_q, scale=NSA_DH ** -0.5)(j, turn)
                    return
                for tt in range(TT):
                    nc.scalar.activation(n_g48[:, tt, :], PS[:, 4 + tt, 0:3 * NSA_H],
                                         ACT.Sigmoid).then_inc(acc_free, 1)
            product(l_nsa_in, queries_and_gates)
            end()
            nsa_double_scalar(act)
            end()
            turn(n_T, 24)
            params(act, st, nsa_params())
            compress_scalar(act, st)
            end()
            params(act, st, norm_params(a["ln_mix_g"][1], a["ln_mix_b"][1]))
            attention_scalar(act, st, nsa_units(), n_att)
            end()
            turn(th, DC)
            product(l_nsa_out)
            root_scalar(act, st, slice(8, 10))
            end()
            moe_layer_scalar(act, st, 1)

            params(act, st, norm_params(a["pre_mix_g_2"][0]) + a_params())
            square_scalar(act, st, X, hn)
            inbox(act, st)
            nc.scalar.activation(trig[:, 1].rearrange("p t f -> p (t f)"), ang[:, 0].rearrange("p t f -> p (t f)"),
                                 ACT.Sin)
            nc.scalar.activation(trig[:, 0].rearrange("p t f -> p (t f)"), ang[:, 1].rearrange("p t f -> p (t f)"),
                                 ACT.Sin)
            nc.scalar.activation(small[:, 44:46], small[:, 42:44], ACT.Exp).then_inc(to_vector, 1)
            end()
            turn(th, DC)
            product(l_a_in, scalar_evacuate(a_proj))
            end()
            turn(a_qkT, 8)
            attention_scalar(act, st, a_units(), a_att)
            end()
            root_scalar(act, st, slice(48, 56))
            end()
            turn(oaT_h, 4)
            product(l_b_in, scalar_evacuate(b_proj))
            end()
            params(act, st, norm_params(a["post_mix_g_2"][0]))
            turn(b_qkT, 24)
            attention_scalar(act, st, b_units(), b_att)
            end()
            turn(obT_h, 4)
            product(l_gates, scalar_evacuate(gates, ACT.Sigmoid))
            product(l_a_out)
            product(l_b_out)
            turn(th, DC)

            def mixed(j, turn):
                for tt in range(TT):
                    nc.scalar.activation(mix_t[:, tt, j * BW:(j + 1) * BW], PS[:, 2 * (j % 3) + tt, :],
                                         ACT.Copy).then_inc(acc_free, 1)
            params(act, st, [(gb[:, 1, :], row(a["pre_ffn_g_2"][0]))])
            product(l_mix, mixed)
            square_scalar(act, st, mix_t, mix)
            inbox(act, st)
            square_scalar(act, st, X, mix)
            end()
            params(act, st, conv_params() + norm_params(a["post_ffn_g_2"][0]))
            turn(th, DC)
            end()
            end()
            product(l_up, ff_scalar(act, st))

            def down(j, turn):
                for tt in range(TT):
                    nc.scalar.activation(ff_y[:, tt, j * BW:(j + 1) * BW], PS[:, 2 * (j % 3) + tt, :],
                                         ACT.Copy).then_inc(acc_free, 1)
            product(l_down, down)
            square_scalar(act, st, ff_y, ff_sq)

        @block.vector
        def _(dve):
            st = State("vector", to_vector)
            o = Order(dve, vector_order)

            def end():
                stage_end(dve, st)

            def turn(hi, lo, chunks):
                turn_vector(dve, st, hi, lo, chunks)
                end()

            def product(l, evacuate=None):
                linear_side(dve, l, split_lo, evacuate)
                end()

            dve.wait_ge(consts_in, 4 * 16)
            o(nc.vector.tensor_copy(ident_r[:, :], ident))
            o.then(nc.vector.tensor_copy(rwh[:, :, :], rw[:, :, :]))
            o(nc.vector.tensor_tensor(rwl[:, :, :], rw[:, :, :], rwh[:, :, :], ALU.subtract))
            params(dve, st, [(None, None)])
            dve.wait_ge(params_in, 16 * st.params)
            end()
            turn(th, tl, DC)
            product(l_ret_in)
            for tt in range(TT):
                for j in range(4):
                    rope_vector(dve, o, ret_proj[:, j, tt, :].rearrange("p (h b d) -> p h b d", h=2, b=2),
                                ret_c[:, R_COS + P * tt:R_COS + P * (tt + 1)],
                                ret_c[:, R_SIN + P * tt:R_SIN + P * (tt + 1)], 2, P)
            end()
            params(dve, st, norm_params(a["ln_mix_g"][0], a["ln_mix_b"][0]))
            turn(ret_qkT, None, 16)
            retention_vector(dve, st, o)
            end()
            turn(ret_oTh, ret_oTl, 16)
            product(l_ret_out, residual_evacuate(o, ALPHA))
            layer_norm_vector(dve, st, o)
            end()
            moe_layer_vector(dve, st, o, 0)

            params(dve, st, [(None, None)])
            turn(th, tl, DC)
            product(l_nsa_kv)
            product(l_nsa_in)
            nsa_rope_vector(dve, st, o)
            end()
            end()
            turn(n_T, None, 24)
            params(dve, st, nsa_params())
            compress_vector(dve, st, o)
            end()
            params(dve, st, norm_params(a["ln_mix_g"][1], a["ln_mix_b"][1]))
            attention_vector(dve, st, o, nsa_units(), n_att)
            end()
            turn(th, tl, DC)
            product(l_nsa_out, residual_evacuate(o, ALPHA))
            layer_norm_vector(dve, st, o)
            end()
            moe_layer_vector(dve, st, o, 1)

            params(dve, st, norm_params(a["pre_mix_g_2"][0]) + a_params())
            rms_vector(dve, st, o, D)
            angles_vector(dve, st, o)
            o.then(nc.vector.tensor_tensor(lam_in[:, 0:3:2, :], lam_in[:, 0:3:2, :], lam_in[:, 1:4:2, :], ALU.mult))
            o.then(nc.vector.tensor_reduce(small[:, 42:44], lam_in[:, 0:3:2, :], AX.X, ALU.add))
            hand(dve, to_scalar)
            scaled_rows(dve, o, hn, X, 0)
            inbox(dve, st)
            o.then(nc.vector.tensor_tensor(small[:, 41:42], small[:, 45:46], small[:, 44:45], ALU.subtract))
            o.then(nc.vector.tensor_scalar(small[:, 40:41], small[:, 41:42], -LAM_INIT, None, ALU.add))
            end()
            turn(th, tl, DC)
            product(l_a_in)
            for tt in range(TT):
                for j in range(2):
                    rope_vector(dve, o, a_proj[:, j, tt, :].rearrange("p (h b d) -> p h b d", h=8, b=2),
                                trig[:, 0, tt, 0:32], trig[:, 1, tt, 0:32], 8, 32)
            end()
            turn(a_qkT, None, 8)
            attention_vector(dve, st, o, a_units(), a_att)
            end()
            heads_norm_vector(dve, st, o)
            end()
            turn(oaT_h, oaT_l, 4)
            product(l_b_in)
            for tt in range(TT):
                for j in range(6):
                    rope_vector(dve, o, b_proj[:, j, tt, :].rearrange("p (h b d) -> p h b d", h=4, b=2),
                                trig[:, 0, tt, 32:96], trig[:, 1, tt, 32:96], 4, 64)
            end()
            params(dve, st, norm_params(a["post_mix_g_2"][0]))
            turn(b_qkT, None, 24)
            attention_vector(dve, st, o, b_units(), b_att)
            end()
            turn(obT_h, obT_l, 4)
            product(l_gates)

            def gated_a(j, turn):
                for tt in range(TT):
                    nc.vector.tensor_tensor(mix[:, tt, j * BW:(j + 1) * BW], PS[:, 2 * (j % 3) + tt, :],
                                            gates[:, j, tt, :], ALU.mult).then_inc(acc_free, 1)

            def gated_b(j, turn):
                for tt in range(TT):
                    s = mix_t[:, tt, j * BW:(j + 1) * BW]
                    o.then(nc.vector.tensor_tensor(s, PS[:, 2 * (j % 3) + tt, :], gates[:, 2 + j, tt, :], ALU.mult))
                    m = mix[:, tt, j * BW:(j + 1) * BW]
                    nc.vector.tensor_tensor(m, m, s, ALU.add).then_inc(acc_free, 1)
            product(l_a_out, gated_a)
            product(l_b_out, gated_b)
            turn(th, tl, DC)
            params(dve, st, [(gb[:, 1, :], row(a["pre_ffn_g_2"][0]))])
            product(l_mix)
            dve.wait_ge(params_in, 16 * st.params)
            rms_vector(dve, st, o, D)
            scaled_rows(dve, o, mix_t, mix_t, 0)
            o.then(nc.vector.tensor_tensor(X[:, :, :], X[:, :, :], mix_t[:, :, :], ALU.add))
            hand(dve, to_scalar)
            rms_vector(dve, st, o, D)
            scaled_rows(dve, o, hn, X, 1)
            end()
            params(dve, st, conv_params() + norm_params(a["post_ffn_g_2"][0]))
            turn_vector(dve, st, th, tl, DC)
            dve.wait_ge(params_in, 16 * st.params)
            end()
            end()
            o(nc.vector.tensor_copy(conv_c[:, :, :].rearrange("p i c -> p (i c)"), PS[:, 0, 0:8 * FFC]))
            end()
            product(l_up, ff_vector(dve, st, o))
            product(l_down)
            rms_vector(dve, st, o, D)
            scaled_rows(dve, o, ff_y, ff_y, 0)
            nc.vector.tensor_tensor(X[:, :, :], X[:, :, :], ff_y[:, :, :], ALU.add).then_inc(out_ready, 1)

        @block.sync
        def _(sp):
            linear_sync(sp, l_ret_in)
            linear_sync(sp, l_ret_out)
            moe_layer_sync(sp, 0)
            for l in (l_nsa_kv, l_nsa_in, l_nsa_out):
                linear_sync(sp, l)
            moe_layer_sync(sp, 1)
            for l in (l_a_in, l_b_in, l_gates, l_a_out, l_b_out, l_mix, l_up, l_down):
                linear_sync(sp, l)
            sp.wait_ge(out_ready, 1)
            sp.dma_start(out.rearrange("b (t p) d -> p (b t) d", p=P), X[:, :, :]).then_inc(out_done, 16)
            sp.wait_ge(out_done, 16)


def shape_constants():
    import numpy as np
    f = np.float32
    i = np.arange(P)
    keep = np.zeros((P, C_END), f)
    keep[:, C_ID:C_ID + P] = np.eye(P)
    keep[:, C_ROW:C_ROW + 2 * P] = np.arange(2 * P)
    keep[:, C_BEFORE:C_BEFORE + P] = i[:, None] < i[None, :]
    keep[:, C_ONES:C_ONES + P] = 1.0
    keep[:, C_COL] = i
    keep[:, C_COL + 1] = i + P
    keep[:, C_I16:C_I16 + E] = np.arange(E)
    keep[:, C_I4:C_I4 + E_GROUPS] = np.arange(E_GROUPS)

    def inverse(d):
        return (f(10000.0) ** (-np.arange(0, d, 2, dtype=f) / f(d))).astype(f)

    def trig_of(d):
        ang = np.arange(SEQ, dtype=f)[:, None] * inverse(d)[None]
        return [t.astype(f).reshape(TT, P, -1).transpose(1, 0, 2).reshape(P, -1) for t in (np.cos(ang), np.sin(ang))]

    ret = np.zeros((P, R_END), f)
    log_gamma = np.log1p(-(2.0 ** (-5.0 - np.arange(RET_H)))).astype(f)
    for h in range(RET_H):
        for n, (kt, qt) in enumerate([(0, 0), (0, 1), (1, 1)]):
            diff = (qt * P + i[None, :]) - (kt * P + i[:, None])
            decay = np.where(diff >= 0, np.exp(log_gamma[h] * np.maximum(diff, 0)), 0.0) * RET_DK ** -0.5
            ret[:, R_DECAY + 3 * P * h + P * n:R_DECAY + 3 * P * h + P * (n + 1)] = decay
    ret[:, R_COS:R_COS + 2 * P], ret[:, R_SIN:R_SIN + 2 * P] = trig_of(RET_DK)

    q = np.arange(SEQ)[:, None]
    k = np.arange(SEQ)[None, :]

    def additive(seen):
        m = np.where(seen, 0.0, NEG).astype(f)
        return m[:P, :P], m[P:, :]

    nsa = np.zeros((P, N_END), f)
    m0, m1 = additive(k <= q)
    nsa[:, N_MASK:N_MASK + P] = m0
    nsa[:, N_MASK + SEQ:N_MASK + 2 * SEQ] = m1
    for tt in range(TT):
        ends = np.arange(N_CMP) * CMP_STRIDE + CMP_LEN - 1
        seen = ends[None, :] <= (tt * P + i)[:, None]
        nsa[:, N_CMASK + 15 * tt:N_CMASK + 15 * tt + 15] = np.where(seen, 0.0, NEG)
        nsa[:, N_VALID + tt] = seen.any(1)
    nsa[:, N_COS:N_COS + 64], nsa[:, N_SIN:N_SIN + 64] = trig_of(NSA_DH)

    blk = np.zeros((P, B_END), f)
    for g, (window, dil) in enumerate(B_PAIRS):
        m0, m1 = additive((k <= q) & (q - k <= window) & ((q - k) % dil == 0))
        blk[:, B_MASK + 3 * P * g:B_MASK + 3 * P * g + P] = m0
        blk[:, B_MASK + 3 * P * g + P:B_MASK + 3 * P * (g + 1)] = m1
    blk[:, B_CAUSAL:B_CAUSAL + SEQ] = additive(k <= q)[1]
    blk[:, B_INV:B_INV + 32] = inverse(A_DQK)
    blk[:, B_INV + 32:B_INV + 96] = inverse(B_DH)
    return {"c_keep": keep, "c_ret": ret, "c_nsa": nsa, "c_block": blk}


INPUTS = ["x", "ret_w_in", "ret_w_out", "nsa_w_kv", "cmp_pe_k", "cmp_pe_v", "cmp_k_w1", "cmp_k_w2", "cmp_v_w1",
          "cmp_v_w2", "nsa_w_in", "nsa_w_out", "router_w", "router_b", "moe_w_gate", "moe_w_up", "moe_w_down",
          "ln_mix_g", "ln_mix_b", "ln_ffn_g", "ln_ffn_b", "positions_2", "pre_mix_g_2", "w_in_2", "diff_lambda_2",
          "diff_head_g_2", "w_a_out_2", "w_b_out_2", "w_mix_out_2", "post_mix_g_2", "pre_ffn_g_2", "w_up_2",
          "conv_w_2", "conv_b_2", "w_down_2", "post_ffn_g_2"]


def kernel(**inputs):
    import numpy as np
    from concourse import bacc
    from concourse.bass_utils import run_bass_kernel_spmd

    nc = bacc.Bacc("TRN2", target_bir_lowering=False, num_devices=1)
    arrays, aps = {}, {}
    for name, value in list((n, inputs[n]) for n in INPUTS) + list(shape_constants().items()):
        v = np.ascontiguousarray(value)
        arrays[f"in_{name}"] = v
        aps[name] = nc.dram_tensor(f"in_{name}", v.shape, mybir.dt.from_np(v.dtype), kind="ExternalInput").ap()
    out = nc.dram_tensor("out_x", (1, SEQ, D), F32, kind="ExternalOutput").ap()
    block_program(nc, aps, out)
    r = run_bass_kernel_spmd(nc, [arrays], core_ids=[0])
    return r.results[0]["out_x"]
```

```python
from contextlib import ExitStack

import concourse.bass as bass
from concourse import mybir

F32 = mybir.dt.float32
F32R = mybir.dt.float32r
I32 = mybir.dt.int32
ALU = mybir.AluOpType
ACT = mybir.ActivationFunctionType
AX = mybir.AxisListType

P = 128
D = 1024
SEQ = 256
TT = SEQ // P
DC = D // P
DEPTH = 2
ALPHA = (2.0 * DEPTH) ** 0.25
LN_EPS = 1e-5
RMS_EPS = 1e-6
NEG = -1e30

RET_H, RET_DK, RET_DV = 4, 256, 512
NSA_H, NSA_G, NSA_DH = 16, 4, 64
NSA_REP = NSA_H // NSA_G
CMP_LEN, CMP_STRIDE, CMP_HID = 32, 16, 256
N_CMP = (SEQ - CMP_LEN) // CMP_STRIDE + 1
E, E_GROUPS, D_EXP = 16, 4, 512
E_PER = E // E_GROUPS

A_H, A_DQK, A_DV = 4, 64, 128
B_PAIRS = ((128, 1), (512, 4), (2048, 16))
B_G, B_H, B_DH = 3, 4, 128
D_FF = 2816
FFC = D_FF // P
CONV_W = 3

KC = 4
BW = 512
RING = 6
AHEAD = 2
ROUND = 12582912.0

C_ID, C_ROW, C_BEFORE, C_ONES, C_COL, C_I16, C_I4, C_END = 0, 128, 384, 512, 640, 642, 658, 662
R_DECAY, R_COS, R_SIN, R_END = 0, 1536, 1792, 2048
N_MASK, N_CMASK, N_VALID, N_COS, N_SIN, N_END = 0, 512, 542, 544, 608, 672
B_MASK, B_CAUSAL, B_INV, B_END = 0, 1152, 1408, 1504
LAM_INIT = 0.8 - 0.6


class Order:

    def __init__(self, eng, sem):
        self.eng, self.sem, self.n = eng, sem, 0

    def __call__(self, ins):
        self.n += 1
        ins.then_inc(self.sem, 1)

    def wait(self):
        self.eng.wait_ge(self.sem, self.n)

    def then(self, ins):
        self(ins)
        self.wait()


class Linear:

    def __init__(self, b0, n0, n, groups, sources, peeled):
        self.b0, self.n0, self.n, self.groups, self.sources = b0, n0, n, groups, sources
        self.peeled = peeled
        self.looped = peeled < n // 3


class State:

    def __init__(self, name, inbox):
        self.name, self.inbox = name, inbox
        self.turn = self.stage = self.hand = self.unit = self.params = 0
        self.pt_a = self.pt_v = 0


def block_program(nc, a, out):
    with ExitStack() as ctx:
        def sem(name):
            return ctx.enter_context(nc.semaphore(name))

        cursor = [16512]

        def size_of(shape):
            size = 4
            for s in shape[1:]:
                size *= s
            return (size + 31) // 32 * 32

        def keep(name, shape, dt):
            t = nc.alloc_sbuf_tensor_at(name, shape, dt, offset=cursor[0])
            cursor[0] += size_of(shape)
            return t

        raw_at = cursor[0]
        raw = keep("raw", [P, RING, KC, BW], F32)
        wlo = nc.alloc_sbuf_tensor_at("wlo", [P, RING, KC, BW], F32R, offset=raw_at)
        whi = keep("whi", [P, RING, KC, BW], F32R)
        cst = keep("cst", [P, C_END], F32)
        ident_r = keep("ident_r", [P, P], F32R)
        X = keep("X", [P, TT, D], F32)
        gb_at = cursor[0]
        gb = keep("gb", [P, 2, D], F32)
        th_at = cursor[0]
        th = keep("th", [P, DC, SEQ], F32R)
        tl = keep("tl", [P, DC, SEQ], F32R)
        small = keep("small", [P, 256], F32)
        flag_i = keep("flag_i", [P, 8], I32)
        rw = keep("rw", [P, DC, E], F32)
        rwh = keep("rwh", [P, DC, E], F32R)
        rwl = keep("rwl", [P, DC, E], F32R)
        rb = keep("rb", [P, E], F32)
        arena = cursor[0]

        class Arena:

            def __init__(self, at=arena):
                self.at = at

            def __call__(self, name, shape, dt=F32, at=None):
                if at is None:
                    at = self.at
                    self.at += size_of(shape)
                assert at + size_of(shape) <= nc.sbuf_usable_end, name
                return nc.alloc_sbuf_tensor_at(name, shape, dt, offset=at)

        PS = ctx.enter_context(nc.psum_tensor("PS", [P, 8, 512], F32))
        ident = cst[:, C_ID:C_ID + P]
        before = cst[:, C_BEFORE:C_BEFORE + P]
        ones = cst[:, C_ONES:C_ONES + P]

        A = Arena()
        K16 = 16384
        ret_proj = A("ret_proj", [P, 12, TT, BW])
        ret_qkT = A("ret_qkT", [P, 16, SEQ])
        ret_c = A("ret_c", [P, R_END])
        ret_sd = A("ret_sd", [P, 2, 3, P], at=th_at)
        ret_o = A("ret_o", [P, TT, RET_H, RET_DV], at=arena)
        ret_oTh = A("ret_oTh", [P, 16, SEQ], F32R, at=arena + K16)
        ret_oTl = A("ret_oTl", [P, 16, SEQ], F32R, at=arena + 3 * K16)
        A = Arena()
        xn_h = A("xn_h", [P, TT, D], F32R)
        xn_l = A("xn_l", [P, TT, D], F32R)
        xg_h = A("xg_h", [P, DC, P], F32R)
        xg_l = A("xg_l", [P, DC, P], F32R)
        slot_of = A("slot_of", [P, E, SEQ])
        pick = A("pick", [P, TT, P], F32R)
        pickT = A("pickT", [P, SEQ], F32R)
        silu = A("silu", [P, D_EXP])
        hbuf = A("hbuf", [P, D_EXP])
        hT_h = A("hT_h", [P, 4, P], F32R)
        hT_l = A("hT_l", [P, 4, P], F32R)
        y_h = A("y_h", [P, 2, BW], F32R)
        y_l = A("y_l", [P, 2, BW], F32R)
        route = A("route", [P, 8, TT, E])
        pairs = A("pairs", [P, 8, TT, E_GROUPS])
        tops = A("tops", [P, 4, TT])
        w_split = A("w_split", [P, TT, E, 2], F32R)
        slot_r = A("slot_r", [P, TT, E], F32R)
        zero_r = A("zero_r", [P, P], F32R)
        w_slot = A("w_slot", [P, 1])
        affinity, picked, slot_no, w_tok, score, rt1, rt2, rt3 = (route[:, i] for i in range(8))
        A = Arena()
        n_kv = A("n_kv", [P, 3, TT, BW])
        n_q = A("n_q", [P, 2, TT, BW])
        n_g48 = A("n_g48", [P, TT, 3 * NSA_H])
        n_gate = A("n_gate", [P, TT, 3, NSA_H])
        n_c = A("n_c", [P, N_END])
        nT_at = A.at
        n_T = A("n_T", [P, 24, SEQ])
        dup_at = A.at
        n_dup = A("n_dup", [P, TT, 4, NSA_G, P])
        cmp_pe = A("cmp_pe", [P, 2, P])
        cmp_peT = A("cmp_peT", [P, 2, CMP_LEN // 2])
        cmp_w2k = A("cmp_w2k", [P, 2, 2, NSA_DH])
        cmp_w2v = A("cmp_w2v", [P, 2, NSA_DH])
        cmp_kT = A("cmp_kT", [P, 64])
        cmp_v = A("cmp_v", [P, NSA_G, NSA_DH])
        cmp_h = A("cmp_h", [P, 2, 2, 60])
        cmp_g = A("cmp_g", [P, 2, CMP_HID])
        cmp_w1 = [A("cmp_w1k", [P, 16, CMP_HID], at=th_at), A("cmp_w1v", [P, 16, CMP_HID], at=dup_at)]
        cmp_x = A("cmp_x", [P, 2, 16, 64], at=gb_at)
        n_o = A("n_o", [P, TT, D], at=nT_at)
        def attention_buffers(A, tag, at):
            t = A("scores_" + tag, [P, 2, 3, SEQ], at=at)
            pt = A("probsT_" + tag, [P, 2, 6, P], at=at + 6144)
            return t, pt, A("tops_" + tag, [P, 2, 4], at=at + 12288), A("sums_" + tag, [P, 4, 4], at=at + 12320), \
                A("coef_" + tag, [P, 2, 4], at=at + 12384), A("rec_" + tag, [P, 2, 4], at=at + 12416)
        n_att = attention_buffers(A, "n", dup_at)
        A = Arena()
        oaT_h = A("oaT_h", [P, 4, SEQ], F32R, at=gb_at + 4096)
        oaT_l = A("oaT_l", [P, 4, SEQ], F32R)
        b_c = A("b_c", [P, B_END])
        trig = A("trig", [P, 2, TT, 96])
        part_at = A.at
        a_proj = A("a_proj", [P, 3, TT, BW])
        a_qkT = A("a_qkT", [P, 8, SEQ])
        a_o = A("a_o", [P, TT, 4, P])
        a_sq = A("a_sq", [P, TT, 4, P])
        head_g = A("head_g", [P, P])
        lam_in = A("lam_in", [P, 4, A_DQK])
        ang = A("ang", [P, 4, TT, 96])
        pos_i = A("pos_i", [P, TT], I32)
        pos_f = A("pos_f", [P, TT])
        at_a = A.at
        a_att = attention_buffers(A, "a", at_a)
        A = Arena(part_at)
        b_qkT = A("b_qkT", [P, 24, SEQ])
        bproj_at = A.at
        b_proj = A("b_proj", [P, 9, TT, BW])
        b_att = attention_buffers(A, "b", bproj_at)
        b_o = A("b_o", [P, TT, 4, P], at=bproj_at + 12800)
        gates = A("gates", [P, 4, TT, BW], at=part_at)
        obT_h = A("obT_h", [P, 4, SEQ], F32R, at=part_at + 16384)
        obT_l = A("obT_l", [P, 4, SEQ], F32R, at=part_at + 20480)
        mix = A("mix", [P, TT, D], at=part_at + 38912)
        mix_t = A("mix_t", [P, TT, D], at=part_at + 47104)
        hn = A("hn", [P, TT, D], at=part_at + 53248)
        A = Arena()
        ffT_h = A("ffT_h", [P, FFC, SEQ], F32R)
        ffT_l = A("ffT_l", [P, FFC, SEQ], F32R)
        ff_u = A("ff_u", [P, 2, 4, SEQ])
        ff_a = A("ff_a", [P, 4, SEQ])
        conv_in = A("conv_in", [P, 4, P])
        conv_c = A("conv_c", [P, 4, 2 * FFC])
        ff_y = A("ff_y", [P, TT, D], at=A.at - size_of([P, 4, 2 * FFC]) - 2048 - 4096 - 8192)
        ff_sq = A("ff_sq", [P, TT, D], at=arena)

        rope_t = nc.alloc_sbuf_tensor_at("rope_t", [P, 4, 256], F32, offset=gb_at)

        stage_done = sem("stage_done")
        value_w1_in = sem("value_w1_in")
        ret_gates = sem("ret_gates")
        raw_ready = [sem(f"raw_ready{i}") for i in range(RING)]
        hi_done, lo_done, block_used, acc_free = (sem(n) for n in ("hi_done", "lo_done", "block_used", "acc_free"))
        x_in, consts_in, params_in = sem("x_in"), sem("consts_in"), sem("params_in")
        turned, turned_hi, turned_lo = sem("turned"), sem("turned_hi"), sem("turned_lo")
        vector_order, scalar_order = sem("vector_order"), sem("scalar_order")
        to_scalar, to_vector, to_tensor = sem("to_scalar"), sem("to_vector"), sem("to_tensor")
        flag_ready, out_ready, out_done = sem("flag_ready"), sem("out_ready"), sem("out_done")
        att_scores, att_max, att_probs, att_turned, att_pt_a, att_pt_v, att_pv, att_out = (
            sem("att_" + n) for n in ("scores", "max", "probs", "turned", "pt_a", "pt_v", "pv", "out"))
        ret_scores, ret_decayed, ret_pv, ret_out = (sem("ret_" + n) for n in ("scores", "decayed", "pv", "out"))
        conv_first, ff_product, ff_gelu, ff_hi = (sem(n) for n in ("conv_first", "ff_product", "ff_gelu", "ff_hi"))
        conv_done = sem("conv_done")
        moe_names = ("silu_done", "h_done", "gathered", "xg_hi", "xg_lo", "h_turned", "h_hi", "h_lo", "y_hi", "y_lo",
                     "wg_done", "wg_out", "pick_ready", "pickT_ready", "scattered")

        class Sweep:

            def __init__(self, tag, ring):
                (self.silu_done, self.h_done, self.gathered, self.xg_hi, self.xg_lo, self.h_turned, self.h_hi,
                 self.h_lo, self.y_hi, self.y_lo, self.wg_done, self.wg_out, self.pick_ready, self.pickT_ready,
                 self.scattered) = (sem(f"{n}_{tag}") for n in moe_names)
                self.raw_ready, self.hi_done, self.lo_done, self.block_used = ring

        ring = (raw_ready, hi_done, lo_done, block_used)
        sweep_first = Sweep("first", ring)
        sweep_second = [Sweep(f"second{i}", ([sem(f"raw_ready{k}_second{i}") for k in range(RING)],
                                             sem(f"hi_done_second{i}"), sem(f"lo_done_second{i}"),
                                             sem(f"block_used_second{i}"))) for i in range(DEPTH)]

        blocks, columns = [0], [0]

        def linear(n, groups, sources, peeled=99):
            l = Linear(blocks[0], columns[0], n, groups, sources, peeled)
            blocks[0] += n * len(groups)
            columns[0] += n
            return l

        def plain(W, first=0):
            def sources(j, turn):
                at = first + BW * j + BW * 3 * turn
                wide = min(BW, W.shape[1] - first - BW * j) if isinstance(turn, int) else BW
                return [(W[:, bass.ds(at, wide)], 0, wide)]
            return sources

        def up_sources(j, turn):
            W = a["w_up_2"][0]
            if j < 10:
                at = (j // 2) * BW + D_FF * (j % 2)
                return [(W[:, at:at + BW], 0, BW)]
            return [(W[:, 5 * BW:D_FF], 0, BW // 2), (W[:, D_FF + 5 * BW:2 * D_FF], BW // 2, BW // 2)]

        l_ret_in = linear(12, [4, 4], plain(a["ret_w_in"][0]), peeled=2)
        l_ret_out = linear(2, [4, 4, 4, 4], plain(a["ret_w_out"][0]))
        moe_b0 = [blocks[0]]
        blocks[0] += 6 * E
        l_nsa_kv = linear(3, [4, 4], plain(a["nsa_w_kv"]))
        l_nsa_in = linear(3, [4, 4], plain(a["nsa_w_in"][0]))
        l_nsa_out = linear(2, [4, 4], plain(a["nsa_w_out"][0]))
        moe_b0.append(blocks[0])
        blocks[0] += 6 * E
        l_a_in = linear(3, [4, 4], plain(a["w_in_2"][0]))
        l_b_in = linear(9, [4, 4], plain(a["w_in_2"][0], 3 * BW))
        l_gates = linear(4, [4, 4], plain(a["w_in_2"][0], 12 * BW))
        l_a_out = linear(2, [4], plain(a["w_a_out_2"][0]))
        l_b_out = linear(2, [4], plain(a["w_b_out_2"][0]))
        l_mix = linear(2, [4, 4], plain(a["w_mix_out_2"][0]))
        l_up = linear(11, [4, 4], up_sources)
        l_down = linear(2, [4, 4, 4, 4, 4, 2], plain(a["w_down_2"][0]))
        two_piece = [l_up.b0 + 20, l_up.b0 + 21]

        def stage_end(eng, st, stages=None):
            st.stage += 1
            eng.drain().then_inc(stage_done, 1)
            eng.wait_ge(stage_done, 3 * st.stage)

        def inbox(eng, st):
            st.hand += 1
            eng.wait_ge(st.inbox, st.hand)

        def hand(eng, s):
            eng.drain().then_inc(s, 1)

        def cols_loop(eng, l, body):
            if not l.looped:
                for j in range(l.n):
                    body(j, 0)
                return
            for j in range(3 * l.peeled):
                body(j, 0)
            with eng.Fori(l.peeled, l.n // 3) as turn:
                for j in range(3):
                    body(j, turn)

        def is_first(turn):
            return isinstance(turn, int) and turn == 0

        def ready_value(b, turn):
            extra = sum(1 for t in two_piece if t % RING == b % RING and t <= b)
            return 16 * (b // RING + 1 + extra) + 16 * turn

        def load_block(sp, s, b, turn, pieces):
            slot = b % RING
            if not is_first(turn) or b >= RING:
                sp.wait_ge(s.block_used, b - RING + 1 + RING * turn)
            for src, kc, at, wide in pieces:
                sp.dma_start(raw[:, slot, 0:kc, at:at + wide],
                             src.rearrange("(c p) n -> p c n", p=P)).then_inc(s.raw_ready[slot], 16)

        def split_hi(act, s, b, turn, kc=KC, wide=BW):
            slot = b % RING
            act.wait_ge(s.raw_ready[slot], ready_value(b, turn))
            nc.scalar.activation(whi[:, slot, 0:kc, 0:wide], raw[:, slot, 0:kc, 0:wide], ACT.Copy).then_inc(s.hi_done, 1)

        def split_lo(dve, s, b, turn, kc=KC, wide=BW):
            slot = b % RING
            dve.wait_ge(s.hi_done, b + 1 + RING * turn)
            nc.vector.tensor_tensor(wlo[:, slot, 0:kc, 0:wide], raw[:, slot, 0:kc, 0:wide], whi[:, slot, 0:kc, 0:wide],
                                    ALU.subtract).then_inc(s.lo_done, 1)

        def width_of(l, j, turn):
            return max(at + wide for _, at, wide in l.sources(j, turn))

        def linear_sync(sp, l):
            def body(j, turn):
                for kb, kc in enumerate(l.groups):
                    row = sum(l.groups[:kb]) * P
                    load_block(sp, sweep_first, l.b0 + len(l.groups) * j + kb, turn,
                               [(src[row:row + kc * P, :], kc, at, wide) for src, at, wide in l.sources(j, turn)])
            cols_loop(sp, l, body)

        def linear_tensor(pe, l, xh, xl, channels=False):
            nk = len(l.groups)

            def body(j, turn):
                p = j % 3
                if not is_first(turn) or j >= 3:
                    pe.wait_ge(acc_free, 2 * (l.n0 + j - 2) + 6 * turn)
                wide = width_of(l, j, turn)
                for kb, kc in enumerate(l.groups):
                    b = l.b0 + nk * j + kb
                    pe.wait_ge(lo_done, b + 1 + RING * turn)
                    c0, q = sum(l.groups[:kb]), b % RING
                    if channels:
                        for m in range(4):
                            for c in range(kc):
                                for i, (w, x) in enumerate(((whi, xh), (wlo, xh), (whi, xl))):
                                    last = nc.tensor.matmul(
                                        PS[:, 2 * p + m // 2, (m % 2) * SEQ:(m % 2 + 1) * SEQ],
                                        w[:, q, c, m * P:(m + 1) * P], x[:, c0 + c, :],
                                        start=(kb == 0 and c == 0 and i == 0 and m % 2 == 0),
                                        stop=(kb == nk - 1 and c == kc - 1 and i == 2), skip_group_check=True)
                    else:
                        for tt in range(TT):
                            for c in range(kc):
                                for i, (x, w) in enumerate(((xh, whi), (xh, wlo), (xl, whi))):
                                    last = nc.tensor.matmul(
                                        PS[:, 2 * p + tt, 0:wide], x[:, c0 + c, tt * P:(tt + 1) * P],
                                        w[:, q, c, 0:wide], start=(kb == 0 and c == 0 and i == 0),
                                        stop=(kb == nk - 1 and c == kc - 1 and i == 2))
                    last.then_inc(block_used, 1)
            cols_loop(pe, l, body)

        def linear_side(eng, l, split, evacuate=None, ahead=True):
            nk = len(l.groups)

            def take(j, turn):
                if evacuate is not None:
                    eng.wait_ge(block_used, l.b0 + nk * (j + 1) + RING * turn)
                    evacuate(j, turn)

            def body(j, turn):
                for kb, kc in enumerate(l.groups):
                    if nk * j + kb >= AHEAD or not is_first(turn):
                        split(eng, sweep_first, l.b0 + nk * j + kb, turn, kc, width_of(l, j, turn))
                if j > 0 or not is_first(turn):
                    take(j - 1, turn)
            cols_loop(eng, l, body)
            if ahead:
                for b in range(AHEAD):
                    split(eng, sweep_first, l.b0 + nk * l.n + b, 0)
            take(l.n - 1, 0)

        def scalar_evacuate(dst, func=ACT.Copy, scale=1.0):
            def evacuate(j, turn):
                for tt in range(TT):
                    o = dst[:, j + 3 * turn, tt, :] if is_first(turn) else dst[:, bass.ds(3 * turn + j, 1), tt, :]
                    src = PS[:, 2 * (j % 3) + tt, :]
                    if not is_first(turn):
                        src = src.unsqueeze(1)
                    nc.scalar.activation(o, src, func, scale=scale).then_inc(acc_free, 1)
            return evacuate

        def turn_tensor(pe, st, source, chunks):
            for c in range(0, chunks, 2):
                if c >= 16:
                    pe.wait_ge(turned_lo, st.turn - 7)
                st.turn += 1
                for i in range(2):
                    for tt in range(TT):
                        last = nc.tensor.transpose(
                            PS[:, (c // 2) % 8, i * SEQ + tt * P:i * SEQ + (tt + 1) * P], source(tt, c + i), ident)
                last.then_inc(turned, 1)

        def turn_scalar(act, st, hi, chunks):
            for c in range(0, chunks, 2):
                st.turn += 1
                act.wait_ge(turned, st.turn)
                nc.scalar.activation(hi[:, c:c + 2, :].rearrange("p c t -> p (c t)"), PS[:, (c // 2) % 8, :],
                                     ACT.Copy).then_inc(turned_hi, 1)

        def turn_vector(dve, st, hi, lo, chunks):
            for c in range(0, chunks, 2):
                st.turn += 1
                dve.wait_ge(turned_hi, st.turn)
                if lo is None:
                    nc.vector.drain().then_inc(turned_lo, 1)
                else:
                    nc.vector.tensor_tensor(lo[:, c:c + 2, :].rearrange("p c t -> p (c t)"), PS[:, (c // 2) % 8, :],
                                            hi[:, c:c + 2, :].rearrange("p c t -> p (c t)"),
                                            ALU.subtract).then_inc(turned_lo, 1)

        def root_scalar(act, st, cols):
            inbox(act, st)
            nc.scalar.activation(small[:, cols], small[:, cols], ACT.Sqrt).then_inc(to_vector, 1)

        def root_vector(dve, st, o, cols):
            hand(dve, to_scalar)
            inbox(dve, st)
            o.then(nc.vector.reciprocal(small[:, cols], small[:, cols]))

        def layer_norm_vector(dve, st, o):
            o.wait()
            for tt in range(TT):
                for h in range(2):
                    o(nc.vector.bn_stats(small[:, 16 + 12 * tt + 6 * h:22 + 12 * tt + 6 * h],
                                         X[:, tt, 512 * h:512 * h + 512]))
            o.wait()
            for tt in range(TT):
                o(nc.vector.bn_aggr(small[:, 2 * tt:2 * tt + 2], small[:, 16 + 12 * tt:28 + 12 * tt]))
            o.wait()
            for tt in range(TT):
                o(nc.vector.tensor_scalar(small[:, 8 + tt:9 + tt], small[:, 2 * tt + 1:2 * tt + 2], LN_EPS, None,
                                          ALU.add))
            dve.wait_ge(params_in, 16 * st.params)
            hand(dve, to_scalar)
            for tt in range(TT):
                o(nc.vector.scalar_tensor_tensor(X[:, tt, :], X[:, tt, :], small[:, 2 * tt:2 * tt + 1], gb[:, 0, :],
                                                 ALU.subtract, ALU.mult))
            inbox(dve, st)
            o.then(nc.vector.reciprocal(small[:, 8:8 + TT], small[:, 8:8 + TT]))
            for tt in range(TT):
                o(nc.vector.scalar_tensor_tensor(X[:, tt, :], X[:, tt, :], small[:, 8 + tt:9 + tt], gb[:, 1, :],
                                                 ALU.mult, ALU.add))
            o.wait()

        def rope_vector(dve, o, x, cos, sin, heads, half):
            c = cos.unsqueeze(1).broadcast_to([P, heads, half])
            s = sin.unsqueeze(1).broadcast_to([P, heads, half])
            t = [rope_t[:, i, 0:heads * half].rearrange("p (h d) -> p h d", h=heads) for i in range(4)]
            x1, x2 = x[:, :, 0, :], x[:, :, 1, :]
            o.wait()
            for i, (u, v) in enumerate(((x1, c), (x2, s), (x2, c), (x1, s))):
                o(nc.vector.tensor_tensor(t[i], u, v, ALU.mult))
            o.wait()
            o(nc.vector.tensor_tensor(x1, t[0], t[1], ALU.subtract))
            o(nc.vector.tensor_tensor(x2, t[2], t[3], ALU.add))

        def ret_pairs():
            return [(0, 0), (0, 1), (1, 1)]

        def retention_tensor(pe, st):
            def products(h):
                if h >= 2:
                    pe.wait_ge(ret_decayed, h - 1)
                for i, (kt, qt) in enumerate(ret_pairs()):
                    for c in range(2):
                        last = nc.tensor.matmul(PS[:, h % 2, i * P:(i + 1) * P],
                                                ret_qkT[:, 8 + 2 * h + c, kt * P:(kt + 1) * P],
                                                ret_qkT[:, 2 * h + c, qt * P:(qt + 1) * P],
                                                start=(c == 0), stop=(c == 1))
                last.then_inc(ret_scores, 1)

            products(0)
            for h in range(RET_H):
                if h + 1 < RET_H:
                    products(h + 1)
                pe.wait_ge(ret_decayed, h + 1)
                if h >= 2:
                    pe.wait_ge(ret_out, 2 * (h - 1))
                sd = ret_sd[:, h % 2]
                v = [ret_proj[:, 4 + h, kt, :] for kt in range(2)]
                nc.tensor.matmul(PS[:, 2 + 2 * (h % 2), :], sd[:, 0, :], v[0], start=True, stop=True)
                nc.tensor.matmul(PS[:, 3 + 2 * (h % 2), :], sd[:, 1, :], v[0], start=True, stop=False)
                nc.tensor.matmul(PS[:, 3 + 2 * (h % 2), :], sd[:, 2, :], v[1], start=False,
                                 stop=True).then_inc(ret_pv, 1)

        def retention_scalar(act, st):
            for h in range(RET_H):
                root_scalar(act, st, slice(8, 10))
                if h == 0:
                    nc.scalar.activation(ret_proj[:, 8:12, :, :], ret_proj[:, 8:12, :, :],
                                         ACT.Silu).then_inc(ret_gates, 1)

        def retention_vector(dve, st, o):
            def decay(h):
                dve.wait_ge(ret_scores, h + 1)
                if h >= 2:
                    dve.wait_ge(ret_pv, h - 1)
                nc.vector.tensor_tensor(ret_sd[:, h % 2].rearrange("p a b -> p (a b)"), PS[:, h % 2, 0:3 * P],
                                        ret_c[:, R_DECAY + 3 * P * h:R_DECAY + 3 * P * (h + 1)],
                                        ALU.mult).then_inc(ret_decayed, 1)

            def gated(h):
                dve.wait_ge(ret_gates, 1)
                dve.wait_ge(ret_out, 2 * (h + 1))
                for qt in range(TT):
                    o(nc.vector.tensor_tensor(ret_o[:, qt, h, :], ret_o[:, qt, h, :], ret_proj[:, 8 + h, qt, :],
                                              ALU.mult))

            decay(0)
            for h in range(RET_H):
                if h + 1 < RET_H:
                    decay(h + 1)
                dve.wait_ge(ret_pv, h + 1)
                for qt in range(TT):
                    o(nc.vector.bn_stats(small[:, 16 + 6 * qt:22 + 6 * qt], PS[:, 2 + 2 * (h % 2) + qt, :]))
                o.wait()
                for qt in range(TT):
                    o(nc.vector.bn_aggr(small[:, 2 * qt:2 * qt + 2], small[:, 16 + 6 * qt:22 + 6 * qt]))
                o.wait()
                for qt in range(TT):
                    o(nc.vector.tensor_scalar(small[:, 8 + qt:9 + qt], small[:, 2 * qt + 1:2 * qt + 2], LN_EPS, None,
                                              ALU.add))
                root_vector(dve, st, o, slice(8, 10))
                for qt in range(TT):
                    nc.vector.tensor_scalar(ret_o[:, qt, h, :], PS[:, 2 + 2 * (h % 2) + qt, :],
                                            small[:, 2 * qt:2 * qt + 1], small[:, 8 + qt:9 + qt],
                                            ALU.subtract, ALU.mult).then_inc(ret_out, 1)
                if h >= 1:
                    gated(h - 1)
            gated(RET_H - 1)
            o.wait()

        def residual_evacuate(o, factor):
            def evacuate(j, turn):
                for tt in range(TT):
                    x = X[:, tt, j * BW:(j + 1) * BW]
                    nc.vector.scalar_tensor_tensor(x, x, factor, PS[:, 2 * (j % 3) + tt, :], ALU.mult,
                                                   ALU.add).then_inc(acc_free, 1)
            return evacuate

        def router_tensor_logits(pe, st):
            for c in range(DC):
                for i, (w, x) in enumerate(((rwh, th), (rwl, th), (rwh, tl))):
                    nc.tensor.matmul(PS[0:E, 4, 0:SEQ], w[:, c, :], x[:, c, :],
                                     start=(c == 0 and i == 0), stop=(c == DC - 1 and i == 2))
            hand(pe, to_scalar)
            inbox(pe, st)
            for tt in range(TT):
                nc.tensor.transpose(PS[:, 0, tt * E:(tt + 1) * E], slot_of[0:E, 0, tt * P:(tt + 1) * P],
                                    cst[0:E, C_ID:C_ID + E])
            hand(pe, to_scalar)

        def router_tensor(pe, st):
            router_tensor_logits(pe, st)
            inbox(pe, st)
            nc.tensor.matmul(PS[:, 1, 0:E], before, picked[:, 0, :], start=True, stop=True)
            nc.tensor.matmul(PS[:, 1, E:2 * E], ones, picked[:, 0, :], start=True, stop=False)
            nc.tensor.matmul(PS[:, 1, E:2 * E], before, picked[:, 1, :], start=False, stop=True)
            nc.tensor.matmul(PS[:, 2, 0:E], ones, picked[:, 0, :], start=True, stop=False)
            nc.tensor.matmul(PS[:, 2, 0:E], ones, picked[:, 1, :], start=False, stop=True)
            hand(pe, to_vector)
            inbox(pe, st)
            for e in range(E):
                for tt in range(TT):
                    at = (e % 2) * SEQ + tt * P
                    nc.tensor.matmul(PS[:, e // 2, at:at + P], slot_r[:, tt, e:e + 1].broadcast_to([P, P]),
                                     ident_r[:, :], start=True, stop=True)

        def router_scalar(act, st):
            inbox(act, st)
            nc.scalar.activation(slot_of[0:E, 0, :], PS[0:E, 4, 0:SEQ], ACT.Sigmoid).then_inc(to_tensor, 1)
            inbox(act, st)
            nc.scalar.activation(affinity.rearrange("p t e -> p (t e)"), PS[:, 0, 0:TT * E],
                                 ACT.Copy).then_inc(to_vector, 1)

        def router_vector(dve, st, o):
            def wide(v, *shape):
                for _ in range(len(shape) - len(v.shape)):
                    v = v.unsqueeze(len(v.shape))
                return v.broadcast_to(list(shape))

            inbox(dve, st)
            o.then(nc.vector.tensor_tensor(score, affinity, rb[:, :].unsqueeze(1).broadcast_to([P, TT, E]), ALU.add))
            s4 = score.rearrange("p t (g e) -> p t g e", e=E_PER)
            pr = [pairs[:, i] for i in range(8)]
            o(nc.vector.tensor_tensor(pr[0], s4[:, :, :, 0], s4[:, :, :, 1], ALU.max))
            o(nc.vector.tensor_tensor(pr[1], s4[:, :, :, 0], s4[:, :, :, 1], ALU.min))
            o(nc.vector.tensor_tensor(pr[2], s4[:, :, :, 2], s4[:, :, :, 3], ALU.max))
            o(nc.vector.tensor_tensor(pr[3], s4[:, :, :, 2], s4[:, :, :, 3], ALU.min))
            o.wait()
            o(nc.vector.tensor_tensor(pr[4], pr[0], pr[2], ALU.max))
            o(nc.vector.tensor_tensor(pr[5], pr[0], pr[2], ALU.min))
            o(nc.vector.tensor_tensor(pr[6], pr[1], pr[3], ALU.max))
            o.wait()
            o.then(nc.vector.tensor_tensor(pr[7], pr[5], pr[6], ALU.max))
            o.then(nc.vector.tensor_tensor(pr[0], pr[4], pr[7], ALU.add))
            top = [tops[:, i] for i in range(4)]
            i4 = cst[:, C_I4:C_I4 + 4].unsqueeze(1).broadcast_to([P, TT, E_GROUPS])
            i16 = cst[:, C_I16:C_I16 + E].unsqueeze(1).broadcast_to([P, TT, E])
            o.then(nc.vector.tensor_reduce(top[0], pr[0], AX.X, ALU.max))
            o.then(nc.vector.tensor_tensor(pr[1], pr[0], wide(top[0], P, TT, E_GROUPS), ALU.is_ge))
            o.then(nc.vector.tensor_scalar(pr[2], pr[1], -99.0, 99.0, ALU.mult, ALU.add))
            o.then(nc.vector.tensor_tensor(pr[3], pr[2], i4, ALU.add))
            o.then(nc.vector.tensor_reduce(top[1], pr[3], AX.X, ALU.min))
            o.then(nc.vector.tensor_tensor(pr[4], i4, wide(top[1], P, TT, E_GROUPS), ALU.is_equal))
            o.then(nc.vector.tensor_scalar(pr[5], pr[4], -NEG, NEG, ALU.mult, ALU.add))
            m4 = rt1.rearrange("p t (g e) -> p t g e", e=E_PER)
            for tt in range(TT):
                o(nc.vector.tensor_tensor(m4[:, tt], s4[:, tt], wide(pr[4][:, tt], P, E_GROUPS, E_PER), ALU.mult))
            o.wait()
            for tt in range(TT):
                o(nc.vector.tensor_tensor(m4[:, tt], m4[:, tt], wide(pr[5][:, tt], P, E_GROUPS, E_PER), ALU.add))
            o.wait()
            for k in range(2):
                o.then(nc.vector.tensor_reduce(top[0], rt1, AX.X, ALU.max))
                o.then(nc.vector.tensor_tensor(rt2, rt1, wide(top[0], P, TT, E), ALU.is_ge))
                o.then(nc.vector.tensor_scalar(rt3, rt2, -99.0, 99.0, ALU.mult, ALU.add))
                o.then(nc.vector.tensor_tensor(rt2, rt3, i16, ALU.add))
                o.then(nc.vector.tensor_reduce(top[1], rt2, AX.X, ALU.min))
                if k == 0:
                    o.then(nc.vector.tensor_tensor(picked, i16, wide(top[1], P, TT, E), ALU.is_equal))
                    o.then(nc.vector.scalar_tensor_tensor(rt1, picked, 3.0 * NEG, rt1, ALU.mult, ALU.add))
                else:
                    o.then(nc.vector.tensor_tensor(rt3, i16, wide(top[1], P, TT, E), ALU.is_equal))
                    o.then(nc.vector.tensor_tensor(picked, picked, rt3, ALU.add))
            hand(dve, to_tensor)
            o.then(nc.vector.tensor_tensor(w_tok, affinity, picked, ALU.mult))
            o.then(nc.vector.tensor_reduce(top[2], w_tok, AX.X, ALU.add))
            o.then(nc.vector.reciprocal(top[3], top[2]))
            o.then(nc.vector.tensor_tensor(w_tok, w_tok, wide(top[3], P, TT, E), ALU.mult))
            o.then(nc.vector.tensor_copy(w_split[:, :, :, 0], w_tok))
            o(nc.vector.tensor_tensor(w_split[:, :, :, 1], w_tok, w_split[:, :, :, 0], ALU.subtract))
            inbox(dve, st)
            o.then(nc.vector.scalar_tensor_tensor(rt2.rearrange("p t e -> p (t e)"), PS[:, 1, 0:TT * E], 1.0,
                                                  picked.rearrange("p t e -> p (t e)"), ALU.add, ALU.mult))
            o.then(nc.vector.tensor_scalar(slot_no, rt2, -1.0, None, ALU.add))
            o.then(nc.vector.tensor_copy(slot_r[:, :, :], slot_no))
            o.then(nc.vector.tensor_reduce(top[0][:, 0:1], PS[:, 2, 0:E], AX.X, ALU.max))
            hand(dve, to_tensor)
            o.then(nc.vector.tensor_scalar(top[1][:, 0:1], top[0][:, 0:1], float(P) + 0.5, None, ALU.is_gt))
            o.then(nc.vector.tensor_copy(flag_i[:, 0:1], top[1][:, 0:1]))
            hand(dve, flag_ready)

        def expert_blocks(layer, e):
            gate, up, down = (a[n][layer] for n in ("moe_w_gate", "moe_w_up", "moe_w_down"))

            def of(W):
                return W[e] if isinstance(e, int) else W[bass.ds(e, 1)].rearrange("a k n -> (a k) n")
            g, u, d = of(gate), of(up), of(down)
            half = KC * P
            return [g[0:half], g[half:], u[0:half], u[half:], d[:, BW:], d[:, 0:BW]]

        def experts_loop(eng, body):
            body(0, True, False)
            with eng.Fori(1, E - 1) as e:
                body(e, False, False)
            body(E - 1, False, True)

        def sweep_sync(sp, s, layer, b0):
            def body(e, first, last):
                for i, src in enumerate(expert_blocks(layer, e)):
                    if isinstance(e, int):
                        load_block(sp, s, b0 + RING * e + i, 0, [(src, KC, 0, BW)])
                    else:
                        load_block(sp, s, b0 + i, e, [(src, KC, 0, BW)])
            experts_loop(sp, body)

        def at_block(b0, i, e):
            return (b0 + i + RING * e, 0) if isinstance(e, int) else (b0 + i, e)

        def sweep_tensor(pe, s, b0, v0, second):
            def gather(v, half):
                for c in range(4 * half, 4 * half + 4):
                    for i, (x, tt) in enumerate(((xn_h, 0), (xn_l, 0), (xn_h, 1), (xn_l, 1))):
                        last = nc.tensor.matmul(PS[:, 6 + half, (c % 4) * P:(c % 4 + 1) * P],
                                                x[:, tt, c * P:(c + 1) * P], pick[:, tt, :],
                                                start=(i == 0), stop=(i == 3))
                last.then_inc(s.gathered, 1)

            def product(bank, b, turn, x0, xh, xl, start, stop):
                pe.wait_ge(s.lo_done, b + 1 + RING * turn)
                q = b % RING
                for c in range(KC):
                    for i, (x, w) in enumerate(((xh, whi), (xh, wlo), (xl, whi))):
                        last = nc.tensor.matmul(PS[:, bank, :], x[:, x0 + c, :], w[:, q, c, :],
                                                start=(start and c == 0 and i == 0),
                                                stop=(stop and c == KC - 1 and i == 2))
                last.then_inc(s.block_used, 1)

            def scatter(v):
                pe.wait_ge(s.pickT_ready, v)
                pe.wait_ge(s.y_lo, 2 * v)
                for tt in range(TT):
                    for half in range(2):
                        for y in (y_h, y_l):
                            last = nc.tensor.matmul(PS[:, 2 * tt + half, :], pickT[:, tt * P:(tt + 1) * P],
                                                    y[:, half, :], start=False, stop=False, skip_group_check=True)
                last.then_inc(s.scattered, 1)

            def body(e, first, last_one):
                v = v0 + e
                blk = [at_block(b0, i, e) for i in range(6)]
                pe.wait_ge(s.xg_lo, 2 * v + 2)
                if not first:
                    pe.wait_ge(s.y_lo, 2 * v - 1)
                product(4, *blk[0], 0, xg_h, xg_l, True, False)
                product(4, *blk[1], 4, xg_h, xg_l, False, True)
                if not first:
                    pe.wait_ge(s.y_lo, 2 * v)
                for tt in range(TT):
                    w = w_split[:, tt, e, :] if isinstance(e, int) else \
                        w_split[:, tt, bass.ds(e, 1), :].rearrange("p a b -> p (a b)")
                    m = nc.tensor.matmul(PS[:, 6, 0:2], pick[:, tt, :], w, start=(tt == 0), stop=(tt == 1))
                m.then_inc(s.wg_done, 1)
                product(5, *blk[2], 0, xg_h, xg_l, True, False)
                product(5, *blk[3], 4, xg_h, xg_l, False, True)
                pe.wait_ge(s.wg_out, v + 1)
                if not last_one:
                    pe.wait_ge(s.pick_ready, v + 2)
                    gather(v + 1, 0)
                    gather(v + 1, 1)
                pe.wait_ge(s.h_done, v + 1)
                for f in range(4):
                    m = nc.tensor.transpose(PS[:, 4, f * P:(f + 1) * P], hbuf[:, f * P:(f + 1) * P], ident)
                m.then_inc(s.h_turned, 1)
                if not first:
                    scatter(v)
                pe.wait_ge(s.h_lo, v + 1)
                product(4, *blk[4], 0, hT_h, hT_l, True, True)
                product(5, *blk[5], 0, hT_h, hT_l, True, True)

            if not second:
                for bank in range(4):
                    nc.tensor.matmul(PS[:, bank, :], zero_r[:, :], xn_h[:, 0, 0:512], start=True, stop=False,
                                     skip_group_check=True)
            pe.wait_ge(s.pick_ready, v0 + 1)
            gather(v0, 0)
            gather(v0, 1)
            experts_loop(pe, body)
            scatter(v0 + E)

        def sweep_scalar(act, s, b0, v0, second):
            def xg(n, half):
                act.wait_ge(s.gathered, n)
                nc.scalar.activation(xg_h[:, 4 * half:4 * half + 4, :].rearrange("p c j -> p (c j)"),
                                     PS[:, 6 + half, :], ACT.Copy).then_inc(s.xg_hi, 1)

            def y(v, half, b, turn):
                act.wait_ge(s.block_used, b + 1 + RING * turn)
                nc.scalar.activation(y_h[:, half, :], PS[:, 5 - half, :], ACT.Identity,
                                     scale=w_slot[:, 0:1]).then_inc(s.y_hi, 1)

            def body(e, first, last_one):
                v = v0 + e
                blk = [at_block(b0, i, e) for i in range(10)]
                split_hi(act, s, *blk[4])
                act.wait_ge(s.block_used, blk[1][0] + 1 + RING * blk[1][1])
                if not first:
                    act.wait_ge(s.h_done, v)
                nc.scalar.activation(silu[:, :], PS[:, 4, :], ACT.Silu).then_inc(s.silu_done, 1)
                split_hi(act, s, *blk[5])
                if not last_one:
                    split_hi(act, s, *blk[6])
                    xg(2 * v + 3, 0)
                    xg(2 * v + 4, 1)
                act.wait_ge(s.h_turned, v + 1)
                nc.scalar.activation(hT_h[:, :, :].rearrange("p f j -> p (f j)"), PS[:, 4, :],
                                     ACT.Copy).then_inc(s.h_hi, 1)
                if not last_one:
                    split_hi(act, s, *blk[7])
                act.wait_ge(s.wg_out, v + 1)
                if not first:
                    act.wait_ge(s.scattered, v)
                y(v, 1, *blk[4])
                if not last_one:
                    split_hi(act, s, *blk[8])
                y(v, 0, *blk[5])
                if not last_one:
                    split_hi(act, s, *blk[9])

            for i in range(0 if second else AHEAD, 4):
                split_hi(act, s, b0 + i, 0)
            xg(2 * v0 + 1, 0)
            xg(2 * v0 + 2, 1)
            experts_loop(act, body)

        def sweep_vector(dve, s, b0, v0, second):
            slots = cst[:, C_ROW + P * second:C_ROW + P * second + P]

            def xg(n, half):
                dve.wait_ge(s.xg_hi, n)
                nc.vector.tensor_tensor(xg_l[:, 4 * half:4 * half + 4, :].rearrange("p c j -> p (c j)"),
                                        PS[:, 6 + half, :],
                                        xg_h[:, 4 * half:4 * half + 4, :].rearrange("p c j -> p (c j)"),
                                        ALU.subtract).then_inc(s.xg_lo, 1)

            def y(n, half):
                dve.wait_ge(s.y_hi, n)
                nc.vector.scalar_tensor_tensor(y_l[:, half, :], PS[:, 5 - half, :], w_slot[:, 0:1], y_h[:, half, :],
                                               ALU.mult, ALU.subtract).then_inc(s.y_lo, 1)

            def selection(e):
                for tt in range(TT):
                    mine = slot_no[:, tt, e:e + 1] if isinstance(e, int) else slot_no[:, tt, bass.ds(e, 1)]
                    last = nc.vector.tensor_scalar(pick[:, tt, :], slots, mine, None, ALU.is_equal)
                last.then_inc(s.pick_ready, 1)

            def body(e, first, last_one):
                v = v0 + e
                blk = [at_block(b0, i, e) for i in range(10)]
                split_lo(dve, s, *blk[4])
                dve.wait_ge(s.wg_done, v + 1)
                nc.vector.tensor_reduce(w_slot[:, 0:1], PS[:, 6, 0:2], AX.X, ALU.add).then_inc(s.wg_out, 1)
                if not last_one:
                    selection(e + 1)
                split_lo(dve, s, *blk[5])
                if not last_one:
                    split_lo(dve, s, *blk[6])
                dve.wait_ge(s.silu_done, v + 1)
                dve.wait_ge(s.block_used, blk[3][0] + 1 + RING * blk[3][1])
                nc.vector.tensor_tensor(hbuf[:, :], silu[:, :], PS[:, 5, :], ALU.mult).then_inc(s.h_done, 1)
                if not last_one:
                    xg(2 * v + 3, 0)
                    xg(2 * v + 4, 1)
                dve.wait_ge(s.h_hi, v + 1)
                nc.vector.tensor_tensor(hT_l[:, :, :].rearrange("p f j -> p (f j)"), PS[:, 4, :],
                                        hT_h[:, :, :].rearrange("p f j -> p (f j)"), ALU.subtract).then_inc(s.h_lo, 1)
                if not last_one:
                    split_lo(dve, s, *blk[7])
                if not first:
                    dve.wait_ge(s.scattered, v)
                rows = slot_of[:, e, :] if isinstance(e, int) else \
                    slot_of[:, bass.ds(e, 1), :].rearrange("p a b -> p (a b)")
                nc.vector.tensor_scalar(pickT[:, :], rows, cst[:, C_COL + second:C_COL + second + 1], None,
                                        ALU.is_equal).then_inc(s.pickT_ready, 1)
                y(2 * v + 1, 1)
                if not last_one:
                    split_lo(dve, s, *blk[8])
                y(2 * v + 2, 0)
                if not last_one:
                    split_lo(dve, s, *blk[9])

            selection(0)
            for i in range(0 if second else AHEAD, 4):
                split_lo(dve, s, b0 + i, 0)
            xg(2 * v0 + 1, 0)
            xg(2 * v0 + 2, 1)
            experts_loop(dve, body)

        class Unit:

            def __init__(self, tt, segs, masks, joint, scale, values, extra=None, finish=None):
                self.tt, self.segs, self.masks, self.joint, self.scale = tt, segs, masks, joint, scale
                self.values, self.extra, self.finish = values, extra, finish
                self.w = P * (tt + 1)
                self.blocks = len(segs) * (tt + 1)
                self.apart = len({q.start_partition() if callable(q.start_partition) else q.start_partition
                                  for q, _ in segs}) > 1

            def scores_at(self, i, k):
                bank, at = (k, 0) if self.apart else (k // 2, (k % 2) * SEQ)
                return PS[:, 2 * (i % 2) + bank, at:at + self.w]

        def attention_tensor(pe, st, units, buf):
            t, pt = buf[0], buf[1]
            u0 = st.unit

            def scores(i):
                u, n = units[i], u0 + i
                if i >= 2:
                    pe.wait_ge(att_max, n - 1)
                for k, (q, key) in enumerate(u.segs):
                    last = nc.tensor.matmul(u.scores_at(i, k), q, key[:, 0:u.w], start=True, stop=True)
                if u.extra:
                    q, key, _, _ = u.extra
                    last = nc.tensor.matmul(PS[:, 2 * (i % 2) + 1, 0:N_CMP], q, key, start=True, stop=True)
                last.then_inc(att_scores, 1)

            def turn_probs(i):
                u = units[i]
                pe.wait_ge(att_probs, u0 + i + 1)
                if i >= 1:
                    pe.wait_ge(att_pt_a, st.pt_a)
                    pe.wait_ge(att_pt_v, st.pt_v)
                for b in range(u.blocks):
                    k, kt = b // (u.tt + 1), b % (u.tt + 1)
                    last = nc.tensor.transpose(PS[:, 4 + b // 4, (b % 4) * P:(b % 4 + 1) * P],
                                               t[:, i % 2, k, kt * P:(kt + 1) * P], ident)
                if u.extra:
                    last = nc.tensor.transpose(PS[0:N_CMP, 5, 0:P], t[:, i % 2, 2, 0:N_CMP], ident)
                last.then_inc(att_turned, 1)
                st.pt_a += 1
                st.pt_v += 1 if (u.blocks > 4 or u.extra) else 0

            def over_values(i):
                u = units[i]
                if i >= 2:
                    pe.wait_ge(att_out, u0 + i - 1)
                o_bank, p = PS[:, 6 + i % 2, :], pt[:, i % 2]
                for k, (at, vals) in enumerate(u.values):
                    for kt in range(u.tt + 1):
                        b = k * (u.tt + 1) + kt
                        width = vals[kt].shape[-1]
                        first = kt == 0 and (k == 0 or not u.joint)
                        final = kt == u.tt and (k == len(u.values) - 1 or not u.joint)
                        last = nc.tensor.matmul(o_bank[:, at:at + width], p[:, b, :], vals[kt], start=first,
                                                stop=final)
                if u.extra:
                    _, _, at, v = u.extra
                    last = nc.tensor.matmul(o_bank[:, at:at + NSA_DH], p[0:N_CMP, 5, :], v, start=True, stop=True)
                last.then_inc(att_pv, 1)

            scores(0)
            scores(1)
            for i in range(len(units)):
                turn_probs(i)
                if i + 2 < len(units):
                    scores(i + 2)
                if i >= 1:
                    over_values(i - 1)
            pe.wait_ge(att_pt_a, st.pt_a)
            pe.wait_ge(att_pt_v, st.pt_v)
            over_values(len(units) - 1)
            st.unit += len(units)

        def attention_scalar(act, st, units, buf):
            t, pt, top, sums = buf[0:4]
            u0 = st.unit

            def probs(i):
                u = units[i]
                act.wait_ge(att_max, u0 + i + 1)
                if i >= 4:
                    act.wait_ge(att_out, u0 + i - 3)
                s, m, n = t[:, i % 2], top[:, i % 2], sums[:, i % 4]
                if u.joint:
                    x = s[:, 0:len(u.segs), 0:u.w]
                    last = nc.scalar.activation(x, x, ACT.Exp, bias=m[:, 0:1], accum_out=n[:, 0:1])
                else:
                    for k in range(len(u.segs)):
                        x = s[:, k, 0:u.w]
                        last = nc.scalar.activation(x, x, ACT.Exp, bias=m[:, k:k + 1], accum_out=n[:, k:k + 1])
                if u.extra:
                    x = s[:, 2, 0:N_CMP]
                    last = nc.scalar.activation(x, x, ACT.Exp, bias=m[:, 2:3], accum_out=n[:, 2:3])
                last.then_inc(att_probs, 1)

            probs(0)
            for i, u in enumerate(units):
                if i + 1 < len(units):
                    probs(i + 1)
                act.wait_ge(att_turned, u0 + i + 1)
                if i >= 2:
                    act.wait_ge(att_pv, u0 + i - 1)
                w = min(u.blocks, 4)
                nc.scalar.activation(pt[:, i % 2, 0:w, :].rearrange("p b q -> p (b q)"), PS[:, 4, 0:w * P],
                                     ACT.Copy).then_inc(att_pt_a, 1)
            st.unit += len(units)

        def attention_vector(dve, st, o, units, buf):
            t, pt, top, sums, coef, rec = buf
            u0 = st.unit

            def masked(i):
                u = units[i]
                dve.wait_ge(att_scores, u0 + i + 1)
                if i >= 2:
                    dve.wait_ge(att_turned, u0 + i - 1)
                s, m = t[:, i % 2], top[:, i % 2]
                if u.joint:
                    for k in range(len(u.segs)):
                        o(nc.vector.scalar_tensor_tensor(s[:, k, 0:u.w], u.scores_at(i, k), u.scale, u.masks[k],
                                                         ALU.mult, ALU.add))
                else:
                    both = PS[:, 2 * (i % 2):2 * (i % 2) + 2, 0:u.w] if u.apart else \
                        PS[:, 2 * (i % 2), :].rearrange("p (k n) -> p k n", k=2)[:, :, 0:u.w]
                    o(nc.vector.scalar_tensor_tensor(s[:, 0:2, 0:u.w], both, u.scale,
                                                     u.masks[0].unsqueeze(1).broadcast_to([P, 2, u.w]),
                                                     ALU.mult, ALU.add))
                if u.extra:
                    o(nc.vector.tensor_tensor(s[:, 2, 0:N_CMP], PS[:, 2 * (i % 2) + 1, 0:N_CMP],
                                              n_c[:, N_CMASK + 15 * u.tt:N_CMASK + 15 * u.tt + 15], ALU.add))
                o.wait()
                n = len(u.segs)
                if u.extra:
                    o(nc.vector.tensor_reduce(m[:, 2:3], s[:, 2, 0:N_CMP], AX.X, ALU.max, negate=True))
                if u.joint:
                    last = nc.vector.tensor_reduce(m[:, 0:1], s[:, 0:n, 0:u.w], AX.XY, ALU.max, negate=True)
                else:
                    last = nc.vector.tensor_reduce(m[:, 0:n], s[:, 0:n, 0:u.w], AX.X, ALU.max, negate=True)
                last.then_inc(att_max, 1)

            def finish(i):
                dve.wait_ge(att_pv, u0 + i + 1)
                u = units[i]
                u.finish(o, u, PS[:, 6 + i % 2, :], sums[:, i % 4], rec[:, i % 2], coef[:, i % 2]).then_inc(att_out, 1)

            masked(0)
            for i, u in enumerate(units):
                if i + 1 < len(units):
                    masked(i + 1)
                if u.blocks > 4 or u.extra:
                    dve.wait_ge(att_turned, u0 + i + 1)
                    if i >= 2:
                        dve.wait_ge(att_pv, u0 + i - 1)
                    if u.extra:
                        nc.vector.tensor_copy(pt[0:N_CMP, i % 2, 5, :], PS[0:N_CMP, 5, 0:P]).then_inc(att_pt_v, 1)
                    else:
                        w = u.blocks - 4
                        nc.vector.tensor_copy(pt[:, i % 2, 4:4 + w, :].rearrange("p b q -> p (b q)"),
                                              PS[:, 5, 0:w * P]).then_inc(att_pt_v, 1)
                if i >= 1:
                    finish(i - 1)
            finish(len(units) - 1)
            dve.wait_ge(att_out, u0 + len(units))
            st.unit += len(units)

        def nsa_rotate(dve, o, x, heads):
            for tt in range(TT):
                cos, sin = (n_c[:, at + 32 * tt:at + 32 * tt + 32] for at in (N_COS, N_SIN))
                rope_vector(dve, o, x[:, tt, 0:heads * NSA_DH].rearrange("p (h b d) -> p h b d", h=heads, b=2),
                            cos, sin, heads, 32)

        def nsa_gates_vector(dve, o):
            for tt in range(TT):
                g = n_g48[:, tt, :].rearrange("p (h k) -> p k h", k=3)
                o(nc.vector.tensor_copy(n_gate[:, tt, 0, :], g[:, 1, :]))
                o(nc.vector.tensor_copy(n_gate[:, tt, 1, :], g[:, 2, :]))
                o(nc.vector.tensor_scalar(n_gate[:, tt, 2, :], g[:, 0, :], n_c[:, N_VALID + tt:N_VALID + tt + 1], None,
                                          ALU.mult))

        def nsa_double(i, copy):
            k, at = ((0, 0), (0, 256), (1, 0), (2, 0))[i]
            for tt in range(TT):
                src = n_kv[:, k, tt, at:at + 256].rearrange("p (g d) -> p g d", g=NSA_G)
                for b in range(2):
                    copy(n_dup[:, tt, i, :, b * NSA_DH:(b + 1) * NSA_DH], src)

        def compress_tensor(pe, st):
            inbox(pe, st)
            half = CMP_LEN // 2
            for k in range(2):
                nc.tensor.transpose(PS[:, 0, k * half:(k + 1) * half], cmp_pe[0:half, k, :], cst[0:half, C_ID:C_ID + half])
            hand(pe, to_vector)
            inbox(pe, st)
            for k in range(2):
                if k == 1:
                    pe.wait_ge(value_w1_in, 16)
                for i in range(half):
                    nc.tensor.matmul(PS[0:60, 1 + 3 * k, 0:CMP_HID], cmp_x[:, k, i, 0:60], cmp_w1[k][:, i, :],
                                     start=(i == 0), stop=(i == half - 1))
                hand(pe, to_scalar)
            for k in range(2):
                inbox(pe, st)
                for c in range(2):
                    nc.tensor.transpose(PS[:, 5 + k, c * 64:c * 64 + 60], cmp_g[0:60, k, c * P:(c + 1) * P],
                                        cst[0:60, C_ID:C_ID + 60])
                hand(pe, to_vector)
            inbox(pe, st)
            for c in range(2):
                nc.tensor.matmul(PS[:, 2, 0:60], cmp_w2k[:, c, :, :].rearrange("p b d -> p (b d)"), cmp_h[:, 0, c, :],
                                 start=(c == 0), stop=(c == 1))
            for g in range(NSA_G):
                for c in range(2):
                    nc.tensor.matmul(PS[0:N_CMP, 3, g * NSA_DH:(g + 1) * NSA_DH], cmp_h[:, 1, c, 15 * g:15 * g + 15],
                                     cmp_w2v[:, c, :], start=(c == 0), stop=(c == 1))
            hand(pe, to_vector)

        def compress_scalar(act, st):
            for k in range(2):
                inbox(act, st)
                nc.scalar.activation(cmp_g[0:60, k, :], PS[0:60, 1 + 3 * k, 0:CMP_HID],
                                     ACT.Gelu_apprx_tanh).then_inc(to_tensor, 1)

        def compress_vector(dve, st, o):
            dve.wait_ge(params_in, 16 * st.params)
            hand(dve, to_tensor)
            inbox(dve, st)
            o.then(nc.vector.tensor_copy(cmp_peT[:, :, :].rearrange("p a b -> p (a b)"), PS[:, 0, 0:CMP_LEN]))
            for k in range(2):
                for g in range(NSA_G):
                    for b in range(2):
                        rows = slice(64 * b, 64 * b + 64)
                        tokens = n_T[rows, 4 * k + g, :].rearrange("p (i s b) -> p s i b", s=8, b=2)
                        for h in range(2):
                            o(nc.vector.tensor_tensor(
                                cmp_x[rows, k, 8 * h:8 * h + 8, 15 * g:15 * g + 15], tokens[:, :, h:h + 15, b],
                                cmp_peT[rows, k, 8 * h:8 * h + 8].unsqueeze(2).broadcast_to([64, 8, 15]), ALU.add))
            hand(dve, to_tensor)
            for k in range(2):
                inbox(dve, st)
                o(nc.vector.tensor_copy(cmp_h[:, k, :, :], PS[:, 5 + k, 0:P].rearrange(
                    "p (c n) -> p c n", c=2)[:, :, 0:60]))
            hand(dve, to_tensor)
            inbox(dve, st)
            o(nc.vector.tensor_copy(cmp_kT[:, 0:60], PS[:, 2, 0:60]))
            o(nc.vector.tensor_copy(cmp_v[0:N_CMP, :, :].rearrange("p g d -> p (g d)"), PS[0:N_CMP, 3, 0:256]))

        def nsa_units():
            def finish(o, u, bank, sums, rec, coef):
                h = u.head
                o.then(nc.vector.reciprocal(rec[:, 0:3], sums[:, 0:3]))
                o.then(nc.vector.tensor_tensor(coef[:, 0:3], rec[:, 0:3], n_gate[:, u.tt, :, h], ALU.mult))
                dst = n_o[:, u.tt, h * NSA_DH:(h + 1) * NSA_DH]
                o.then(nc.vector.tensor_scalar(dst, bank[:, 0:64], coef[:, 0:1], None, ALU.mult))
                o.then(nc.vector.scalar_tensor_tensor(dst, bank[:, 64:128], coef[:, 1:2], dst, ALU.mult, ALU.add))
                return nc.vector.scalar_tensor_tensor(dst, bank[:, 128:192], coef[:, 2:3], dst, ALU.mult, ALU.add)

            units = []
            for h in range(NSA_H):
                g, rows = h // NSA_REP, slice(64 * (h % 2), 64 * (h % 2) + 64)
                for tt in range(TT):
                    q = n_T[rows, 16 + h // 2, tt * P:(tt + 1) * P]
                    mask = n_c[:, N_MASK + SEQ * tt:N_MASK + SEQ * tt + P * (tt + 1)]
                    vals = [[n_kv[:, k, kt, 256 + g * 64:320 + g * 64] for kt in range(2)] for k in (1, 2)]
                    u = Unit(tt, [(q, n_T[rows, 8 + g, :]), (q, n_T[rows, 12 + g, :])], [mask, mask], False,
                             1.0, [(0, vals[0]), (64, vals[1])],
                             (q, cmp_kT[rows, 15 * g:15 * g + 15], 128, cmp_v[0:N_CMP, g, :]), finish)
                    u.head = h
                    units.append(u)
            return units

        def square_scalar(act, st, src, scratch):
            for tt in range(TT):
                nc.scalar.activation(scratch[:, tt], src[:, tt], ACT.Square, accum_out=small[:, 8 + tt:9 + tt])
            hand(act, to_vector)
            root_scalar(act, st, slice(8, 10))

        def rms_vector(dve, st, o, n):
            inbox(dve, st)
            o(nc.vector.tensor_scalar(small[:, 8:10], small[:, 8:10], 1.0 / n, RMS_EPS, ALU.mult, ALU.add))
            root_vector(dve, st, o, slice(8, 10))

        def scaled_rows(dve, o, dst, src, gain):
            o.wait()
            for tt in range(TT):
                o(nc.vector.scalar_tensor_tensor(dst[:, tt, :], src[:, tt, :], small[:, 8 + tt:9 + tt],
                                                 gb[:, gain, :], ALU.mult, ALU.mult))
            o.wait()

        def heads_norm_vector(dve, st, o):
            heads = a_o[:, :, :, :].rearrange("p t h d -> p (t h) d")
            squares = a_sq[:, :, :, :].rearrange("p t h d -> p (t h) d")
            o.then(nc.vector.tensor_tensor(squares, heads, heads, ALU.mult))
            o.then(nc.vector.tensor_reduce(small[:, 48:56], squares, AX.X, ALU.add))
            o.then(nc.vector.tensor_scalar(small[:, 48:56], small[:, 48:56], 1.0 / A_DV, RMS_EPS, ALU.mult, ALU.add))
            root_vector(dve, st, o, slice(48, 56))
            for i in range(8):
                o(nc.vector.scalar_tensor_tensor(heads[:, i, :], heads[:, i, :], small[:, 48 + i:49 + i],
                                                 head_g[:, :], ALU.mult, ALU.mult))
            o.wait()
            o.then(nc.vector.tensor_scalar(a_o[:, :, :, :], a_o[:, :, :, :], 1.0 - LAM_INIT, None, ALU.mult))

        def angles_vector(dve, st, o):
            two_pi = 6.283185307179586
            c1 = 6.28125
            c2 = 0.0019350051879882812
            c3 = two_pi - c1 - c2
            half = 3.1415925
            dve.wait_ge(params_in, 16 * st.params)
            o.then(nc.vector.tensor_copy(pos_f[:, :], pos_i[:, :]))
            for tt in range(TT):
                o(nc.vector.tensor_scalar(ang[:, 0, tt, :], b_c[:, B_INV:B_INV + 96], pos_f[:, tt:tt + 1], None,
                                          ALU.mult))
            o.wait()
            x, k, r, m = (ang[:, i].rearrange("p t f -> p (t f)") for i in range(4))
            o.then(nc.vector.tensor_scalar(k, x, 1.0 / two_pi, ROUND, ALU.mult, ALU.add))
            o.then(nc.vector.tensor_scalar(k, k, -ROUND, None, ALU.add))
            o.then(nc.vector.scalar_tensor_tensor(r, k, -c1, x, ALU.mult, ALU.add))
            o.then(nc.vector.scalar_tensor_tensor(r, k, -c2, r, ALU.mult, ALU.add))
            o.then(nc.vector.scalar_tensor_tensor(r, k, -c3, r, ALU.mult, ALU.add))

            def wrap():
                o.then(nc.vector.tensor_scalar(m, r, two_pi / 2, None, ALU.is_gt))
                o.then(nc.vector.scalar_tensor_tensor(r, m, -two_pi, r, ALU.mult, ALU.add))
                o.then(nc.vector.tensor_scalar(m, r, -two_pi / 2, None, ALU.is_lt))
                o.then(nc.vector.scalar_tensor_tensor(r, m, two_pi, r, ALU.mult, ALU.add))
            wrap()
            o.then(nc.vector.tensor_scalar(x, r, half, -half, ALU.min, ALU.max))
            o.then(nc.vector.tensor_scalar(r, r, two_pi / 4, None, ALU.add))
            wrap()
            o.then(nc.vector.tensor_scalar(k, r, half, -half, ALU.min, ALU.max))

        def a_units():
            def finish(o, u, bank, sums, rec, coef):
                o.then(nc.vector.reciprocal(rec[:, 0:2], sums[:, 0:2]))
                o.then(nc.vector.tensor_tensor(coef[:, 1:2], rec[:, 1:2], small[:, 40:41], ALU.mult))
                dst = a_o[:, u.tt, u.head, :]
                o.then(nc.vector.tensor_scalar(dst, bank[:, 0:P], rec[:, 0:1], None, ALU.mult))
                return nc.vector.scalar_tensor_tensor(dst, bank[:, P:2 * P], coef[:, 1:2], dst, ALU.mult, ALU.add)

            units = []
            for h in range(A_H):
                for tt in range(TT):
                    mask = b_c[:, B_MASK:B_MASK + P] if tt == 0 else b_c[:, B_CAUSAL:B_CAUSAL + SEQ]
                    segs = [(a_qkT[64 * c:64 * c + 64, h, tt * P:(tt + 1) * P], a_qkT[64 * c:64 * c + 64, 4 + h, :])
                            for c in range(2)]
                    vals = [a_proj[:, 2, kt, h * P:(h + 1) * P] for kt in range(2)]
                    u = Unit(tt, segs, [mask, mask], False, A_DQK ** -0.5, [(0, vals), (P, vals)], None, finish)
                    u.head = h
                    units.append(u)
            return units

        def b_units():
            def finish(o, u, bank, sums, rec, coef):
                o.then(nc.vector.reciprocal(rec[:, 0:1], sums[:, 0:1]))
                return nc.vector.tensor_scalar(b_o[:, u.tt, u.head, :], bank[:, 0:P], rec[:, 0:1], None, ALU.mult)

            units = []
            for h in range(B_H):
                for tt in range(TT):
                    masks, segs, values = [], [], []
                    for g in range(B_G):
                        at = B_MASK + 3 * P * g + P * tt
                        masks.append(b_c[:, at:at + P * (tt + 1)])
                        segs.append((b_qkT[:, 4 * g + h, tt * P:(tt + 1) * P], b_qkT[:, 12 + 4 * g + h, :]))
                        values.append((0, [b_proj[:, 6 + g, kt, h * P:(h + 1) * P] for kt in range(2)]))
                    u = Unit(tt, segs, masks, True, B_DH ** -0.5, values, None, finish)
                    u.head = h
                    units.append(u)
            return units

        def conv_coef(j, m):
            if j < 10:
                return 4 * (j // 2) + m + FFC * (j % 2)
            return 20 + m if m < 2 else FFC + 20 + m - 2

        def ff_place(j, m):
            return (j % 2, m) if j < 10 else (m // 2, m % 2)

        def ff_scalar(act, st):
            def evacuate(j, turn):
                if j % 2 == 0 and j > 0:
                    act.wait_ge(ff_product, j // 2)
                for m in range(4):
                    k, c = ff_place(j, m)
                    n = conv_coef(j, m)
                    last = nc.scalar.activation(
                        ff_u[:, k, c, :], PS[:, 2 * (j % 3) + m // 2, (m % 2) * SEQ:(m % 2 + 1) * SEQ], ACT.Identity,
                        scale=conv_c[:, 2, n:n + 1], bias=conv_c[:, 3, n:n + 1])
                    if m % 2:
                        last.then_inc(conv_first, 1)
                if j % 2 or j == 10:
                    pair, n = j // 2, 4 if j < 10 else 2
                    act.wait_ge(conv_done, 2 * (j + 1))
                    nc.scalar.activation(ff_u[:, 0, 0:n, :], ff_u[:, 0, 0:n, :],
                                         ACT.Gelu_apprx_tanh).then_inc(ff_gelu, 1)
                    act.wait_ge(ff_product, pair + 1)
                    nc.scalar.activation(ffT_h[:, 4 * pair:4 * pair + n, :], ff_a[:, 0:n, :],
                                         ACT.Copy).then_inc(ff_hi, 1)
            return evacuate

        def ff_vector(dve, st, o):
            def evacuate(j, turn):
                for half in range(2):
                    dve.wait_ge(conv_first, 2 * j + half + 1)
                    for tap in (1, 0):
                        for m in (2 * half, 2 * half + 1):
                            k, c = ff_place(j, m)
                            n = conv_coef(j, m)
                            late = 2 - tap
                            src = PS[:, 2 * (j % 3) + half, (m % 2) * SEQ:(m % 2 + 1) * SEQ]
                            dst = ff_u[:, k, c, late:SEQ]
                            last = nc.vector.scalar_tensor_tensor(dst, src[:, 0:SEQ - late], conv_c[:, tap, n:n + 1],
                                                                  dst, ALU.mult, ALU.add)
                            o(last)
                        o.wait()
                    nc.vector.drain().then_inc(conv_done, 1)
                    nc.vector.drain().then_inc(acc_free, 1)
                if j % 2 or j == 10:
                    pair, n = j // 2, 4 if j < 10 else 2
                    dve.wait_ge(ff_gelu, pair + 1)
                    if pair:
                        dve.wait_ge(ff_hi, pair)
                        o.wait()
                    nc.vector.tensor_tensor(ff_a[:, 0:n, :], ff_u[:, 0, 0:n, :], ff_u[:, 1, 0:n, :],
                                            ALU.mult).then_inc(ff_product, 1)
                    dve.wait_ge(ff_hi, pair + 1)
                    o(nc.vector.tensor_tensor(ffT_l[:, 4 * pair:4 * pair + n, :], ff_a[:, 0:n, :],
                                              ffT_h[:, 4 * pair:4 * pair + n, :], ALU.subtract))
            return evacuate

        def params(eng, st, loads):
            for dst, src in loads:
                st.params += 1
                if st.name == "scalar":
                    eng.dma_start(dst, src, allow_slow_non_contiguous=dst.dtype == I32).then_inc(params_in, 16)

        def row(v):
            return v.unsqueeze(0).broadcast_to([P, v.shape[0]])

        def norm_params(g, b=None):
            return [(gb[:, 0, :], row(g))] + ([(gb[:, 1, :], row(b))] if b is not None else [])

        def nsa_params():
            w2k = a["cmp_k_w2"].rearrange("(c p) d -> p c d", p=P)
            return [(cmp_w1[0][:, :, :], a["cmp_k_w1"].rearrange("(c p) n -> p c n", p=P))] + [
                (cmp_w2k[:, :, 0, :], w2k), (cmp_w2k[:, :, 1, :], w2k),
                (cmp_w2v[:, :, :], a["cmp_v_w2"].rearrange("(c p) d -> p c d", p=P))] + [
                (cmp_pe[0:CMP_LEN // 2, k, :], a[n].rearrange("(s b) d -> s (b d)", b=2))
                for k, n in enumerate(("cmp_pe_k", "cmp_pe_v"))]

        def a_params():
            return [(b_c[:, :], a["c_block"]), (pos_i[:, :], a["positions_2"].rearrange("a (t p) -> p (a t)", p=P)),
                    (lam_in[:, :, :].rearrange("p a d -> p (a d)"), row(a["diff_lambda_2"].rearrange("l a d -> (l a d)"))),
                    (head_g[:, :], row(a["diff_head_g_2"][0]))]

        def conv_params():
            return [(conv_in[0:2 * FFC, i, :], a["conv_w_2"][0, i].rearrange("(c p) -> c p", p=P))
                    for i in range(CONV_W)] + [
                (conv_in[0:2 * FFC, CONV_W, :], a["conv_b_2"][0].rearrange("(c p) -> c p", p=P))]

        def moe_layer_tensor(pe, st, layer):
            turn_tensor(pe, st, lambda tt, c: X[:, tt, c * P:(c + 1) * P], DC)
            pe.wait_ge(turned_lo, st.turn)
            router_tensor(pe, st)
            stage_end(pe, st)
            stage_end(pe, st)
            sweep_tensor(pe, sweep_first, moe_b0[layer], E * layer, 0)
            stage_end(pe, st)
            crowded = pe.value_load(flag_i[0:1, 0:1], min_val=0, max_val=1)
            with pe.If(crowded > 0):
                sweep_tensor(pe, sweep_second[layer], 0, 0, 1)
            stage_end(pe, st)
            stage_end(pe, st)

        def moe_layer_scalar(act, st, layer):
            params(act, st, norm_params(a["ln_ffn_g"][layer], a["ln_ffn_b"][layer]))
            turn_scalar(act, st, th, DC)
            nc.scalar.activation(xn_h[:, :, :], X[:, :, :], ACT.Copy).then_inc(to_vector, 1)
            router_scalar(act, st)
            stage_end(act, st)
            for i in range(4):
                nc.scalar.activation(slot_of[:, 2 * i:2 * i + 2, :].rearrange("p e t -> p (e t)"), PS[:, i, :], ACT.Copy)
            stage_end(act, st)
            sweep_scalar(act, sweep_first, moe_b0[layer], E * layer, 0)
            stage_end(act, st)
            crowded = act.value_load(flag_i[0:1, 0:1], min_val=0, max_val=1)
            with act.If(crowded > 0):
                sweep_scalar(act, sweep_second[layer], 0, 0, 1)
            stage_end(act, st)
            for b in range(AHEAD):
                split_hi(act, sweep_first, moe_b0[layer] + RING * E + b, 0)
            root_scalar(act, st, slice(8, 10))
            stage_end(act, st)

        def moe_layer_vector(dve, st, o, layer):
            params(dve, st, norm_params(a["ln_ffn_g"][layer], a["ln_ffn_b"][layer]))
            turn_vector(dve, st, th, tl, DC)
            inbox(dve, st)
            o(nc.vector.tensor_tensor(xn_l[:, :, :], X[:, :, :], xn_h[:, :, :], ALU.subtract))
            o(nc.vector.memset(zero_r[:, :].bitcast(F32), 0.0))
            router_vector(dve, st, o)
            stage_end(dve, st)
            for i in range(4, 8):
                o(nc.vector.tensor_copy(slot_of[:, 2 * i:2 * i + 2, :].rearrange("p e t -> p (e t)"), PS[:, i, :]))
            stage_end(dve, st)
            sweep_vector(dve, sweep_first, moe_b0[layer], E * layer, 0)
            stage_end(dve, st)
            crowded = dve.value_load(flag_i[0:1, 0:1], min_val=0, max_val=1)
            with dve.If(crowded > 0):
                sweep_vector(dve, sweep_second[layer], 0, 0, 1)
            stage_end(dve, st)
            for tt in range(TT):
                for half in range(2):
                    x = X[:, tt, half * BW:(half + 1) * BW]
                    o(nc.vector.scalar_tensor_tensor(x, x, ALPHA, PS[:, 2 * tt + half, :], ALU.mult, ALU.add))
            layer_norm_vector(dve, st, o)
            for b in range(AHEAD):
                split_lo(dve, sweep_first, moe_b0[layer] + RING * E + b, 0)
            stage_end(dve, st)

        def moe_layer_sync(sp, layer):
            sweep_sync(sp, sweep_first, layer, moe_b0[layer])
            sp.wait_ge(flag_ready, layer + 1)
            crowded = sp.value_load(flag_i[0:1, 0:1], min_val=0, max_val=1)
            with sp.If(crowded > 0):
                sp.wait_ge(block_used, moe_b0[layer] + RING * E)
                sweep_sync(sp, sweep_second[layer], layer, 0)
                sp.wait_ge(sweep_second[layer].block_used, RING * E)

        block = ctx.enter_context(nc.Block())

        def tokens(t):
            return lambda tt, c: t[:, tt, c * P:(c + 1) * P]

        def by_column(t, per=4):
            return lambda tt, c: t[:, c // per, tt, (c % per) * P:(c % per + 1) * P]

        @block.tensor
        def _(pe):
            st = State("tensor", to_tensor)

            def end():
                stage_end(pe, st)

            def turn(source, chunks):
                turn_tensor(pe, st, source, chunks)
                end()

            def product(l, xh, xl, channels=False):
                linear_tensor(pe, l, xh, xl, channels)
                end()

            end()
            turn(tokens(X), DC)
            product(l_ret_in, th, tl)
            turn(by_column(ret_proj), 16)
            retention_tensor(pe, st)
            end()
            turn(lambda tt, c: ret_o[:, tt, c // 4, (c % 4) * P:(c % 4 + 1) * P], 16)
            product(l_ret_out, ret_oTh, ret_oTl)
            end()
            moe_layer_tensor(pe, st, 0)

            turn(tokens(X), DC)
            product(l_nsa_kv, th, tl)
            product(l_nsa_in, th, tl)
            turn(lambda tt, c: n_dup[:, tt, c // 4, c % 4, :] if c < 16 else by_column(n_q)(tt, c - 16), 24)
            compress_tensor(pe, st)
            end()
            attention_tensor(pe, st, nsa_units(), n_att)
            end()
            turn(tokens(n_o), DC)
            product(l_nsa_out, th, tl)
            end()
            moe_layer_tensor(pe, st, 1)

            end()
            turn(tokens(hn), DC)
            product(l_a_in, th, tl)
            turn(by_column(a_proj), 8)
            attention_tensor(pe, st, a_units(), a_att)
            end()
            end()
            turn(lambda tt, c: a_o[:, tt, c, :], 4)
            product(l_b_in, th, tl)
            turn(by_column(b_proj), 24)
            attention_tensor(pe, st, b_units(), b_att)
            end()
            turn(lambda tt, c: b_o[:, tt, c, :], 4)
            product(l_gates, th, tl)
            product(l_a_out, oaT_h, oaT_l)
            product(l_b_out, obT_h, obT_l)
            turn(tokens(mix), DC)
            product(l_mix, th, tl)
            end()
            turn(tokens(hn), DC)
            for i in range(4):
                nc.tensor.transpose(PS[:, 0, 2 * FFC * i:2 * FFC * (i + 1)], conv_in[0:2 * FFC, i, :],
                                    cst[0:2 * FFC, C_ID:C_ID + 2 * FFC])
            end()
            end()
            product(l_up, th, tl, channels=True)
            product(l_down, ffT_h, ffT_l)

        @block.scalar
        def _(act):
            st = State("scalar", to_scalar)

            def end():
                stage_end(act, st)

            def turn(hi, chunks):
                turn_scalar(act, st, hi, chunks)
                end()

            def product(l, evacuate=None, ahead=True):
                linear_side(act, l, split_hi, evacuate, ahead)
                end()

            act.dma_start(X[:, :, :], a["x"].rearrange("b (t p) d -> p (b t) d", p=P)).then_inc(x_in, 16)
            act.dma_start(cst[:, :], a["c_keep"]).then_inc(x_in, 16)
            act.dma_start(ret_c[:, :], a["c_ret"]).then_inc(consts_in, 16)
            act.dma_start(rw[:, :, :], a["router_w"].rearrange("(c p) e -> p c e", p=P)).then_inc(consts_in, 16)
            act.dma_start(rb[:, :], row(a["router_b"])).then_inc(consts_in, 16)
            for b in range(AHEAD):
                split_hi(act, sweep_first, b, 0)
            end()
            turn(th, DC)
            product(l_ret_in, scalar_evacuate(ret_proj))
            params(act, st, norm_params(a["ln_mix_g"][0], a["ln_mix_b"][0]))
            turn(ret_qkT, 16)
            retention_scalar(act, st)
            end()
            turn(ret_oTh, 16)
            product(l_ret_out)
            root_scalar(act, st, slice(8, 10))
            end()
            moe_layer_scalar(act, st, 0)

            params(act, st, [(n_c[:, :], a["c_nsa"])])
            turn(th, DC)
            product(l_nsa_kv, scalar_evacuate(n_kv))

            def double(i):
                nsa_double(i, lambda dst, src: nc.scalar.activation(dst, src, ACT.Copy))

            def queries_and_gates(j, turn):
                for i in ((0, 1), (2,), ())[j]:
                    double(i)
                if j < 2:
                    scalar_evacuate(n_q, scale=NSA_DH ** -0.5)(j, turn)
                    return
                for tt in range(TT):
                    nc.scalar.activation(n_g48[:, tt, :], PS[:, 4 + tt, 0:3 * NSA_H],
                                         ACT.Sigmoid).then_inc(acc_free, 1)
            product(l_nsa_in, queries_and_gates)
            params(act, st, nsa_params())
            turn(n_T, 24)
            act.dma_start(cmp_w1[1][:, :, :],
                          a["cmp_v_w1"].rearrange("(c p) n -> p c n", p=P)).then_inc(value_w1_in, 16)
            compress_scalar(act, st)
            end()
            params(act, st, norm_params(a["ln_mix_g"][1], a["ln_mix_b"][1]))
            attention_scalar(act, st, nsa_units(), n_att)
            end()
            turn(th, DC)
            product(l_nsa_out)
            root_scalar(act, st, slice(8, 10))
            end()
            moe_layer_scalar(act, st, 1)

            params(act, st, norm_params(a["pre_mix_g_2"][0]) + a_params())
            square_scalar(act, st, X, hn)
            inbox(act, st)
            nc.scalar.activation(trig[:, 1].rearrange("p t f -> p (t f)"), ang[:, 0].rearrange("p t f -> p (t f)"),
                                 ACT.Sin)
            nc.scalar.activation(trig[:, 0].rearrange("p t f -> p (t f)"), ang[:, 1].rearrange("p t f -> p (t f)"),
                                 ACT.Sin)
            nc.scalar.activation(small[:, 44:46], small[:, 42:44], ACT.Exp).then_inc(to_vector, 1)
            end()
            turn(th, DC)
            product(l_a_in, scalar_evacuate(a_proj))
            turn(a_qkT, 8)
            attention_scalar(act, st, a_units(), a_att)
            end()
            root_scalar(act, st, slice(48, 56))
            end()
            turn(oaT_h, 4)
            product(l_b_in, scalar_evacuate(b_proj))
            params(act, st, norm_params(a["post_mix_g_2"][0]))
            turn(b_qkT, 24)
            attention_scalar(act, st, b_units(), b_att)
            end()
            turn(obT_h, 4)
            product(l_gates, scalar_evacuate(gates, ACT.Sigmoid))
            product(l_a_out)
            product(l_b_out)
            turn(th, DC)

            def mixed(j, turn):
                for tt in range(TT):
                    nc.scalar.activation(mix_t[:, tt, j * BW:(j + 1) * BW], PS[:, 2 * (j % 3) + tt, :],
                                         ACT.Copy).then_inc(acc_free, 1)
            params(act, st, [(gb[:, 1, :], row(a["pre_ffn_g_2"][0]))])
            product(l_mix, mixed)
            square_scalar(act, st, mix_t, mix)
            inbox(act, st)
            square_scalar(act, st, X, mix)
            end()
            params(act, st, conv_params() + norm_params(a["post_ffn_g_2"][0]))
            turn(th, DC)
            end()
            end()
            product(l_up, ff_scalar(act, st))

            def down(j, turn):
                for tt in range(TT):
                    nc.scalar.activation(ff_y[:, tt, j * BW:(j + 1) * BW], PS[:, 2 * (j % 3) + tt, :],
                                         ACT.Copy).then_inc(acc_free, 1)
            product(l_down, down, ahead=False)
            square_scalar(act, st, ff_y, ff_sq)

        @block.vector
        def _(dve):
            st = State("vector", to_vector)
            o = Order(dve, vector_order)

            def end():
                stage_end(dve, st)

            def turn(hi, lo, chunks):
                turn_vector(dve, st, hi, lo, chunks)
                end()

            def product(l, evacuate=None, ahead=True):
                linear_side(dve, l, split_lo, evacuate, ahead)
                end()

            dve.wait_ge(x_in, 2 * 16)
            o(nc.vector.tensor_copy(ident_r[:, :], ident))
            for b in range(AHEAD):
                split_lo(dve, sweep_first, b, 0)
            end()
            turn(th, tl, DC)
            dve.wait_ge(consts_in, 3 * 16)
            o.then(nc.vector.tensor_copy(rwh[:, :, :], rw[:, :, :]))
            o(nc.vector.tensor_tensor(rwl[:, :, :], rw[:, :, :], rwh[:, :, :], ALU.subtract))

            def rotate_behind(l, rotate, n):
                def evacuate(j, turn):
                    if is_first(turn) and 1 <= j <= n:
                        dve.wait_ge(acc_free, 2 * (l.n0 + j))
                        rotate(j - 1)
                return evacuate

            def rotate_ret(j):
                for tt in range(TT):
                    rope_vector(dve, o, ret_proj[:, j, tt, :].rearrange("p (h b d) -> p h b d", h=2, b=2),
                                ret_c[:, R_COS + P * tt:R_COS + P * (tt + 1)],
                                ret_c[:, R_SIN + P * tt:R_SIN + P * (tt + 1)], 2, P)
            product(l_ret_in, rotate_behind(l_ret_in, rotate_ret, 4))
            params(dve, st, norm_params(a["ln_mix_g"][0], a["ln_mix_b"][0]))
            turn(ret_qkT, None, 16)
            retention_vector(dve, st, o)
            end()
            turn(ret_oTh, ret_oTl, 16)
            product(l_ret_out, residual_evacuate(o, ALPHA))
            layer_norm_vector(dve, st, o)
            end()
            moe_layer_vector(dve, st, o, 0)

            params(dve, st, [(None, None)])
            turn(th, tl, DC)
            dve.wait_ge(params_in, 16 * st.params)
            product(l_nsa_kv, rotate_behind(l_nsa_kv, lambda j: nsa_rotate(dve, o, n_kv[:, j], 4), 2))

            def rotate_rest(j, turn):
                if j == 0:
                    nsa_rotate(dve, o, n_kv[:, 2], 4)
                    o.wait()
                    nsa_double(3, lambda dst, src: o(nc.vector.tensor_copy(dst, src)))
                else:
                    dve.wait_ge(acc_free, 2 * (l_nsa_in.n0 + j))
                    nsa_rotate(dve, o, n_q[:, j - 1], 8)
                if j == 2:
                    dve.wait_ge(acc_free, 2 * (l_nsa_in.n0 + 3))
                    nsa_gates_vector(dve, o)
            product(l_nsa_in, rotate_rest)
            turn(n_T, None, 24)
            params(dve, st, nsa_params())
            compress_vector(dve, st, o)
            end()
            params(dve, st, norm_params(a["ln_mix_g"][1], a["ln_mix_b"][1]))
            attention_vector(dve, st, o, nsa_units(), n_att)
            end()
            turn(th, tl, DC)
            product(l_nsa_out, residual_evacuate(o, ALPHA))
            layer_norm_vector(dve, st, o)
            end()
            moe_layer_vector(dve, st, o, 1)

            params(dve, st, norm_params(a["pre_mix_g_2"][0]) + a_params())
            rms_vector(dve, st, o, D)
            angles_vector(dve, st, o)
            o.then(nc.vector.tensor_tensor(lam_in[:, 0:3:2, :], lam_in[:, 0:3:2, :], lam_in[:, 1:4:2, :], ALU.mult))
            o.then(nc.vector.tensor_reduce(small[:, 42:44], lam_in[:, 0:3:2, :], AX.X, ALU.add))
            hand(dve, to_scalar)
            scaled_rows(dve, o, hn, X, 0)
            inbox(dve, st)
            o.then(nc.vector.tensor_tensor(small[:, 41:42], small[:, 45:46], small[:, 44:45], ALU.subtract))
            o.then(nc.vector.tensor_scalar(small[:, 40:41], small[:, 41:42], -LAM_INIT, None, ALU.add))
            end()
            turn(th, tl, DC)

            def rotate_a(j):
                for tt in range(TT):
                    rope_vector(dve, o, a_proj[:, j, tt, :].rearrange("p (h b d) -> p h b d", h=8, b=2),
                                trig[:, 0, tt, 0:32], trig[:, 1, tt, 0:32], 8, 32)
            product(l_a_in, rotate_behind(l_a_in, rotate_a, 2))
            turn(a_qkT, None, 8)
            attention_vector(dve, st, o, a_units(), a_att)
            end()
            heads_norm_vector(dve, st, o)
            end()
            turn(oaT_h, oaT_l, 4)

            def rotate_b(j):
                for tt in range(TT):
                    rope_vector(dve, o, b_proj[:, j, tt, :].rearrange("p (h b d) -> p h b d", h=4, b=2),
                                trig[:, 0, tt, 32:96], trig[:, 1, tt, 32:96], 4, 64)
            product(l_b_in, rotate_behind(l_b_in, rotate_b, 6))
            params(dve, st, norm_params(a["post_mix_g_2"][0]))
            turn(b_qkT, None, 24)
            attention_vector(dve, st, o, b_units(), b_att)
            end()
            turn(obT_h, obT_l, 4)
            product(l_gates)

            def gated_a(j, turn):
                for tt in range(TT):
                    nc.vector.tensor_tensor(mix[:, tt, j * BW:(j + 1) * BW], PS[:, 2 * (j % 3) + tt, :],
                                            gates[:, j, tt, :], ALU.mult).then_inc(acc_free, 1)

            def gated_b(j, turn):
                for tt in range(TT):
                    s = mix_t[:, tt, j * BW:(j + 1) * BW]
                    o.then(nc.vector.tensor_tensor(s, PS[:, 2 * (j % 3) + tt, :], gates[:, 2 + j, tt, :], ALU.mult))
                    m = mix[:, tt, j * BW:(j + 1) * BW]
                    nc.vector.tensor_tensor(m, m, s, ALU.add).then_inc(acc_free, 1)
            product(l_a_out, gated_a)
            product(l_b_out, gated_b)
            turn(th, tl, DC)
            params(dve, st, [(gb[:, 1, :], row(a["pre_ffn_g_2"][0]))])
            product(l_mix)
            dve.wait_ge(params_in, 16 * st.params)
            rms_vector(dve, st, o, D)
            scaled_rows(dve, o, mix_t, mix_t, 0)
            o.then(nc.vector.tensor_tensor(X[:, :, :], X[:, :, :], mix_t[:, :, :], ALU.add))
            hand(dve, to_scalar)
            rms_vector(dve, st, o, D)
            scaled_rows(dve, o, hn, X, 1)
            end()
            params(dve, st, conv_params() + norm_params(a["post_ffn_g_2"][0]))
            turn_vector(dve, st, th, tl, DC)
            dve.wait_ge(params_in, 16 * st.params)
            end()
            end()
            o(nc.vector.tensor_copy(conv_c[:, :, :].rearrange("p i c -> p (i c)"), PS[:, 0, 0:8 * FFC]))
            end()
            product(l_up, ff_vector(dve, st, o))
            product(l_down, ahead=False)
            rms_vector(dve, st, o, D)
            scaled_rows(dve, o, ff_y, ff_y, 0)
            nc.vector.tensor_tensor(X[:, :, :], X[:, :, :], ff_y[:, :, :], ALU.add).then_inc(out_ready, 1)

        @block.sync
        def _(sp):
            linear_sync(sp, l_ret_in)
            linear_sync(sp, l_ret_out)
            moe_layer_sync(sp, 0)
            for l in (l_nsa_kv, l_nsa_in, l_nsa_out):
                linear_sync(sp, l)
            moe_layer_sync(sp, 1)
            for l in (l_a_in, l_b_in, l_gates, l_a_out, l_b_out, l_mix, l_up, l_down):
                linear_sync(sp, l)
            sp.wait_ge(out_ready, 1)
            sp.dma_start(out.rearrange("b (t p) d -> p (b t) d", p=P), X[:, :, :]).then_inc(out_done, 16)
            sp.wait_ge(out_done, 16)


def shape_constants():
    import numpy as np
    f = np.float32
    i = np.arange(P)
    keep = np.zeros((P, C_END), f)
    keep[:, C_ID:C_ID + P] = np.eye(P)
    keep[:, C_ROW:C_ROW + 2 * P] = np.arange(2 * P)
    keep[:, C_BEFORE:C_BEFORE + P] = i[:, None] < i[None, :]
    keep[:, C_ONES:C_ONES + P] = 1.0
    keep[:, C_COL] = i
    keep[:, C_COL + 1] = i + P
    keep[:, C_I16:C_I16 + E] = np.arange(E)
    keep[:, C_I4:C_I4 + E_GROUPS] = np.arange(E_GROUPS)

    def inverse(d):
        return (f(10000.0) ** (-np.arange(0, d, 2, dtype=f) / f(d))).astype(f)

    def trig_of(d):
        ang = np.arange(SEQ, dtype=f)[:, None] * inverse(d)[None]
        return [t.astype(f).reshape(TT, P, -1).transpose(1, 0, 2).reshape(P, -1) for t in (np.cos(ang), np.sin(ang))]

    ret = np.zeros((P, R_END), f)
    log_gamma = np.log1p(-(2.0 ** (-5.0 - np.arange(RET_H)))).astype(f)
    for h in range(RET_H):
        for n, (kt, qt) in enumerate([(0, 0), (0, 1), (1, 1)]):
            diff = (qt * P + i[None, :]) - (kt * P + i[:, None])
            decay = np.where(diff >= 0, np.exp(log_gamma[h] * np.maximum(diff, 0)), 0.0) * RET_DK ** -0.5
            ret[:, R_DECAY + 3 * P * h + P * n:R_DECAY + 3 * P * h + P * (n + 1)] = decay
    ret[:, R_COS:R_COS + 2 * P], ret[:, R_SIN:R_SIN + 2 * P] = trig_of(RET_DK)

    q = np.arange(SEQ)[:, None]
    k = np.arange(SEQ)[None, :]

    def additive(seen):
        m = np.where(seen, 0.0, NEG).astype(f)
        return m[:P, :P], m[P:, :]

    nsa = np.zeros((P, N_END), f)
    m0, m1 = additive(k <= q)
    nsa[:, N_MASK:N_MASK + P] = m0
    nsa[:, N_MASK + SEQ:N_MASK + 2 * SEQ] = m1
    for tt in range(TT):
        ends = np.arange(N_CMP) * CMP_STRIDE + CMP_LEN - 1
        seen = ends[None, :] <= (tt * P + i)[:, None]
        nsa[:, N_CMASK + 15 * tt:N_CMASK + 15 * tt + 15] = np.where(seen, 0.0, NEG)
        nsa[:, N_VALID + tt] = seen.any(1)
    nsa[:, N_COS:N_COS + 64], nsa[:, N_SIN:N_SIN + 64] = trig_of(NSA_DH)

    blk = np.zeros((P, B_END), f)
    for g, (window, dil) in enumerate(B_PAIRS):
        m0, m1 = additive((k <= q) & (q - k <= window) & ((q - k) % dil == 0))
        blk[:, B_MASK + 3 * P * g:B_MASK + 3 * P * g + P] = m0
        blk[:, B_MASK + 3 * P * g + P:B_MASK + 3 * P * (g + 1)] = m1
    blk[:, B_CAUSAL:B_CAUSAL + SEQ] = additive(k <= q)[1]
    blk[:, B_INV:B_INV + 32] = inverse(A_DQK)
    blk[:, B_INV + 32:B_INV + 96] = inverse(B_DH)
    return {"c_keep": keep, "c_ret": ret, "c_nsa": nsa, "c_block": blk}


INPUTS = ["x", "ret_w_in", "ret_w_out", "nsa_w_kv", "cmp_pe_k", "cmp_pe_v", "cmp_k_w1", "cmp_k_w2", "cmp_v_w1",
          "cmp_v_w2", "nsa_w_in", "nsa_w_out", "router_w", "router_b", "moe_w_gate", "moe_w_up", "moe_w_down",
          "ln_mix_g", "ln_mix_b", "ln_ffn_g", "ln_ffn_b", "positions_2", "pre_mix_g_2", "w_in_2", "diff_lambda_2",
          "diff_head_g_2", "w_a_out_2", "w_b_out_2", "w_mix_out_2", "post_mix_g_2", "pre_ffn_g_2", "w_up_2",
          "conv_w_2", "conv_b_2", "w_down_2", "post_ffn_g_2"]


def kernel(**inputs):
    import numpy as np
    from concourse import bacc
    from concourse.bass_utils import run_bass_kernel_spmd

    nc = bacc.Bacc("TRN2", target_bir_lowering=False, num_devices=1)
    arrays, aps = {}, {}
    for name, value in list((n, inputs[n]) for n in INPUTS) + list(shape_constants().items()):
        v = np.ascontiguousarray(value)
        arrays[f"in_{name}"] = v
        aps[name] = nc.dram_tensor(f"in_{name}", v.shape, mybir.dt.from_np(v.dtype), kind="ExternalInput").ap()
    out = nc.dram_tensor("out_x", (1, SEQ, D), F32, kind="ExternalOutput").ap()
    block_program(nc, aps, out)
    r = run_bass_kernel_spmd(nc, [arrays], core_ids=[0])
    return r.results[0]["out_x"]
```
